# Optimizing a Trainium2 kernel written in Bass

```python
import math
import jax, jax.numpy as jnp
from jax import lax
import numpy as np

D_MODEL = 1024
BATCH = 1
SEQ = 512
DEPTH = 1

D_MIX = D_MODEL
N_GROUPS = 4
GROUP_W = D_MIX // N_GROUPS

A_HEADS = 4
A_QK_DIM = GROUP_W // A_HEADS // 2
A_V_DIM = 2 * A_QK_DIM

B_HEADS = 4
B_HEAD_DIM = GROUP_W // B_HEADS
MOBA_BLOCK = 256
MOBA_TOPK = 3

C_HEADS = 4
C_V_DIM = GROUP_W // C_HEADS
C_K_DIM = C_V_DIM // 2
GLA_RANK = 16
GLA_TAU = 16.0
GLA_CHUNK = 64

D_WIDTH = GROUP_W
D_BLOCKS = 4
D_BLOCK_DIM = D_WIDTH // D_BLOCKS
CONV_W = 4
LRU_C = 8.0

N_EXPERTS = 32
TOP_K = 4
D_FF = D_MODEL
SWIGLU_ALPHA = 1.702
SWIGLU_LIMIT = 7.0
MOE_BLOCK = 128

Q_BLOCK = 128
EPS = 1e-6

A_Q = A_HEADS * 2 * A_QK_DIM
A_K = A_HEADS * 2 * A_QK_DIM
A_V = A_HEADS * A_V_DIM
B_Q = GROUP_W
B_K = GROUP_W
B_V = GROUP_W
C_Q = C_HEADS * C_K_DIM
C_K = C_HEADS * C_K_DIM
C_V = C_HEADS * C_V_DIM
C_G = GLA_RANK
C_R = C_HEADS * C_V_DIM
D_X = D_WIDTH
D_G = D_WIDTH
D_IN = A_Q + A_K + A_V + B_Q + B_K + B_V + C_Q + C_K + C_V + C_G + C_R + D_X + D_G


def rms_norm(x, gain):
    xf = x.astype(jnp.float32)
    y = xf * lax.rsqrt(jnp.mean(xf * xf, axis=-1, keepdims=True) + EPS)
    return (y * gain.astype(jnp.float32)).astype(x.dtype)

def to_heads(t, n):
    b, s, f = t.shape
    return t.reshape(b, s, n, f // n).transpose(0, 2, 1, 3)

def merge_heads(t):
    b, h, s, d = t.shape
    return t.transpose(0, 2, 1, 3).reshape(b, s, h * d)

def split_columns(proj):
    sizes = (A_Q, A_K, A_V, B_Q, B_K, B_V, C_Q, C_K, C_V, C_G, C_R, D_X, D_G)
    out, off = [], 0
    for sz in sizes:
        out.append(proj[..., off:off + sz])
        off += sz
    return out

def diff_attention(q, k, v, q_gain, k_gain, lam_q1, lam_k1, lam_q2, lam_k2, out_gain, layer_idx):
    bsz, s, _ = q.shape
    q = rms_norm(q.reshape(bsz, s, A_HEADS, 2, A_QK_DIM), q_gain).transpose(0, 2, 3, 1, 4)
    k = rms_norm(k.reshape(bsz, s, A_HEADS, 2, A_QK_DIM), k_gain).transpose(0, 2, 3, 1, 4)
    v = to_heads(v, A_HEADS)
    lam_init = 0.8 - 0.6 * math.exp(-0.3 * layer_idx)
    lam = (jnp.exp(jnp.sum(lam_q1.astype(jnp.float32) * lam_k1.astype(jnp.float32)))
           - jnp.exp(jnp.sum(lam_q2.astype(jnp.float32) * lam_k2.astype(jnp.float32))) + lam_init)
    scale = A_QK_DIM ** -0.5
    nq = s // Q_BLOCK
    qb = q.reshape(bsz, A_HEADS, 2, nq, Q_BLOCK, A_QK_DIM).transpose(3, 0, 1, 2, 4, 5)
    kpos = jnp.arange(s)

    def block(args):
        j, qj = args
        qpos = j * Q_BLOCK + jnp.arange(Q_BLOCK)
        sc = jnp.einsum('bhiqd,bhikd->bhiqk', qj, k).astype(jnp.float32) * scale
        sc = jnp.where(kpos[None, :] <= qpos[:, None], sc, -jnp.inf)
        p = jax.nn.softmax(sc, axis=-1)
        w = p[:, :, 0] - lam * p[:, :, 1]
        return jnp.einsum('bhqk,bhkd->bhqd', w.astype(v.dtype), v)

    o = lax.map(block, (jnp.arange(nq), qb))
    o = o.transpose(1, 2, 0, 3, 4).reshape(bsz, A_HEADS, s, A_V_DIM)
    o = rms_norm(o, out_gain) * (1.0 - lam_init)
    return merge_heads(o)

def moba_attention(q, k, v, q_gain, k_gain):
    bsz, s, _ = q.shape
    q = rms_norm(to_heads(q, B_HEADS), q_gain)
    k = rms_norm(to_heads(k, B_HEADS), k_gain)
    v = to_heads(v, B_HEADS)
    nb = -(-s // MOBA_BLOCK)
    pad = nb * MOBA_BLOCK - s
    k_p = jnp.pad(k, ((0, 0), (0, 0), (0, pad), (0, 0)))
    v_p = jnp.pad(v, ((0, 0), (0, 0), (0, pad), (0, 0)))
    kb = k_p.reshape(bsz, B_HEADS, nb, MOBA_BLOCK, B_HEAD_DIM)
    vb = v_p.reshape(bsz, B_HEADS, nb, MOBA_BLOCK, B_HEAD_DIM)
    k_mean = jnp.mean(kb.astype(jnp.float32), axis=3)
    topk = min(MOBA_TOPK, nb)
    scale = B_HEAD_DIM ** -0.5
    nq = s // Q_BLOCK
    qb = q.reshape(bsz, B_HEADS, nq, Q_BLOCK, B_HEAD_DIM).transpose(2, 0, 1, 3, 4)
    b_idx = jnp.arange(bsz)[:, None, None, None]
    h_idx = jnp.arange(B_HEADS)[None, :, None, None]
    blk_ids = jnp.arange(nb)

    def block(args):
        j, qj = args
        qpos = j * Q_BLOCK + jnp.arange(Q_BLOCK)
        own = (j * Q_BLOCK) // MOBA_BLOCK
        gate = jnp.einsum('bhqd,bhnd->bhqn', qj.astype(jnp.float32), k_mean)
        gate = jnp.where(blk_ids < own, gate, -jnp.inf)
        _, sel = lax.top_k(gate, topk)
        valid = sel < own
        k_sel = kb[b_idx, h_idx, sel]
        v_sel = vb[b_idx, h_idx, sel]
        s_sel = jnp.einsum('bhqd,bhqnkd->bhqnk', qj, k_sel).astype(jnp.float32) * scale
        s_sel = jnp.where(valid[..., None], s_sel, -jnp.inf).reshape(bsz, B_HEADS, Q_BLOCK, topk * MOBA_BLOCK)
        k_own = lax.dynamic_slice_in_dim(k_p, own * MOBA_BLOCK, MOBA_BLOCK, axis=2)
        v_own = lax.dynamic_slice_in_dim(v_p, own * MOBA_BLOCK, MOBA_BLOCK, axis=2)
        kpos = own * MOBA_BLOCK + jnp.arange(MOBA_BLOCK)
        s_own = jnp.einsum('bhqd,bhkd->bhqk', qj, k_own).astype(jnp.float32) * scale
        s_own = jnp.where(kpos[None, :] <= qpos[:, None], s_own, -jnp.inf)
        p = jax.nn.softmax(jnp.concatenate([s_sel, s_own], axis=-1), axis=-1).astype(v.dtype)
        p_sel = p[..., :topk * MOBA_BLOCK].reshape(bsz, B_HEADS, Q_BLOCK, topk, MOBA_BLOCK)
        p_own = p[..., topk * MOBA_BLOCK:]
        return (jnp.einsum('bhqnk,bhqnkd->bhqd', p_sel, v_sel)
                + jnp.einsum('bhqk,bhkd->bhqd', p_own, v_own))

    o = lax.map(block, (jnp.arange(nq), qb))
    o = o.transpose(1, 2, 0, 3, 4).reshape(bsz, B_HEADS, s, B_HEAD_DIM)
    return merge_heads(o)

def gla(q, k, v, g_low, r, w_g2, b_g, out_gain):
    bsz, s, _ = q.shape
    dt = q.dtype
    f32 = jnp.float32
    q = to_heads(q, C_HEADS).astype(f32) * (C_K_DIM ** -0.5)
    k = to_heads(k, C_HEADS).astype(f32)
    v = to_heads(v, C_HEADS).astype(f32)
    g = jax.nn.log_sigmoid((g_low @ w_g2 + b_g).astype(f32)) / GLA_TAU
    g = to_heads(g, C_HEADS)
    nc = s // GLA_CHUNK

    def chunks(t):
        return t.reshape(bsz, C_HEADS, nc, GLA_CHUNK, t.shape[-1]).transpose(2, 0, 1, 3, 4)

    causal = jnp.tril(jnp.ones((GLA_CHUNK, GLA_CHUNK), bool))

    def step(state, inp):
        qc, kc, vc, gc = inp
        bcum = jnp.cumsum(gc, axis=2)
        o_inter = jnp.einsum('bhcd,bhde->bhce', qc * jnp.exp(bcum), state)
        diff = bcum[:, :, :, None, :] - bcum[:, :, None, :, :]
        decay = jnp.exp(jnp.where(causal[:, :, None], diff, -jnp.inf))
        att = jnp.einsum('bhid,bhjd,bhijd->bhij', qc, kc, decay)
        o_intra = jnp.einsum('bhij,bhje->bhie', att, vc)
        b_last = bcum[:, :, -1:, :]
        state = (jnp.exp(b_last[:, :, 0, :])[..., None] * state
                 + jnp.einsum('bhcd,bhce->bhde', kc * jnp.exp(b_last - bcum), vc))
        return state, o_inter + o_intra

    state0 = jnp.zeros((bsz, C_HEADS, C_K_DIM, C_V_DIM), f32)
    _, o = lax.scan(step, state0, (chunks(q), chunks(k), chunks(v), chunks(g)))
    o = o.transpose(1, 2, 0, 3, 4).reshape(bsz, C_HEADS, s, C_V_DIM)
    o = merge_heads(rms_norm(o, out_gain)) * jax.nn.silu(r.astype(f32))
    return o.astype(dt)

def rg_lru(xb, gate_in, conv_w, conv_b, w_a, b_a, w_x, b_x, lam):
    bsz, s, cw = xb.shape
    f32 = jnp.float32
    xc = lax.conv_general_dilated(xb, conv_w[:, None, :], window_strides=(1,),
                                  padding=[(CONV_W - 1, 0)],
                                  dimension_numbers=('NWC', 'WIO', 'NWC'),
                                  feature_group_count=cw) + conv_b
    xs = xc.reshape(bsz, s, D_BLOCKS, D_BLOCK_DIM)
    r_gate = jax.nn.sigmoid((jnp.einsum('bsnd,nde->bsne', xs, w_a).reshape(bsz, s, cw) + b_a).astype(f32))
    i_gate = jax.nn.sigmoid((jnp.einsum('bsnd,nde->bsne', xs, w_x).reshape(bsz, s, cw) + b_x).astype(f32))
    log_a = LRU_C * r_gate * jax.nn.log_sigmoid(lam.astype(f32))
    a = jnp.exp(log_a)
    bt = jnp.sqrt(-jnp.expm1(2.0 * log_a)) * (i_gate * xc.astype(f32))

    def combine(c1, c2):
        a1, b1 = c1
        a2, b2 = c2
        return a1 * a2, a2 * b1 + b2

    _, h = lax.associative_scan(combine, (a, bt), axis=1)
    return (h * jax.nn.gelu(gate_in.astype(f32))).astype(xb.dtype)

def hybrid_mixer(h, w_in, w_out, a_q_gain, a_k_gain, a_lam_q1, a_lam_k1, a_lam_q2, a_lam_k2,
                 a_out_gain, b_q_gain, b_k_gain, c_w_g2, c_b_g, c_out_gain, d_conv_w, d_conv_b,
                 d_w_a, d_b_a, d_w_x, d_b_x, d_lambda, layer_idx):
    proj = h @ w_in
    aq, ak, av, bq, bk, bv, cq, ck, cv, cg, cr, dx, dg = split_columns(proj)
    o_a = diff_attention(aq, ak, av, a_q_gain, a_k_gain, a_lam_q1, a_lam_k1, a_lam_q2, a_lam_k2,
                         a_out_gain, layer_idx)
    o_b = moba_attention(bq, bk, bv, b_q_gain, b_k_gain)
    o_c = gla(cq, ck, cv, cg, cr, c_w_g2, c_b_g, c_out_gain)
    o_d = rg_lru(dx, dg, d_conv_w, d_conv_b, d_w_a, d_b_a, d_w_x, d_b_x, d_lambda)
    y = jnp.concatenate([o_a.astype(h.dtype), o_b.astype(h.dtype), o_c, o_d], axis=-1)
    return y @ w_out

def moe(h, router_w, router_b, w_up, b_up, w_down, b_down):
    bsz, s, d = h.shape
    t = bsz * s
    xt = h.reshape(t, d)
    logits = (xt @ router_w + router_b).astype(jnp.float32)
    top_vals, top_idx = lax.top_k(logits, TOP_K)
    gates = jax.nn.softmax(top_vals, axis=-1)
    n = t * TOP_K
    e_flat = top_idx.reshape(n)
    tok_flat = jnp.arange(n, dtype=jnp.int32) // TOP_K
    g_flat = gates.reshape(n)
    order = jnp.argsort(e_flat)
    e_sorted = e_flat[order]
    tok_sorted = tok_flat[order]
    g_sorted = g_flat[order]
    counts = jax.ops.segment_sum(jnp.ones((n,), jnp.int32), e_flat, num_segments=N_EXPERTS)
    starts = jnp.cumsum(counts) - counts
    padded = (counts + MOE_BLOCK - 1) // MOE_BLOCK * MOE_BLOCK
    pad_ends = jnp.cumsum(padded)
    pad_starts = pad_ends - padded
    dest = pad_starts[e_sorted] + (jnp.arange(n, dtype=jnp.int32) - starts[e_sorted])
    n_rows = -(-n // MOE_BLOCK) * MOE_BLOCK + N_EXPERTS * MOE_BLOCK
    n_blocks = n_rows // MOE_BLOCK
    row_tok = jnp.full((n_rows,), t, jnp.int32).at[dest].set(tok_sorted)
    row_gate = jnp.zeros((n_rows,), jnp.float32).at[dest].set(g_sorted)
    blk_expert = jnp.minimum(jnp.searchsorted(pad_ends, jnp.arange(n_blocks) * MOE_BLOCK, side='right'),
                             N_EXPERTS - 1)
    x_pad = jnp.concatenate([xt, jnp.zeros((1, d), xt.dtype)], axis=0)
    x_rows = x_pad[row_tok].reshape(n_blocks, MOE_BLOCK, d)

    def expert_block(args):
        e, xb = args
        hu = xb @ w_up[e] + b_up[e]
        g = jnp.minimum(hu[:, :D_FF], SWIGLU_LIMIT)
        lin = jnp.clip(hu[:, D_FF:], -SWIGLU_LIMIT, SWIGLU_LIMIT)
        glu = g * jax.nn.sigmoid(SWIGLU_ALPHA * g)
        return ((lin + 1.0) * glu) @ w_down[e] + b_down[e]

    y_rows = lax.map(expert_block, (blk_expert, x_rows)).reshape(n_rows, d)
    y = jax.ops.segment_sum(y_rows * row_gate[:, None].astype(y_rows.dtype), row_tok, num_segments=t + 1)[:t]
    return y.reshape(bsz, s, d)

def first_inputs(seed: int = 0) -> dict:
    key = jax.random.key(seed)
    ks = iter(jax.random.split(key, 40))
    L = DEPTH
    f32 = jnp.float32

    def nrm(shape, scale):
        return jax.random.normal(next(ks), shape, f32) * scale

    def gain(shape):
        return 1.0 + nrm(shape, 0.05)

    x = nrm((BATCH, SEQ, D_MODEL), 1.0)
    c = nrm((BATCH, D_MODEL), 1.0)
    ada_w = nrm((L, D_MODEL, 6 * D_MODEL), 0.5 * D_MODEL ** -0.5)
    ada_b = nrm((L, 6 * D_MODEL), 0.02)
    norm1_g = gain((L, D_MODEL))
    norm2_g = gain((L, D_MODEL))
    w_in = nrm((L, D_MODEL, D_IN), D_MODEL ** -0.5)
    w_out = nrm((L, D_MIX, D_MODEL), D_MIX ** -0.5)
    a_q_gain = gain((L, A_QK_DIM))
    a_k_gain = gain((L, A_QK_DIM))
    a_lam_q1 = nrm((L, A_QK_DIM), 0.1)
    a_lam_k1 = nrm((L, A_QK_DIM), 0.1)
    a_lam_q2 = nrm((L, A_QK_DIM), 0.1)
    a_lam_k2 = nrm((L, A_QK_DIM), 0.1)
    a_out_gain = gain((L, A_V_DIM))
    b_q_gain = gain((L, B_HEAD_DIM))
    b_k_gain = gain((L, B_HEAD_DIM))
    c_w_g2 = nrm((L, GLA_RANK, C_HEADS * C_K_DIM), GLA_RANK ** -0.5)
    c_b_g = nrm((L, C_HEADS * C_K_DIM), 0.1)
    c_out_gain = gain((L, C_V_DIM))
    d_conv_w = nrm((L, CONV_W, D_WIDTH), CONV_W ** -0.5)
    d_conv_b = nrm((L, D_WIDTH), 0.02)
    d_w_a = nrm((L, D_BLOCKS, D_BLOCK_DIM, D_BLOCK_DIM), D_BLOCK_DIM ** -0.5)
    d_b_a = nrm((L, D_WIDTH), 0.02)
    d_w_x = nrm((L, D_BLOCKS, D_BLOCK_DIM, D_BLOCK_DIM), D_BLOCK_DIM ** -0.5)
    d_b_x = nrm((L, D_WIDTH), 0.02)
    u = jax.random.uniform(next(ks), (L, D_WIDTH), f32, 0.9, 0.999)
    p = u ** (1.0 / LRU_C)
    d_lambda = jnp.log(p) - jnp.log1p(-p)
    router_w = nrm((L, D_MODEL, N_EXPERTS), D_MODEL ** -0.5)
    router_b = nrm((L, N_EXPERTS), 0.01)
    exp_w_up = nrm((L, N_EXPERTS, D_MODEL, 2 * D_FF), D_MODEL ** -0.5)
    exp_b_up = nrm((L, N_EXPERTS, 2 * D_FF), 0.01)
    exp_w_down = nrm((L, N_EXPERTS, D_FF, D_MODEL), D_FF ** -0.5)
    exp_b_down = nrm((L, N_EXPERTS, D_MODEL), 0.01)
    return {"x": x, "c": c, "ada_w": ada_w, "ada_b": ada_b, "norm1_g": norm1_g, "norm2_g": norm2_g,
            "w_in": w_in, "w_out": w_out, "a_q_gain": a_q_gain, "a_k_gain": a_k_gain,
            "a_lam_q1": a_lam_q1, "a_lam_k1": a_lam_k1, "a_lam_q2": a_lam_q2, "a_lam_k2": a_lam_k2,
            "a_out_gain": a_out_gain, "b_q_gain": b_q_gain, "b_k_gain": b_k_gain,
            "c_w_g2": c_w_g2, "c_b_g": c_b_g, "c_out_gain": c_out_gain,
            "d_conv_w": d_conv_w, "d_conv_b": d_conv_b, "d_w_a": d_w_a, "d_b_a": d_b_a,
            "d_w_x": d_w_x, "d_b_x": d_b_x, "d_lambda": d_lambda,
            "router_w": router_w, "router_b": router_b, "exp_w_up": exp_w_up, "exp_b_up": exp_b_up,
            "exp_w_down": exp_w_down, "exp_b_down": exp_b_down}

def first_block(x, c, ada_w, ada_b, norm1_g, norm2_g, w_in, w_out, a_q_gain, a_k_gain,
              a_lam_q1, a_lam_k1, a_lam_q2, a_lam_k2, a_out_gain, b_q_gain, b_k_gain,
              c_w_g2, c_b_g, c_out_gain, d_conv_w, d_conv_b, d_w_a, d_b_a, d_w_x, d_b_x, d_lambda,
              router_w, router_b, exp_w_up, exp_b_up, exp_w_down, exp_b_down):
    cond = jax.nn.silu(c)
    for l in range(DEPTH):
        mod = cond @ ada_w[l] + ada_b[l]
        sh1, sc1, g1, sh2, sc2, g2 = jnp.split(mod, 6, axis=-1)
        h = rms_norm(x, norm1_g[l]) * (1.0 + sc1[:, None, :]) + sh1[:, None, :]
        y = hybrid_mixer(h, w_in[l], w_out[l], a_q_gain[l], a_k_gain[l], a_lam_q1[l], a_lam_k1[l],
                         a_lam_q2[l], a_lam_k2[l], a_out_gain[l], b_q_gain[l], b_k_gain[l],
                         c_w_g2[l], c_b_g[l], c_out_gain[l], d_conv_w[l], d_conv_b[l],
                         d_w_a[l], d_b_a[l], d_w_x[l], d_b_x[l], d_lambda[l], l)
        x = x + g1[:, None, :] * y
        h = rms_norm(x, norm2_g[l]) * (1.0 + sc2[:, None, :]) + sh2[:, None, :]
        y = moe(h, router_w[l], router_b[l], exp_w_up[l], exp_b_up[l], exp_w_down[l], exp_b_down[l])
        x = x + g2[:, None, :] * y
    return x


DEPTH_2 = 2

HEAD_DIM = 64
SB_HEADS = 8
SB_WIDTH = SB_HEADS * HEAD_DIM
NSA_HEADS = 8
NSA_KV_HEADS = 2
NSA_GROUP = NSA_HEADS // NSA_KV_HEADS
NSA_WIDTH = NSA_HEADS * HEAD_DIM
NSA_KV_WIDTH = NSA_KV_HEADS * HEAD_DIM
NSA_BRANCHES = 3
CMP_LEN = 32
CMP_STRIDE = 16
CMP_HIDDEN = 256
SEL_BLOCK = 64
SEL_TOP_N = 8
WINDOW = 512
ROPE_THETA = 10000.0
NORM_EPS = 1e-6
FORCED_BONUS = 1e4
NEG_INF = -1e30

IN_SPLITS = (SB_WIDTH, SB_WIDTH, SB_WIDTH, SB_WIDTH,
             NSA_WIDTH,
             NSA_KV_WIDTH, NSA_KV_WIDTH,
             NSA_KV_WIDTH, NSA_KV_WIDTH,
             NSA_KV_WIDTH, NSA_KV_WIDTH,
             NSA_BRANCHES * NSA_HEADS,
             NSA_WIDTH,
             D_MODEL, D_MODEL)
N_IN = 4 * SB_WIDTH + NSA_WIDTH + 6 * NSA_KV_WIDTH + NSA_BRANCHES * NSA_HEADS + NSA_WIDTH + 2 * D_MODEL


def rms_norm_2(x, g):
    xf = x.astype(jnp.float32)
    y = xf * lax.rsqrt(jnp.mean(xf * xf, axis=-1, keepdims=True) + NORM_EPS)
    return (y * g.astype(jnp.float32)).astype(x.dtype)

def rope(x, pos):
    half = HEAD_DIM // 2
    inv_freq = ROPE_THETA ** (-jnp.arange(half, dtype=jnp.float32) / half)
    ang = pos.astype(jnp.float32)[:, None, :, None] * inv_freq
    cos, sin = jnp.cos(ang), jnp.sin(ang)
    xf = x.astype(jnp.float32)
    x1, x2 = xf[..., :half], xf[..., half:]
    return jnp.concatenate([x1 * cos - x2 * sin, x2 * cos + x1 * sin], axis=-1).astype(x.dtype)

def split_heads(t, n):
    b, l, _ = t.shape
    return t.reshape(b, l, n, HEAD_DIM).transpose(0, 2, 1, 3)

def merge_heads_2(t):
    b, n, l, d = t.shape
    return t.transpose(0, 2, 1, 3).reshape(b, l, n * d)

def masked_softmax(s, mask):
    return jax.nn.softmax(jnp.where(mask, s.astype(jnp.float32), NEG_INF), axis=-1)

def stick_breaking_attention(q, k, v):
    s_len = q.shape[2]
    scale = HEAD_DIM ** -0.5
    outs = []
    for i in range(s_len // Q_BLOCK):
        end = (i + 1) * Q_BLOCK
        qb = q[:, :, i * Q_BLOCK:end]
        kb, vb = k[:, :, :end], v[:, :, :end]
        z = jnp.einsum('bhqd,bhkd->bhqk', qb, kb).astype(jnp.float32) * scale
        t = i * Q_BLOCK + jnp.arange(Q_BLOCK)
        s = jnp.arange(end)
        mask = s[None, :] < t[:, None]
        log_1m = jnp.where(mask, jax.nn.log_sigmoid(-z), 0.0)
        between = lax.cumsum(log_1m, axis=3, reverse=True) - log_1m
        w = jnp.where(mask, jnp.exp(jax.nn.log_sigmoid(z) + between), 0.0)
        outs.append(jnp.einsum('bhqk,bhkd->bhqd', w.astype(vb.dtype), vb))
    return jnp.concatenate(outs, axis=2)

def compress_blocks(x, idx, pe, w1, b1, w2):
    blocks = x[:, :, idx] + pe
    flat = blocks.reshape(blocks.shape[:3] + (CMP_LEN * HEAD_DIM,))
    return jax.nn.silu(flat @ w1 + b1) @ w2

def nsa_attention(q, k_cmp, v_cmp, k_slc, v_slc, k_win, v_win, branch_gate, pos,
                  k_cmp_norm_g, cmp_pe, cmp_w1, cmp_b1, cmp_w2):
    b, _, s_len, _ = q.shape
    g_n, r_n = NSA_KV_HEADS, NSA_GROUP
    scale = HEAD_DIM ** -0.5
    t = jnp.arange(s_len)
    qg = q.reshape(b, g_n, r_n, s_len, HEAD_DIM)

    n_cmp = (s_len - CMP_LEN) // CMP_STRIDE + 1
    cmp_start = jnp.arange(n_cmp) * CMP_STRIDE
    idx = cmp_start[:, None] + jnp.arange(CMP_LEN)[None, :]
    kc = compress_blocks(k_cmp, idx, cmp_pe[0], cmp_w1[0], cmp_b1[0], cmp_w2[0])
    vc = compress_blocks(v_cmp, idx, cmp_pe[1], cmp_w1[1], cmp_b1[1], cmp_w2[1])
    kc = rope(rms_norm_2(kc, k_cmp_norm_g), jnp.mean(pos[:, idx].astype(jnp.float32), axis=-1))
    s_cmp = jnp.einsum('bgrqd,bgcd->bgrqc', qg, kc) * scale
    mask_c = (cmp_start + CMP_LEN - 1)[None, :] <= t[:, None]
    p_cmp = masked_softmax(s_cmp, mask_c) * jnp.any(mask_c, axis=-1)[:, None]
    o_cmp = jnp.einsum('bgrqc,bgcd->bgrqd', p_cmp.astype(vc.dtype), vc)

    n_sel = s_len // SEL_BLOCK
    top_n = min(SEL_TOP_N, n_sel)
    sel_start = jnp.arange(n_sel) * SEL_BLOCK
    overlap = ((cmp_start[:, None] < sel_start[None, :] + SEL_BLOCK)
               & (cmp_start[:, None] + CMP_LEN > sel_start[None, :])).astype(jnp.float32)
    imp = jnp.einsum('bgrqc,cj->bgqj', p_cmp, overlap)
    cur = t // SEL_BLOCK
    j = jnp.arange(n_sel)
    forced = (j[None, :] == 0) | (j[None, :] == cur[:, None]) | (j[None, :] == cur[:, None] - 1)
    imp = jnp.where(sel_start[None, :] <= t[:, None],
                    imp + jnp.where(forced, FORCED_BONUS, 0.0), NEG_INF)
    _, sel_idx = lax.top_k(imp, top_n)

    nb = s_len // Q_BLOCK
    q_blocks = qg.reshape(b, g_n, r_n, nb, Q_BLOCK, HEAD_DIM).transpose(3, 0, 1, 2, 4, 5)
    idx_blocks = sel_idx.reshape(b, g_n, nb, Q_BLOCK, top_n).transpose(2, 0, 1, 3, 4)
    pad = ((0, 0), (0, 0), (WINDOW, 0), (0, 0))
    kw_pad, vw_pad = jnp.pad(k_win, pad), jnp.pad(v_win, pad)
    gather = jax.vmap(jax.vmap(lambda arr, ii: arr[ii]))
    n_keys = top_n * SEL_BLOCK

    def block_step(args):
        qb, ib, i = args
        tq = i * Q_BLOCK + jnp.arange(Q_BLOCK)
        tok = (ib[..., None] * SEL_BLOCK + jnp.arange(SEL_BLOCK)).reshape(b, g_n, Q_BLOCK * n_keys)
        ks = gather(k_slc, tok).reshape(b, g_n, Q_BLOCK, n_keys, HEAD_DIM)
        vs = gather(v_slc, tok).reshape(b, g_n, Q_BLOCK, n_keys, HEAD_DIM)
        tok = tok.reshape(b, g_n, Q_BLOCK, n_keys)
        ss = jnp.einsum('bgrqd,bgqkd->bgrqk', qb, ks) * scale
        ps = masked_softmax(ss, (tok <= tq[:, None])[:, :, None])
        o_s = jnp.einsum('bgrqk,bgqkd->bgrqd', ps.astype(vs.dtype), vs)
        kw = lax.dynamic_slice_in_dim(kw_pad, i * Q_BLOCK, WINDOW + Q_BLOCK, axis=2)
        vw = lax.dynamic_slice_in_dim(vw_pad, i * Q_BLOCK, WINDOW + Q_BLOCK, axis=2)
        p = i * Q_BLOCK - WINDOW + jnp.arange(WINDOW + Q_BLOCK)
        mw = (p[None, :] <= tq[:, None]) & (p[None, :] > tq[:, None] - WINDOW) & (p[None, :] >= 0)
        sw = jnp.einsum('bgrqd,bgkd->bgrqk', qb, kw) * scale
        pw = masked_softmax(sw, mw)
        o_w = jnp.einsum('bgrqk,bgkd->bgrqd', pw.astype(vw.dtype), vw)
        return o_s, o_w

    o_slc, o_win = lax.map(block_step, (q_blocks, idx_blocks, jnp.arange(nb)))
    o_slc = o_slc.transpose(1, 2, 3, 0, 4, 5).reshape(b, g_n, r_n, s_len, HEAD_DIM)
    o_win = o_win.transpose(1, 2, 3, 0, 4, 5).reshape(b, g_n, r_n, s_len, HEAD_DIM)

    gates = jax.nn.sigmoid(branch_gate.astype(jnp.float32)).reshape(b, s_len, NSA_BRANCHES, g_n, r_n)
    gates = gates.transpose(2, 0, 3, 4, 1)[..., None]
    o = gates[0] * o_cmp + gates[1] * o_slc + gates[2] * o_win
    return o.transpose(0, 3, 1, 2, 4).reshape(b, s_len, NSA_WIDTH)

def hybrid_layer(x, pos, norm_g, w_in, q_norm_g, k_norm_g, cmp_pe, cmp_w1, cmp_b1, cmp_w2,
                 w_up_a, w_up_b, w_out):
    h = rms_norm_2(x, norm_g)
    proj = h @ w_in
    (sb_q, sb_k, sb_v, sb_z, n_q, n_kc, n_vc, n_ks, n_vs, n_kw, n_vw,
     n_gate, n_z, gate_a, gate_b) = jnp.split(proj, list(np.cumsum(IN_SPLITS)[:-1]), axis=-1)

    o_a = stick_breaking_attention(split_heads(sb_q, SB_HEADS), split_heads(sb_k, SB_HEADS),
                                   split_heads(sb_v, SB_HEADS))
    y_a = merge_heads_2(o_a) * jax.nn.silu(sb_z)

    q = rope(rms_norm_2(split_heads(n_q, NSA_HEADS), q_norm_g), pos)
    k_slc = rope(rms_norm_2(split_heads(n_ks, NSA_KV_HEADS), k_norm_g[1]), pos)
    k_win = rope(rms_norm_2(split_heads(n_kw, NSA_KV_HEADS), k_norm_g[2]), pos)
    o_b = nsa_attention(q, split_heads(n_kc, NSA_KV_HEADS), split_heads(n_vc, NSA_KV_HEADS),
                        k_slc, split_heads(n_vs, NSA_KV_HEADS),
                        k_win, split_heads(n_vw, NSA_KV_HEADS),
                        n_gate, pos, k_norm_g[0], cmp_pe, cmp_w1, cmp_b1, cmp_w2)
    y_b = o_b * jax.nn.silu(n_z)

    merged = jax.nn.sigmoid(gate_a) * (y_a @ w_up_a) + jax.nn.sigmoid(gate_b) * (y_b @ w_up_b)
    return (x + merged @ w_out).astype(x.dtype)

def second_inputs(seed: int = 0) -> dict:
    key = jax.random.key(seed)
    ks = jax.random.split(key, 14)
    f32 = jnp.float32
    x = jax.random.normal(ks[0], (BATCH, SEQ, D_MODEL), f32)
    offsets = jax.random.randint(ks[1], (BATCH, 1), 0, SEQ, dtype=jnp.int32)
    positions = (jnp.arange(SEQ, dtype=jnp.int32)[None, :] + offsets).astype(jnp.int32)
    norm_g = 1.0 + 0.02 * jax.random.normal(ks[2], (DEPTH_2, D_MODEL), f32)
    w_in = jax.random.normal(ks[3], (DEPTH_2, D_MODEL, N_IN), f32) * D_MODEL ** -0.5
    q_norm_g = 1.0 + 0.02 * jax.random.normal(ks[4], (DEPTH_2, HEAD_DIM), f32)
    k_norm_g = 1.0 + 0.02 * jax.random.normal(ks[5], (DEPTH_2, NSA_BRANCHES, HEAD_DIM), f32)
    cmp_pe = 0.1 * jax.random.normal(ks[6], (DEPTH_2, 2, CMP_LEN, HEAD_DIM), f32)
    cmp_w1 = jax.random.normal(ks[7], (DEPTH_2, 2, CMP_LEN * HEAD_DIM, CMP_HIDDEN), f32) * (CMP_LEN * HEAD_DIM) ** -0.5
    cmp_b1 = 0.01 * jax.random.normal(ks[8], (DEPTH_2, 2, CMP_HIDDEN), f32)
    cmp_w2 = jax.random.normal(ks[9], (DEPTH_2, 2, CMP_HIDDEN, HEAD_DIM), f32) * CMP_HIDDEN ** -0.5
    w_up_a = jax.random.normal(ks[10], (DEPTH_2, SB_WIDTH, D_MODEL), f32) * SB_WIDTH ** -0.5
    w_up_b = jax.random.normal(ks[11], (DEPTH_2, NSA_WIDTH, D_MODEL), f32) * NSA_WIDTH ** -0.5
    w_out = jax.random.normal(ks[12], (DEPTH_2, D_MODEL, D_MODEL), f32) * D_MODEL ** -0.5
    return {'x': x, 'positions': positions, 'norm_g': norm_g, 'w_in': w_in,
            'q_norm_g': q_norm_g, 'k_norm_g': k_norm_g, 'cmp_pe': cmp_pe,
            'cmp_w1': cmp_w1, 'cmp_b1': cmp_b1, 'cmp_w2': cmp_w2,
            'w_up_a': w_up_a, 'w_up_b': w_up_b, 'w_out': w_out}

def second_block(x, positions, norm_g, w_in, q_norm_g, k_norm_g, cmp_pe, cmp_w1, cmp_b1, cmp_w2,
              w_up_a, w_up_b, w_out):
    for layer in range(DEPTH_2):
        x = hybrid_layer(x, positions, norm_g[layer], w_in[layer], q_norm_g[layer], k_norm_g[layer],
                         cmp_pe[layer], cmp_w1[layer], cmp_b1[layer], cmp_w2[layer],
                         w_up_a[layer], w_up_b[layer], w_out[layer])
    return x


def setup_inputs(seed=0):
    out = dict(first_inputs(seed))
    for name, value in second_inputs(seed + 1).items():
        if name != "x":
            out[name + "_2"] = value
    return out


def reference(
    x, c, ada_w, ada_b, norm1_g, norm2_g, w_in, w_out, a_q_gain, a_k_gain, a_lam_q1, a_lam_k1,
    a_lam_q2, a_lam_k2, a_out_gain, b_q_gain, b_k_gain, c_w_g2, c_b_g, c_out_gain, d_conv_w,
    d_conv_b, d_w_a, d_b_a, d_w_x, d_b_x, d_lambda, router_w, router_b, exp_w_up, exp_b_up,
    exp_w_down, exp_b_down, positions_2, norm_g_2, w_in_2, q_norm_g_2, k_norm_g_2, cmp_pe_2,
    cmp_w1_2, cmp_b1_2, cmp_w2_2, w_up_a_2, w_up_b_2, w_out_2,
):
    x = first_block(
        x, c, ada_w, ada_b, norm1_g, norm2_g, w_in, w_out, a_q_gain, a_k_gain, a_lam_q1,
        a_lam_k1, a_lam_q2, a_lam_k2, a_out_gain, b_q_gain, b_k_gain, c_w_g2, c_b_g, c_out_gain,
        d_conv_w, d_conv_b, d_w_a, d_b_a, d_w_x, d_b_x, d_lambda, router_w, router_b, exp_w_up,
        exp_b_up, exp_w_down, exp_b_down,
    )
    return second_block(
        x, positions_2, norm_g_2, w_in_2, q_norm_g_2, k_norm_g_2, cmp_pe_2, cmp_w1_2, cmp_b1_2,
        cmp_w2_2, w_up_a_2, w_up_b_2, w_out_2,
    )


_drawn_inputs = setup_inputs


def setup_inputs(seed=0):
    import zlib

    import numpy as np

    out = dict(_drawn_inputs(seed))
    spreads = {}
    factors = {'norm1_g': 2.715,
     'a_q_gain': 7.854,
     'a_k_gain': 8.0,
     'a_lam_q1': 4.29,
     'a_lam_k1': 7.227,
     'a_lam_q2': 64.0,
     'a_lam_k2': 3.783,
     'a_out_gain': 5.412,
     'b_q_gain': 8.0,
     'b_k_gain': 8.0,
     'c_b_g': 6.568,
     'c_out_gain': 6.493,
     'd_conv_b': 3.838,
     'd_b_a': 8.0,
     'd_b_x': 8.0,
     'router_b': 4.481,
     'exp_b_up': 8.0,
     'exp_b_down': 8.0,
     'norm_g_2': 5.924,
     'q_norm_g_2': 8.0,
     'k_norm_g_2': 8.0,
     'cmp_pe_2': 4.148,
     'cmp_b1_2': 8.0}
    for name, (base, spread) in spreads.items():
        noise = np.random.default_rng([zlib.crc32(name.encode()), seed]).standard_normal(out[name].shape)
        drawn = base * np.exp(spread * noise) if base else spread * noise
        out[name] = __import__('jax').numpy.asarray(drawn.astype(out[name].dtype))
    for name, factor in factors.items():
        out[name] = (out[name] * factor).astype(out[name].dtype)
    return out
```

```python
from contextlib import ExitStack
import math

import numpy as np
import concourse.bass as bass
from concourse import mybir

F32 = mybir.dt.float32
F32R = mybir.dt.float32r
BF16 = mybir.dt.bfloat16
I32 = mybir.dt.int32
U32 = mybir.dt.uint32
ALU = mybir.AluOpType
ACT = mybir.ActivationFunctionType
AX = mybir.AxisListType.X

NEG = -1e30
EPS = 1e-6
S = 512
D = 1024
NB = 4
NE = 32
NOV = 15
NSLOT = 3
NSCR = 10
NHI = 3
NF0 = 1
ADA_AT = (4, 6, 14, 19, 22, 25, 28, 31)
NF1 = 1
NF2 = 5
LEVELS = [64, 32, 16, 8, 4, 2, 1, 0]

CONST = [
    ("ident", 128), ("iota", 128), ("tri", 128), ("causal", 128), ("strict", 128), ("invf", 32),
    ("avg", 128), ("cmask", 128), ("cany", 4), ("tok", 4), ("code", 96), ("thr", 96), ("ob", 16),
    ("c", 8), ("ada_b", 48), ("n1", 8), ("n2", 8), ("ng", 16), ("aqg", 1), ("akg", 1), ("aog", 1),
    ("bqg", 1), ("bkg", 1), ("cbg", 1), ("cog", 1), ("lam", 128), ("wg2", 128), ("convw", 8), ("convb", 2),
    ("dba", 2), ("dbx", 2), ("dlam", 2), ("dwa", 256), ("dwx", 256), ("rw", 256), ("rb", 32),
    ("pmod", 1), ("room", 512), ("qg2", 128), ("kg2", 384), ("pe", 64), ("cb1", 8), ("cw2", 512),
]
COL = {}
_at = 0
for _n, _w in CONST:
    COL[_n] = (_at, _w)
    _at += _w
NCONST = _at


class Sem:

    def __init__(self, handle):
        self.handle, self.n = handle, 0


class Engine:

    def __init__(self, handle):
        self.sem = Sem(handle)
        self.q = []
        self.stack = []
        self.passed = {}
        self.vals = {}

    def wait(self, *toks):
        for t in toks:
            if t is None:
                continue
            if isinstance(t, list):
                self.wait(*t)
                continue
            sem, n = t
            if self.passed.get(sem, 0) < n:
                self.passed[sem] = n
                self.q.append(lambda e, h=sem.handle, n=n: e.wait_ge(h, n))

    def put(self, fn, *toks):
        self.wait(*toks)
        self.q.append(fn)

    def do(self, fn, *toks):
        self.wait(*toks)
        self.sem.n += 1
        self.q.append(lambda e, h=self.sem.handle: fn(e).then_inc(h, 1))
        return (self.sem, self.sem.n)

    def dma(self, sem, out, in_, *toks):
        self.wait(*toks)
        sem.n += 16
        self.q.append(lambda e: e.dma_start(out, in_).then_inc(sem.handle, 16))
        return (sem, sem.n)

    def now(self):
        return (self.sem, self.sem.n)

    def load(self, name, ap, top, *toks):
        self.wait(*toks)

        def fn(e):
            self.vals[name] = e.value_load(ap, min_val=0, max_val=top)
        self.q.append(fn)

    def enter(self, sems):
        self.stack.append((self.q, dict(self.passed), [(s, s.n) for s in [self.sem] + sems]))
        self.q = []

    def leave(self, name, thr):
        body, (self.q, self.passed, before) = self.q, self.stack.pop()
        moved = [(s, n, s.n - n) for s, n in before if s.n > n]

        def fn(e):
            with e.If(self.vals[name] > thr):
                for f in body:
                    f(e)
            if moved:
                with e.Else():
                    for s, n, k in moved:
                        if n:
                            e.wait_ge(s.handle, n)
                        e.sem_inc(s.handle, k)
        if body:
            self.q.append(fn)

    def flush(self, e):
        for f in self.q:
            f(e)


class Tile:
    def __init__(self, ring, n, ap):
        self.ring, self.n, self.ap, self.rel = ring, n, ap, []

    def __getitem__(self, k):
        return self.ap[k]

    def free(self, *toks):
        assert self not in self.ring.idle
        self.rel = list(toks)
        self.ring.idle.append(self)


class Ring:

    def __init__(self, aps):
        self.idle = [Tile(self, n, a) for n, a in enumerate(aps)]
        self.tiles = list(self.idle)

    def take(self):
        return self.idle.pop(0)


class Stream:

    def __init__(self, eng, slots, sems, items):
        self.eng, self.slots, self.sems, self.items = eng, slots, sems, items
        self.keys = [i[0] for i in items]
        self.sent, self.used, self.freed = 0, 0, 0
        self.toks = {}
        for _ in range(len(slots)):
            self.send(None)

    def send(self, tok):
        if self.sent >= len(self.items):
            return
        n = self.sent
        self.sent += 1
        slot, sem = self.slots[n % len(self.slots)], self.sems[n % len(self.slots)]
        cond, parts = self.items[n][1], self.items[n][2]
        self.eng.wait(tok)
        if cond is not None:
            self.eng.enter([sem])
        for dst, src in parts(slot):
            self.toks[n] = self.eng.dma(sem, dst, src)
        if cond is not None:
            self.eng.leave("nov", cond)

    def get(self, key):
        n = self.used
        assert self.keys[n] == key, (self.keys[n], key)
        self.used += 1
        return self.slots[n % len(self.slots)], self.toks[n]

    def done(self, tok):
        self.freed += 1
        self.send(tok)


def build(nc, io, dbg=None):
    with ExitStack() as ctx:
        program(nc, ctx, io, dbg)


def program(nc, ctx, io, dbg):
    def sem(name):
        return Sem(ctx.enter_context(nc.semaphore(name)))

    def sb(name, shape, dt=F32, stack=ctx):
        return stack.enter_context(nc.sbuf_tensor("t_" + name, shape, dt))

    T, V, A, G, Y = [Engine(ctx.enter_context(nc.semaphore(n))) for n in ("s_pe", "s_dve", "s_act", "s_pool", "s_sp")]
    dump = {}

    def mm(out, lhsT, rhs, start, stop, *w):
        T.put(lambda e: e.matmul(out, lhsT, rhs, start=start, stop=stop, skip_group_check=True), *w)

    def mmt(out, lhsT, rhs, start, stop, *w):
        return T.do(lambda e: e.matmul(out, lhsT, rhs, start=start, stop=stop, skip_group_check=True), *w)

    def tr(out, in_, ident, *w):
        return T.do(lambda e: e.transpose(out, in_, ident), *w)

    def tt(out, a, b, op, *w, E=None):
        return (E or V).do(lambda e: e.tensor_tensor(out, a, b, op), *w)

    def ts(out, a, s1, o1, *w, s2=None, o2=ALU.bypass, E=None):
        return (E or V).do(lambda e: e.tensor_scalar(out, a, s1, s2, o1, o2), *w)

    def stt(out, a, s, b, o1, o2, *w):
        return V.do(lambda e: e.scalar_tensor_tensor(out=out, in0=a, scalar=s, in1=b, op0=o1, op1=o2), *w)

    def red(out, a, op, *w, negate=False):
        return V.do(lambda e: e.tensor_reduce(out, a, AX, op, negate=negate), *w)

    def rec(out, a, *w):
        return V.do(lambda e: e.reciprocal(out, a), *w)

    def vcopy(out, a, *w):
        return V.do(lambda e: e.tensor_copy(out, a), *w)

    def scan(out, a, b, *w):
        return V.do(lambda e: e.tensor_tensor_scan(out, a, b, 0.0, ALU.mult, ALU.add), *w)

    def act(out, a, f, *w, bias=0.0, scale=1.0, acc=None):
        return A.do(lambda e: e.activation(out, a, f, bias=bias, scale=scale, accum_out=acc), *w)

    def acopy(out, a, *w):
        return A.do(lambda e: e.activation(out, a, ACT.Copy), *w)

    cst = sb("cst", [128, NCONST])
    xT = sb("xT", [128, 8, S])
    hT = None
    modT = sb("modT", [128, 48])
    cond = sb("cond", [128, 8])
    ab = sb("ab", [128, 16])
    ones = sb("ones", [128, 128])
    epsc = sb("epsc", [128, 1])
    identb = sb("identb", [128, 128], BF16)
    causb = sb("causb", [128, 128], BF16)
    stricb = sb("stricb", [128, 128], BF16)
    rstd = sb("rstd", [128, S])
    st = sb("st", [128, 512])
    wslot = [sb(f"w{i}", [128, 4096]) for i in range(NSLOT)]
    scr = Ring([sb(f"scr{i}", [128, 512]) for i in range(NSCR)])
    ps = Ring([ctx.enter_context(nc.psum_tensor(f"ps{i}", [128, 512], F32)) for i in range(8)])
    h2d = nc.dram_tensor("h2d", [S, D], F32, kind="Internal").ap()
    yrd = nc.dram_tensor("yrd", [4 * S, D], F32, kind="Internal").ap()

    def C(name, a=0, b=None):
        o, w = COL[name]
        return cst[:, o + a:o + (w if b is None else b)]

    stn = [0]

    def stat(n):
        if stn[0] + n > 512:
            stn[0] = 0
        a = stn[0]
        stn[0] += n
        return st[:, a:a + n]

    items = []

    def kcols(name, w, c0, c1, cond=None):
        n = c1 - c0

        def parts(slot):
            k = w.shape[0] // 128
            return [(slot[:, 0:k * n].rearrange("p (k n) -> p k n", k=k),
                     w[:, c0:c1].rearrange("(k p) n -> p k n", p=128))]
        items.append((name, cond, parts))

    for j in range(4):
        kcols(("ada", j), io["ada_w"], 512 * j, 512 * j + 512)
    WIN = [("g0", 0, 512), ("g1", 512, 1024), ("g2", 1024, 1536), ("g5", 2320, 2832), ("g3", 1536, 2048), ("g4", 2048, 2320)]
    for n, a, b in WIN:
        kcols(("win", n), io["w_in"], a, b)
        for j in {"g5": (4, 5), "g3": (6,), "g4": range(7, 12)}.get(n, ()):
            kcols(("ada", j), io["ada_w"], 512 * j, 512 * j + 512)
    for j in range(2):
        kcols(("wout", j), io["w_out"], 512 * j, 512 * j + 512)

    def expert(tag, wu, wd, cond=None):
        for q, c0 in enumerate((0, 1024, 512, 1536)):
            kcols((tag, q), wu, c0, c0 + 512, cond)
        for q in range(2):
            kcols((tag, 4 + q), wd[512 * q:512 * q + 512, :], 0, 1024, cond)

    for e in range(NE):
        expert(("e", e), io["exp_w_up"][e], io["exp_w_down"][e])

    def over_item(ob, q):
        c0 = (0, 1024, 512, 1536, 0, 0)[q]

        def parts(slot):
            def src():
                v = Y.vals[f"eid{ob}"]
                if q < 4:
                    w = io["exp_w_up"][bass.ds(v, 1), :, c0:c0 + 512]
                    return w.rearrange("a (k p) n -> p (a k) n", p=128)
                w = io["exp_w_down"][bass.ds(v, 1), 512 * (q - 4):512 * (q - 4) + 512, :]
                return w.rearrange("a (k p) n -> p (a k) n", p=128)
            k = 8 if q < 4 else 4
            return [(slot[:, :].rearrange("p (k n) -> p k n", k=k), src)]
        items.append(((("o", ob), q), ob, parts))

    for ob in range(NOV):
        for q in range(6):
            over_item(ob, q)
    W2 = [("sbq", 0, 512), ("sbk", 512, 1024), ("sbv", 1024, 1536), ("nq", 2048, 2560), ("kv", 2560, 3072),
          ("kw", 3072, 3352)]
    for l in range(2):
        for n, a, b in W2:
            kcols((l, n), io["w_in_2"][l], a, b)
        for kv in range(2):
            def parts(slot, l=l, kv=kv):
                return [(slot[:, :].rearrange("p (k n) -> p k n", k=16),
                         io["cmp_w1_2"][l, kv].rearrange("(k p) n -> p k n", p=128))]
            items.append(((l, "w1", kv), None, parts))
        kcols((l, "nz"), io["w_in_2"][l], 3352, 3864)
        kcols((l, "sbz"), io["w_in_2"][l], 1536, 2048)
        for j in range(2):
            kcols((l, "ga", j), io["w_in_2"][l], 3864 + 512 * j, 4376 + 512 * j)
        for j in range(2):
            def parts(slot, l=l, j=j):
                return [(slot[:, 2048 * a:2048 * a + 2048].rearrange("p (k n) -> p k n", k=4),
                         io[n][l][:, 512 * j:512 * j + 512].rearrange("(k p) n -> p k n", p=128))
                        for a, n in enumerate(("w_up_a_2", "w_up_b_2"))]
            items.append(((l, "up", j), None, parts))
            kcols((l, "gb", j), io["w_in_2"][l], 4888 + 512 * j, 5400 + 512 * j)
        for j in range(2):
            kcols((l, "wout", j), io["w_out_2"][l], 512 * j, 512 * j + 512)

    s_c, s_x = sem("s_c"), sem("s_x")
    tc = A.dma(s_c, cst[:, :], io["cst"])
    tx = A.dma(s_x, xT[:, :, :], io["xT"].rearrange("(k p) t -> p k t", p=128))
    Y_dma = Y.dma

    def dyn_dma(sem_, out, in_, *toks):
        Y.wait(*toks)
        sem_.n += 16
        Y.q.append(lambda e: e.dma_start(out, in_() if callable(in_) else in_).then_inc(sem_.handle, 16))
        return (sem_, sem_.n)
    Y.dma = dyn_dma
    W = Stream(Y, wslot, [sem(f"s_w{i}") for i in range(NSLOT)], items)

    t0 = V.do(lambda e: e.memset(ones[:, :], 1.0))
    t1 = V.do(lambda e: e.memset(epsc[:, :], EPS))
    V.wait(tc)
    vcopy(identb[:, :], C("ident"))
    vcopy(causb[:, :], C("causal"))
    tk = vcopy(stricb[:, :], C("strict"))
    for E in (T, A):
        E.wait(tk, tc)
    ident = C("ident")

    a1 = act(cond[:, :], C("c"), ACT.Sigmoid, tc)
    tcond = tt(cond[:, :], cond[:, :], C("c"), ALU.mult, a1)

    def ada(j, pool=False):
        slot, tw = W.get(("ada", j))
        w = slot[:, :].rearrange("p (k n) -> p k n", k=8)
        q = scr.take()
        if pool:
            r = scr.take()
            t = ts(q[:, :], w[:, 0, :], cond[:, 0:1], ALU.mult, tw, tcond, q.rel, E=G)
            t2 = r.rel
            for k in range(1, 8):
                t2 = ts(r[:, :], w[:, k, :], cond[:, k:k + 1], ALU.mult, t2, E=G)
                t2 = t = tt(q[:, :], q[:, :], r[:, :], ALU.add, t, t2, E=G)
            r.free(t)
        else:
            t = ts(q[:, :], w[:, 0, :], cond[:, 0:1], ALU.mult, tw, tcond, q.rel)
            for k in range(1, 8):
                t = stt(q[:, :], w[:, k, :], cond[:, k:k + 1], q[:, :], ALU.mult, ALU.add, t)
        W.done(t)

        def rest():
            b = ps.take()
            T.wait(t, t0, b.rel)
            for n in range(4):
                t2 = mmt(b[:, n:n + 1], q[:, 128 * n:128 * n + 128], ones[:, 0:1], True, True)
            q.free(t2)
            o, _ = COL["ada_b"]
            t2 = tt(modT[:, 4 * j:4 * j + 4], b[:, 0:4], cst[:, o + 4 * j:o + 4 * j + 4], ALU.add, t2, tc)
            b.free(t2)
            return t2
        return rest

    def rms(tx, a, bias, *w):
        b = ps.take()
        for k in range(8):
            q = scr.take()
            t = act(q[:, :], xT[:, k, :], ACT.Square, tx, q.rel)
            t = mmt(b[:, :], ones[:, :], q[:, :], k == 0, k == 7, t, b.rel, t0)
            q.free(t)
        t = act(rstd[:, :], b[:, :], ACT.Ln, t, t1, w[0] if w else None, bias=epsc[:, 0:1], scale=1.0 / D)
        b.free(t)
        tr_ = act(rstd[:, :], rstd[:, :], ACT.Exp, t, scale=-0.5)
        V.wait(*w)
        out = []
        for k in range(8):
            t = stt(hT[:, k, :], xT[:, k, :], a[:, k:k + 1], rstd[:, :], ALU.mult, ALU.mult, tr_, tx)
            if bias is not None:
                t = ts(hT[:, k, :], hT[:, k, :], bias[:, k:k + 1], ALU.add, t)
            out.append(t)
        return out

    def projT(slot, c0, m, th, n=8, src=None):
        nw = slot.shape[2]
        b = ps.take()
        T.wait(b.rel)
        for k in range(n):
            f = mmt if k == n - 1 else mm
            t = f(b[0:m, :], slot[:, k, c0:c0 + m], src[k] if isinstance(src, list) else (src or hT)[:, k, :], k == 0, k == n - 1, th[k])
        return b, t

    def projR(slot, c0, n, blk, th):
        b = ps.take()
        T.wait(b.rel)
        for k in range(8):
            f = mmt if k == 7 else mm
            t = f(b[:, 0:n], hT[:, k, 128 * blk:128 * blk + 128], slot[:, k, c0:c0 + n], k == 0, k == 7, th[k])
        return b, t

    def weights(key, n):
        slot, tw = W.get(key)
        T.wait(tw)
        return slot[:, 0:8 * n].rearrange("p (k n) -> p k n", k=8)

    def heads_rstd(src, n, hd, *w):
        q = scr.take()
        P = src.shape[0]
        ta = act(q[0:P, 0:n * hd], src, ACT.Square, w and list(w), q.rel)
        s1 = stat(n)[0:P, :]
        t = red(s1, q[0:P, 0:n * hd].rearrange("p (n d) -> p n d", n=n), ALU.add, ta)
        q.free(t)
        t = act(s1, s1, ACT.Sqrt, t, t1, bias=epsc[0:P, 0:1], scale=1.0 / hd)
        t = rec(s1, s1, t)
        return s1, t, ta

    def bc(ap, n, d):
        return ap.rearrange("p (n o) -> p n o", o=1).to_broadcast([ap.shape[0], n, d])

    def bcm(ap, n, d):
        return ap.rearrange("p (o d) -> p o d", o=1).to_broadcast([ap.shape[0], n, d])

    class Unit:
        def __init__(self, kind, q, k, i, v, fin, deps):
            self.kind, self.q, self.k, self.i, self.v, self.fin, self.deps = kind, q, k, i, v, fin, deps

        def scores(self):
            i, w = self.i, 128 * self.i + 128
            b = ps.take()
            T.wait(b.rel, self.deps)
            mm(b[:, 0:w], self.q[:, 128 * i:w], self.k[:, 0:w], True, False)
            t = mmt(b[:, 128 * i:w], identb[:, :], (causb if self.kind == "soft" else stricb)[:, :], False, True)
            if self.kind == "soft":
                mx = stat(2)
                tm = red(mx[:, 0:1], b[:, 0:w], ALU.max, t, negate=True)
                p = scr.take()
                self.rs = mx[:, 1:2]
                self.tp = act(p[:, 0:w], b[:, 0:w], ACT.Exp, tm, p.rel, bias=mx[:, 0:1], acc=self.rs)
                b.free(self.tp)
                self.p = p
            else:
                a, c = scr.take(), scr.take()
                ta = act(a[:, 0:w], b[:, 0:w], ACT.Sigmoid, t, a.rel, scale=-1.0)
                tb = act(c[:, 0:w], b[:, 0:w], ACT.Sigmoid, c.rel)
                b.free(tb)
                one = ones[:, 0:1].to_broadcast([128, w])
                ta = V.do(lambda e: e.tensor_tensor_scan(a[:, 0:w][:, ::-1], a[:, 0:w][:, ::-1], one, 1.0,
                                                         ALU.mult, ALU.mult), ta, t0)
                self.tp = tt(c[:, 0:w - 1], c[:, 0:w - 1], a[:, 1:w], ALU.mult, ta, tb)
                a.free(self.tp)
                self.p = c

        def turn(self, on_act):
            i, w = self.i, 128 * self.i + 128
            b = ps.take()
            T.wait(b.rel, self.tp)
            for k in range(i + 1):
                t = tr(b[:, 128 * k:128 * k + 128], self.p[:, 128 * k:128 * k + 128], ident)
            self.p.free(t)
            self.pt = scr.take()
            self.tt = (acopy if on_act else vcopy)(self.pt[:, 0:w], b[:, 0:w], t, self.pt.rel)
            b.free(self.tt)

        def mix(self):
            b = ps.take()
            T.wait(b.rel, self.tt)
            for k in range(self.i + 1):
                f = mmt if k == self.i else mm
                t = f(b[:, 0:64], self.pt[:, 128 * k:128 * k + 128], self.v(k), k == 0, k == self.i)
            self.pt.free(t)
            b.free(self.fin(b, t, self))

    def attend(units, filler=None):
        n = len(units)
        for t in range(n + 3):
            if t < n:
                units[t].scores()
            if 0 <= t - 2 < n:
                units[t - 2].turn(t % 2 == 0)
            if 0 <= t - 3 < n:
                units[t - 3].mix()
            if filler is not None:
                filler(t)

    class Fill:

        def __init__(self, *gens):
            self.gens = list(gens)

        def step(self, n=1):
            while n > 0 and self.gens:
                if next(self.gens[0], self) is self:
                    self.gens.pop(0)
                else:
                    n -= 1

        def drain(self):
            self.step(1 << 30)

    def barrier():
        toks = [E.now() for E in (T, V, A, G)]
        for E in (T, V, A, G):
            E.wait(*toks)

    for j in range(4):
        t = ada(j)()
    a1 = ab[:, 0:8]
    t = stt(a1, modT[:, 8:16], 1.0, C("n1"), ALU.add, ALU.mult, t, tc)
    arena = ExitStack()
    hT = sb("h0", [128, 8, S], stack=arena)
    th = rms(tx, a1, modT[:, 0:8], t)
    extra = [Tile(scr, NSCR + i, sb(f"scr{NSCR + i}", [128, 512], stack=arena)) for i in range(4)]
    scr.idle += extra
    aqT = sb("aqT", [128, 2, S], stack=arena)
    akT = sb("akT", [128, 2, S], stack=arena)
    bqT = sb("bqT", [128, 2, S], stack=arena)
    bkT = sb("bkT", [128, 2, S], stack=arena)
    vR = sb("vR", [128, NB, 768], stack=arena)
    cq = sb("cq", [128, S], stack=arena)
    ck = sb("ck", [128, S], stack=arena)
    bcum = sb("bcum", [128, S], stack=arena)
    dx = sb("dx", [128, 2, S + 3], stack=arena)
    dg = sb("dg", [128, 2, S], stack=arena)
    hd_ = dx[:, :, 3:S + 3]
    crs = sb("crs", [128, NB, 256], stack=arena)
    gmask = sb("gmask", [128, len(LEVELS) * 128], stack=arena)
    sta = sb("sta", [128, 256], stack=arena)
    sm = sb("sm", [128, 32], stack=arena)
    glow = sb("glow", [16, S], stack=arena)
    yab = sb("yab", [128, 4, S], stack=arena)
    yT = [yab[:, k, :] for k in range(4)] + [hT[:, k, :] for k in (4, 5)] + [dx[:, c, 3:S + 3] for c in range(2)]
    s_g = sem("s_g")
    tgm = A.dma(s_g, gmask[:, :], io["gmask"])

    q = scr.take()
    lm = C("lam").rearrange("p (a b d) -> p a b d", a=2, b=2)
    t = tt(q[:, 0:64].rearrange("p (a d) -> p a d", a=2), lm[:, :, 0, :], lm[:, :, 1, :], ALU.mult, tc, q.rel)
    t = red(sm[:, 0:2], q[:, 0:64].rearrange("p (a d) -> p a d", a=2), ALU.add, t)
    q.free(t)
    t = act(sm[:, 0:2], sm[:, 0:2], ACT.Exp, t)
    t = tt(sm[:, 2:3], sm[:, 1:2], sm[:, 0:1], ALU.subtract, t)
    tlam = ts(sm[:, 2:3], sm[:, 2:3], 0.2, ALU.subtract, t)
    nlam = sm[:, 2:3]

    def norm_turn(b, tpe, c0, n, hd, outs):
        wdt = n * hd
        s1, tr_, ta = heads_rstd(b[:, c0:c0 + wdt], n, hd, tpe)
        x = scr.take()
        t = tt(x[:, 0:wdt].rearrange("p (n d) -> p n d", n=n), b[:, c0:c0 + wdt].rearrange("p (n d) -> p n d", n=n),
               bc(s1, n, hd), ALU.mult, tr_, x.rel)
        def turn():
            b2 = ps.take()
            T.wait(b2.rel, t)
            nch = wdt // 128
            for k in range(nch):
                t2 = tr(b2[:, 128 * k:128 * k + 128], x[:, 128 * k:128 * k + 128], ident)
            x.free(t2)
            k = 0
            for m, dst, gain, scale in outs:
                t2 = ts(dst, b2[:, 128 * k:128 * k + 128 * m].rearrange("p (m t) -> p m t", m=m), gain, ALU.mult, t2,
                        s2=scale, o2=ALU.mult)
                k += m
            b2.free(t2)
            return t2
        return [t, ta], turn

    tAB = [[] for _ in range(NB)]
    pend = None
    for name in ("g0", "g1", "g2"):
        w = weights(("win", name), 512)
        for blk in range(NB):
            sl = slice(128 * blk, 128 * blk + 128)
            b, tpe = projR(w, 0, 512, blk, th)
            t3 = None
            if name == "g0":
                c0, n, hd = 0, 16, 32
                outs = [(2, aqT[:, :, sl], C("aqg"), 32.0 ** -0.5), (2, akT[:, :, sl], C("akg"), 1.0)]
            elif name == "g1":
                t3 = acopy(vR[:, blk, 0:256], b[:, 0:256], tpe)
                c0, n, hd, outs = 256, 4, 64, [(2, bqT[:, :, sl], C("bqg"), 0.125)]
            else:
                t3 = acopy(vR[:, blk, 256:512], b[:, 256:512], tpe)
                c0, n, hd, outs = 0, 4, 64, [(2, bkT[:, :, sl], C("bkg"), 1.0)]
            r_, turn = norm_turn(b, tpe, c0, n, hd, outs)
            b.free(t3, *r_)
            if pend:
                tAB[pend[1]].append(pend[0]())
            pend = (turn, blk)
            tAB[blk].append(t3)
        W.done(tpe)
    tAB[pend[1]].append(pend[0]())

    td = []

    def group_d():
        w = weights(("win", "g5"), 512)
        tz = V.do(lambda e: e.memset(dx[:, :, 0:3], 0.0))
        tdx, tdg = [], []
        for c in range(2):
            b, t = projT(w, 128 * c, 128, th)
            t = acopy(dx[:, c, 3:S + 3], b[:, :], t)
            b.free(t)
            tdx.append(t)
            yield
        for c in range(2):
            b, tpe = projT(w, 256 + 128 * c, 128, th)
            t = vcopy(dg[:, c, :], b[:, :], tpe)
            b.free(t)
            tdg.append(t)
            if c == 1:
                W.done(tpe)
            yield
        t = act(sm[:, 4:6], C("dlam"), ACT.Abs)
        t = act(sm[:, 4:6], sm[:, 4:6], ACT.Exp, t, scale=-1.0)
        t = act(sm[:, 4:6], sm[:, 4:6], ACT.Ln, t, bias=ones[:, 0:1])
        tls = stt(sm[:, 6:8], C("dlam"), 0.0, sm[:, 4:6], ALU.min, ALU.subtract, t)
        cw = C("convw").rearrange("p (c w) -> p c w", c=2)

        def lru(c):
            xc = scr.take()
            t = ts(xc[:, :], dx[:, c, 3:S + 3], cw[:, c, 3:4], ALU.mult, tdx[c], tz, xc.rel, s2=C("convb", c, c + 1), o2=ALU.add)
            for k in range(3):
                t = stt(xc[:, :], dx[:, c, k:k + S], cw[:, c, k:k + 1], xc[:, :], ALU.mult, ALU.add, t)
            gates = []
            for name, nb in (("dwa", "dba"), ("dwx", "dbx")):
                b = ps.take()
                wv = C(name).rearrange("p (c e) -> p c e", c=2)
                T.wait(b.rel, t)
                tg = mmt(b[:, :], wv[:, c, :], xc[:, :], True, True)
                g = scr.take()
                tg = act(g[:, :], b[:, :], ACT.Sigmoid, tg, g.rel, bias=C(nb, c, c + 1))
                b.free(tg)
                gates.append((g, tg))
            yield
            (r, tr_), (ig, ti) = gates
            tla = ts(r[:, :], r[:, :], sm[:, 6 + c:7 + c], ALU.mult, tr_, tls, s2=8.0, o2=ALU.mult)
            th_ = scr.take()
            t2 = act(th_[:, :], r[:, :], ACT.Tanh, tla, th_.rel)
            ta = act(r[:, :], r[:, :], ACT.Exp, tla)
            u = scr.take()
            t3 = ts(u[:, :], th_[:, :], -1.0, ALU.mult, t2, u.rel, s2=1.0, o2=ALU.add)
            t3 = rec(u[:, :], u[:, :], t3)
            t3 = tt(u[:, :], u[:, :], th_[:, :], ALU.mult, t3)
            th_.free(t3)
            t3 = act(u[:, :], u[:, :], ACT.Sqrt, t3, scale=-2.0)
            t4 = tt(ig[:, :], ig[:, :], xc[:, :], ALU.mult, ti)
            xc.free(t4)
            t4 = tt(ig[:, :], ig[:, :], u[:, :], ALU.mult, t4, t3)
            u.free(t4)
            t4 = scan(hd_[:, c, :], r[:, :], ig[:, :], t4, ta)
            r.free(t4)
            ig.free(t4)
            g = scr.take()
            t5 = tt(g[:, :], dg[:, c, :], dg[:, c, :], ALU.mult, tdg[c], g.rel)
            t5 = ts(g[:, :], g[:, :], 0.044715, ALU.mult, t5, s2=1.0, o2=ALU.add)
            t5 = tt(g[:, :], g[:, :], dg[:, c, :], ALU.mult, t5)
            t5 = act(g[:, :], g[:, :], ACT.Sigmoid, t5, scale=2.0 * math.sqrt(2.0 / math.pi))
            t5 = tt(g[:, :], g[:, :], dg[:, c, :], ALU.mult, t5)
            t5 = tt(hd_[:, c, :], hd_[:, c, :], g[:, :], ALU.mult, t5, t4)
            g.free(t5)
            td.append(t5)
            yield

        yield from lru(0)
        yield from lru(1)

    def group_c():
        w = weights(("win", "g3"), 512)
        b, t = projT(w, 0, 128, th)
        tcq = ts(cq[:, :], b[:, :], 32.0 ** -0.5, ALU.mult, t)
        b.free(tcq)
        yield
        b, t = projT(w, 128, 128, th)
        tck = acopy(ck[:, :], b[:, :], t)
        b.free(tck)
        yield
        tv = {}
        for blk in range(NB):
            b, tpe = projR(w, 256, 256, blk, th)
            t = acopy(vR[:, blk, 512:768], b[:, 0:256], tpe)
            b.free(t)
            if blk == NB - 1:
                W.done(tpe)
            yield
        tcv = t
        w = weights(("win", "g4"), 272)
        b, t = projT(w, 0, 16, th)
        tgl = acopy(glow[:, :], b[0:16, :], t)
        b.free(tgl)
        yield
        tcr = []
        for blk in range(NB):
            b, tpe = projR(w, 16, 256, blk, th)
            q = scr.take()
            t = act(q[:, 0:256], b[:, 0:256], ACT.Sigmoid, tpe, q.rel)
            t = tt(crs[:, blk, :], b[:, 0:256], q[:, 0:256], ALU.mult, t)
            b.free(t)
            q.free(t)
            tcr.append(t)
            if blk == NB - 1:
                W.done(tpe)
            yield

        b = ps.take()
        t = mmt(b[:, :], C("wg2")[0:16, :], glow[:, :], True, True, tgl, b.rel)
        q = scr.take()
        tabs = act(q[:, :], b[:, :], ACT.Abs, t, q.rel, bias=C("cbg"))
        ta = act(q[:, :], q[:, :], ACT.Exp, tabs, scale=-1.0)
        ta = act(q[:, :], q[:, :], ACT.Ln, ta, bias=ones[:, 0:1])
        z = scr.take()
        t = ts(z[:, :], b[:, :], C("cbg"), ALU.add, tabs, z.rel, s2=0.0, o2=ALU.min)
        b.free(t)
        t = tt(q[:, :], z[:, :], q[:, :], ALU.subtract, t, ta)
        z.free(t)
        for n in range(NB):
            sl = slice(128 * n, 128 * n + 128)
            t = scan(bcum[:, sl], ones[:, :], q[:, sl], t)
        q.free(t)
        tb = ts(bcum[:, :], bcum[:, :], 1.0 / 16.0, ALU.mult, t)
        bv = bcum[:, :].rearrange("p (n t) -> p n t", n=NB)
        AT = [scr.take() for _ in range(NB)]
        tat = [V.do(lambda e, a=a: e.memset(a[:, :], 0.0), a.rel) for a in AT]
        for li, L in enumerate(LEVELS):
            if L:
                f = scr.take()
                nbk = S // (2 * L)
                bl = bcum[:, :].rearrange("p (n t) -> p n t", n=nbk)
                fl = f[:, :].rearrange("p (n t) -> p n t", n=nbk)
                t = tt(fl, bl, bl[:, :, L - 1:L].to_broadcast([128, nbk, 2 * L]), ALU.subtract, tb, f.rel)
                t = act(f[:, :], f[:, :], ACT.Abs, t)
                t = act(f[:, :], f[:, :], ACT.Exp, t, scale=-1.0)
                ql, kl = scr.take(), scr.take()
                tq = tt(ql[:, :], cq[:, :], f[:, :], ALU.mult, t, tcq, ql.rel)
                tk = tt(kl[:, :], ck[:, :], f[:, :], ALU.mult, t, tck, kl.rel)
                f.free(tk)
                qa, ka = ql.ap, kl.ap
            else:
                qa, ka, tq, tk = cq, ck, tcq, tck
            for h in range(4):
                b = ps.take()
                T.wait(b.rel, tq, tk)
                for n in range(NB):
                    sl = slice(128 * n, 128 * n + 128)
                    f_ = mmt if n == NB - 1 else mm
                    t = f_(b[:, sl], ka[32 * h:32 * h + 32, sl], qa[32 * h:32 * h + 32, sl], True, True)
                m = bcm(gmask[:, 128 * li:128 * li + 128].bitcast(I32), 4, 128)
                tat[h] = V.do(lambda e, h=h, b=b, m=m: e.copy_predicated(
                    AT[h][:, :].rearrange("p (n t) -> p n t", n=NB), m, b[:, :].rearrange("p (n t) -> p n t", n=NB)),
                    t, tat[h], tgm)
                b.free(tat[h])
                if h % 2:
                    yield
            if L:
                ql.free(t)
                kl.free(t)
        qe, kd = scr.take(), scr.take()
        t = act(qe[:, :], bcum[:, :], ACT.Exp, tb, qe.rel)
        tqe = tt(qe[:, :], qe[:, :], cq[:, :], ALU.mult, t, tcq)
        t = tt(kd[:, :].rearrange("p (n t) -> p n t", n=NB), bv[:, :, 127:128].to_broadcast([128, NB, 128]), bv,
               ALU.subtract, tb, kd.rel)
        t = act(kd[:, :], kd[:, :], ACT.Exp, t)
        tkd = tt(kd[:, :], kd[:, :], ck[:, :], ALU.mult, t, tck)
        teb = act(sm[:, 16:20], bv[:, :, 127], ACT.Exp, tb)
        tst = None
        tsz = V.do(lambda e: e.memset(sta[:, :], 0.0))
        for n in range(NB):
            sl = slice(128 * n, 128 * n + 128)
            o = ps.take()
            T.wait(o.rel, tat, tcv, tst, tqe)
            if n:
                mm(o[:, 0:256], qe[:, sl], sta[:, :], True, False)
            for h in range(4):
                f_ = mmt if h == 3 else mm
                t = f_(o[:, 64 * h:64 * h + 64], AT[h][:, sl], vR[:, n, 512 + 64 * h:576 + 64 * h], n == 0, True)
            to = t
            if n < NB - 1:
                b = ps.take()
                t = tr(b[:, 0:128], kd[:, sl], ident, b.rel, tkd)
                kr = scr.take()
                t = acopy(kr[:, 0:128], b[:, 0:128], t, kr.rel)
                b.free(t)
                yield
                b = ps.take()
                t = mmt(b[:, 0:256], kr[:, 0:128], vR[:, n, 512:768], True, True, t, b.rel)
                kr.free(t)
                V.wait(to)
                for h in range(4):
                    pr = slice(32 * h, 32 * h + 32)
                    hs = slice(64 * h, 64 * h + 64)
                    if n == 0:
                        t2 = vcopy(sta[pr, hs], b[pr, hs], t, tsz)
                    else:
                        t2 = stt(sta[pr, hs], sta[pr, hs], sm[pr, 16 + n:17 + n], b[pr, hs], ALU.mult, ALU.add, t, teb, tst)
                b.free(t2)
                tst = t2
            s1, t2, ta = heads_rstd(o[:, 0:256], 4, 64, to)
            y = scr.take()
            yv = y[:, 0:256].rearrange("p (n d) -> p n d", n=4)
            t = tt(yv, o[:, 0:256].rearrange("p (n d) -> p n d", n=4), bc(s1, 4, 64), ALU.mult, t2, y.rel)
            o.free(t, ta)
            t = tt(y[:, 0:256], y[:, 0:256], crs[:, n, :], ALU.mult, t, tcr[n])
            yield
            b = ps.take()
            T.wait(b.rel, t)
            for k in range(2):
                t = tr(b[:, 128 * k:128 * k + 128], y[:, 128 * k:128 * k + 128], ident)
            y.free(t)
            t = ts(hT[:, 4:6, sl], b[:, 0:256].rearrange("p (m t) -> p m t", m=2), C("cog"), ALU.mult, t)
            b.free(t)
            typ.append(t)
        for x in [qe, kd] + AT:
            x.free(T.now())


    units = []
    ystate = {}
    typ = []

    def y_tile(blk):
        if blk not in ystate:
            q = scr.take()
            ystate[blk] = [q, q.rel]
        return ystate[blk]

    def finA(h, m, i):
        def fin(b, t, u):
            y, rel = y_tile(i)
            r = stat(2)
            t2 = rec(r[:, 0:1], u.rs, u.tp)
            o = y[:, 64 * h:64 * h + 64]
            if m == 0:
                return ts(o, b[:, 0:64], r[:, 0:1], ALU.mult, t, t2, rel)
            t2 = tt(r[:, 1:2], r[:, 0:1], nlam, ALU.mult, t2, tlam)
            return stt(o, b[:, 0:64], r[:, 1:2], o, ALU.mult, ALU.add, t, t2)
        return fin

    def finB(h, i):
        def fin(b, t, u):
            y, rel = y_tile(i)
            r = stat(1)
            t2 = rec(r, u.rs, u.tp)
            t = ts(y[:, 256 + 64 * h:320 + 64 * h], b[:, 0:64], r, ALU.mult, t, t2, rel)
            if h == 3:
                finish_ab(i, t)
            return t
        return fin

    def finish_ab(i, t):
        y, _ = ystate[i]
        s1, t2, _ = heads_rstd(y[:, 0:256], 4, 64, t)
        yv = y[:, 0:256].rearrange("p (n d) -> p n d", n=4)
        t = tt(yv, yv, bc(s1, 4, 64), ALU.mult, t2)
        b = ps.take()
        T.wait(b.rel, t)
        for k in range(4):
            t = tr(b[:, 128 * k:128 * k + 128], y[:, 128 * k:128 * k + 128], ident)
        y.free(t)
        bv = b[:, :].rearrange("p (m t) -> p m t", m=4)
        sl = slice(128 * i, 128 * i + 128)
        ts(yab[:, 0:2, sl], bv[:, 0:2, :], C("aog"), ALU.mult, t, s2=0.8, o2=ALU.mult)
        t = vcopy(yab[:, 2:4, sl], bv[:, 2:4, :], t)
        b.free(t)
        typ.append(t)

    for i in range(NB):
        for h in range(4):
            for m in range(2):
                r = 2 * h + m
                p0 = 32 * (r % 4)
                units.append(Unit("soft", aqT[p0:p0 + 32, r // 4, :], akT[p0:p0 + 32, r // 4, :], i,
                                  lambda k, h=h: vR[:, k, 64 * h:64 * h + 64], finA(h, m, i), tAB[i]))
        for h in range(4):
            p0 = 64 * (h % 2)
            units.append(Unit("soft", bqT[p0:p0 + 64, h // 2, :], bkT[p0:p0 + 64, h // 2, :], i,
                              lambda k, h=h: vR[:, k, 256 + 64 * h:320 + 64 * h], finB(h, i), tAB[i]))
    def side():
        n, left, rest = 0, list(range(4, 12)), None
        for g in (group_d(), group_c()):
            for _ in g:
                n += 1
                if left and n in ADA_AT:
                    if rest:
                        rest()
                    rest = ada(left.pop(0), True)
                yield
        if rest:
            rest()
        while left:
            ada(left.pop(0))()

    fill = Fill(side())
    attend(units, lambda t: fill.step(NF0))
    fill.drain()
    tmod = V.now()

    def add_out(key, src, deps, gain):
        for j in range(2):
            slot, tw = W.get(key(j))
            w = slot[:, :].rearrange("p (k n) -> p k n", k=8)
            T.wait(tw, deps)
            for c in range(4):
                b, tpe = projT(w, 128 * c, 128, [None] * 8, src=src)
                f = 4 * j + c
                if isinstance(gain, float):
                    t = stt(xT[:, f, :], b[:, :], gain, xT[:, f, :], ALU.mult, ALU.add, tpe)
                else:
                    t = stt(xT[:, f, :], b[:, :], gain[:, f:f + 1], xT[:, f, :], ALU.mult, ALU.add, tpe, tmod)
                b.free(t)
            W.done(tpe)
        return t

    tx = add_out(lambda j: ("wout", j), yT, typ + td, modT[:, 16:24])
    barrier()
    for x in extra:
        scr.idle.remove(x)
    arena.close()
    if dbg == "mixer":
        return finish(nc, ctx, T, V, A, G, Y, io, xT, tx, sem)

    arena = ExitStack()
    lg = sb("lg", [128, NB, 32], stack=arena)
    top = sb("top", [128, NB, 8], stack=arena)
    tix = sb("tix", [128, NB, 8], U32, stack=arena)
    tif = sb("tif", [128, NB, 4], stack=arena)
    gt = sb("gt", [128, NB, 4], stack=arena)
    oh = C("room").rearrange("p (n j e) -> p n j e", n=NB, j=4)
    mask = sb("mask", [128, NB, 32], stack=arena)
    posm = sb("posm", [128, NB, 32], stack=arena)
    vals = sb("vals", [128, NB, 32, 2], stack=arena)
    gm = sb("gm", [128, NB, 32], stack=arena)
    gmT = sb("gmT", [32, S], stack=arena)
    cnt = sb("cnt", [128, 32], stack=arena)
    ovl = sb("ovl", [128, 64], stack=arena)
    ovi = sb("ovi", [1, 32], I32, stack=arena)
    idx = sb("idx", [128, 64], U32, stack=arena)
    idxo = sb("idxo", [128, 2], U32, stack=arena)
    gfl = sb("gfl", [128, 1], stack=arena)
    bdn = sb("bdn", [32, D], stack=arena)
    xg = Ring([sb(f"xg{i}", [128, D], stack=arena) for i in range(2)])
    xt = Ring([sb(f"xt{i}", [128, 2 * D], stack=arena) for i in range(2)])
    bsp = sb("bsp", [96, 2 * D], BF16, stack=arena)
    selb = sb("selb", [96, 33], BF16, stack=arena)
    ac = Ring([sb(f"ac{i}", [128, D], stack=arena) for i in range(2)])
    og = Ring([sb(f"og{i}", [128, D], stack=arena) for i in range(2)])
    arena_h = ExitStack()
    hT = sb("h1", [128, 8, S], stack=arena_h)
    s_b, s_h, s_bo = sem("s_b"), sem("s_h"), sem("s_bo")
    s_xg = [sem(f"s_xg{i}") for i in range(2)]
    s_og = [sem(f"s_og{i}") for i in range(2)]
    tbd = G.dma(s_b, bdn[:, :], io["exp_b_down"], G.now())

    t = stt(ab[:, 8:16], modT[:, 32:40], 1.0, C("n2"), ALU.add, ALU.mult, tmod)
    th = rms(tx, ab[:, 8:16], modT[:, 24:32], t)

    tst = []
    for blk in range(NB):
        o = og.take() if blk < 2 else xg.take()
        for hf in range(2):
            b = ps.take()
            T.wait(b.rel)
            for k in range(4):
                t = tr(b[:, 128 * k:128 * k + 128], hT[:, 4 * hf + k, 128 * blk:128 * blk + 128], ident, th[4 * hf + k])
            t = (acopy if hf else vcopy)(o[:, 512 * hf:512 * hf + 512], b[:, :], t)
            b.free(t)
            G.wait(t)
        t = G.dma(s_h, h2d[128 * blk:128 * blk + 128, :], o[:, :])
        o.free(t)
        th2 = t
    th2 = (s_h, 64)
    for r in (og, xg):
        for tile in r.tiles:
            tile.rel = [th2]

    b = ps.take()
    rw = C("rw").rearrange("p (k n) -> p k n", k=8)
    T.wait(b.rel)
    for blk in range(NB):
        for k in range(8):
            f = mmt if k == 7 else mm
            t = f(b[:, 32 * blk:32 * blk + 32], hT[:, k, 128 * blk:128 * blk + 128], rw[:, k, :], k == 0, k == 7, th[k])
    t = tt(lg[:, :, :], b[:, 0:128].rearrange("p (n e) -> p n e", n=NB), bcm(C("rb"), NB, 32), ALU.add, t)
    b.free(t)
    io32 = C("iota", 0, 32)
    tl = t
    ti = []
    for blk in range(NB):
        t = V.do(lambda e, k=blk: e.max(top[:, k, :], lg[:, k, :]), tl)
        t = V.do(lambda e, k=blk: e.max_index(tix[:, k, :], top[:, k, :], lg[:, k, :]), t)
        ti.append(t)
    t = vcopy(tif[:, :, :], tix[:, :, 0:4], *ti)
    for blk in range(NB):
        for j in range(4):
            t2 = ts(oh[:, blk, j, :], io32, tif[:, blk, j:j + 1], ALU.is_equal, t)
    tmk = red(mask[:, :, :], oh[:, :, :, :].rearrange("p n j e -> p n e j"), ALU.add, t2)
    g1 = stat(4)
    t = tt(gt[:, :, :], top[:, :, 0:4], top[:, :, 0:1].to_broadcast([128, NB, 4]), ALU.subtract, ti[-1])
    t = act(gt[:, :, :], gt[:, :, :], ACT.Exp, t)
    t = red(g1, gt[:, :, :], ALU.add, t)
    t = rec(g1, g1, t)
    tgt = tt(gt[:, :, :], gt[:, :, :], bc(g1, NB, 4), ALU.mult, t)
    b = ps.take()
    T.wait(b.rel, tmk)
    for blk in range(NB):
        for k in range(blk + 1):
            f = mmt if k == blk else mm
            t = f(b[:, 32 * blk:32 * blk + 32], C("tri") if k == blk else ones[:, :], mask[:, k, :], k == 0, k == blk)
    for k in range(NB):
        f = mmt if k == 3 else mm
        t = f(b[:, 128:160], ones[:, :], mask[:, k, :], k == 0, k == 3)
    t2 = ts(posm[:, :, :], mask[:, :, :], -1.0, ALU.add, tmk, s2=1e6, o2=ALU.mult)
    tpos = tt(posm[:, :, :], posm[:, :, :], b[:, 0:128].rearrange("p (n e) -> p n e", n=NB), ALU.add, t, t2)
    tcn = vcopy(cnt[:, :], b[:, 128:160], t)
    b.free(tcn)
    q = scr.take()
    qv = q[:, 0:128].rearrange("p (n e) -> p n e", n=NB)
    t = ts(qv, oh[:, :, 2, :], 2.0, ALU.mult, t2, q.rel)
    t = tt(qv, qv, oh[:, :, 1, :], ALU.add, t)
    q2 = scr.take()
    q2v = q2[:, 0:128].rearrange("p (n e) -> p n e", n=NB)
    t3 = ts(q2v, oh[:, :, 3, :], 3.0, ALU.mult, q2.rel)
    t = tt(qv, qv, q2v, ALU.add, t, t3)
    q2.free(t)
    for blk in range(NB):
        tk = C("tok", blk, blk + 1)
        ts(vals[:, blk, :, 0], io32, 0.0, ALU.mult, s2=tk, o2=ALU.add)
        t4 = ts(q[:, 256 + blk:257 + blk], tk, 4.0, ALU.mult, s2=-4096.0, o2=ALU.add)
        t5 = ts(vals[:, blk, :, 1], qv[:, blk, :], q[:, 256 + blk:257 + blk], ALU.add, t, t4)
    q.free(t5)
    tva = t5
    tgm_ = None
    for blk in range(NB):
        for j in range(4):
            if j == 0:
                t = ts(gm[:, blk, :], oh[:, blk, 0, :], gt[:, blk, 0:1], ALU.mult, tgt)
            else:
                t = stt(gm[:, blk, :], oh[:, blk, j, :], gt[:, blk, j:j + 1], gm[:, blk, :], ALU.mult, ALU.add, t)
    b = ps.take()
    T.wait(b.rel, t)
    for blk in range(NB):
        t = tr(b[0:32, 128 * blk:128 * blk + 128], gm[:, blk, :], ident)
    tgmT = acopy(gmT[:, :], b[0:32, :], t)
    b.free(tgmT)
    q, q2 = scr.take(), scr.take()
    fl = q[:, 0:96]
    t = tt(fl.rearrange("p (a e) -> p a e", a=3), bcm(cnt[:, :], 3, 32), C("thr").rearrange("p (a e) -> p a e", a=3),
           ALU.is_gt, tcn, q.rel)
    inc = q[:, 96:192]
    t = scan(inc, ones[:, 0:96], fl, t)
    tno = vcopy(ovi[0:1, 31:32], inc[0:1, 95:96], t)
    t = tt(inc, inc, fl, ALU.mult, tno)
    for ob in range(NOV):
        t2 = ts(q2[:, 0:96], inc, float(ob + 1), ALU.is_equal, t, q2.rel if ob == 0 else t2)
        t2 = tt(q2[:, 0:96], q2[:, 0:96], C("code"), ALU.mult, t2)
        t2 = red(ovl[:, ob:ob + 1], q2[:, 0:96], ALU.add, t2)
    t = ts(ovl[:, 16:31], ovl[:, 0:15], 63.5, ALU.is_gt, t2)
    t = ts(ovl[:, 32:47], ovl[:, 0:15], 95.5, ALU.is_gt, t)
    t = tt(ovl[:, 16:31], ovl[:, 16:31], ovl[:, 32:47], ALU.add, t)
    t = ts(ovl[:, 16:31], ovl[:, 16:31], 1.0, ALU.add, t)
    t = stt(ovl[:, 0:15], ovl[:, 16:31], -32.0, ovl[:, 0:15], ALU.mult, ALU.add, t)
    t = ts(ovl[:, 0:15], ovl[:, 0:15], 0.0, ALU.max, t)
    tov = ts(ovl[:, 16:31], ovl[:, 16:31], 128.0, ALU.mult, t)
    tovi = vcopy(ovi[0:1, 0:15], ovl[0:1, 0:15], tov)
    q.free(tov)
    q2.free(tov)
    tb_ = ps.take()
    T.wait(tb_.rel, tva)
    for e in range(NE):
        q = scr.take()
        for blk in range(NB):
            t = ts(q[:, 128 * blk:128 * blk + 128], C("iota"), posm[:, blk, e:e + 1], ALU.is_equal, tpos, q.rel)
        for blk in range(NB):
            t2 = mmt(tb_[:, 2 * e:2 * e + 2], q[:, 128 * blk:128 * blk + 128], vals[:, blk, e, :], blk == 0, blk == 3, t)
        q.free(t2)
    iv = idx[:, :].rearrange("p (e a) -> p e a", a=2)
    bv_ = tb_[:, 0:64].rearrange("p (e a) -> p e a", a=2)
    vcopy(iv[:, :, 0], bv_[:, :, 0], t2)
    tix_ = ts(iv[:, :, 1], bv_[:, :, 1], 4096.0, ALU.add)
    tb_.free(tix_)

    sc_n = [0]

    def gather(col, dep, s_=None):
        x = xg.take()
        s_ = s_ or s_xg[x.n]
        G.wait(x.rel, dep, th2)
        s_.n += 16
        G.put(lambda e: e.indirect_dma_start(x[:, :], None, h2d, bass.IndirectOffsetOnAxis(ap=col, axis=0))
              .then_inc(s_.handle, 16))
        return x, (s_, s_.n)

    def r32(ap):
        return ap.bitcast(F32R)

    class Pieces:

        def __init__(self, tags):
            self.keys = [(tag, q, hf) for tag in tags for q in range(6) for hf in range(2)]
            self.n, self.ready, self.slot, self.last = 0, [], None, []
            for _ in range(2):
                self.split()

        def split(self):
            if self.n == len(self.keys):
                return
            tag, q, hf = self.keys[self.n]
            if hf == 0:
                self.slot = W.get((tag, q))
            slot, tw = self.slot
            raw = slot[:, 2048 * hf:2048 * hf + 2048]
            h, l = whi.take(), wlo.take()
            ta = act(r32(h[:, :]), raw, ACT.Copy, tw, h.rel)
            tl = tt(r32(l[:, :]), raw, h[:, :], ALU.subtract, ta, tw, l.rel, E=G if self.n % 4 == 3 else V)
            self.n += 1
            self.last = (self.last + [tl])[-2:]
            if hf == 1:
                W.done(self.last)
            self.ready.append((h, l, [ta, tl]))

        def take(self):
            return self.ready.pop(0)

        def done(self, piece, t):
            piece[0].free(t)
            piece[1].free(t)
            self.split()

    def parts(dst, b, t, rel):
        ta = act(r32(dst[:, 0:512]), b[:, :], ACT.Copy, t, rel)
        tl = tt(r32(dst[:, 512:1024]), b[:, :], dst[:, 0:512], ALU.subtract, ta, rel)
        b.free(tl)
        return [ta, tl]

    def turn_x(x, tg):
        o = xt.take()
        to = []
        for hf in range(2):
            b = ps.take()
            T.wait(b.rel, tg)
            for k in range(4):
                t = tr(b[:, 128 * k:128 * k + 128], x[:, 512 * hf + 128 * k:512 * hf + 128 * k + 128], ident)
            to.append(parts(o[:, 1024 * hf:1024 * hf + 1024], b, t, o.rel))
        x.free(t)
        return o, to

    def three(out, xs, k, wh, wl, first, last, tok):
        xh, xl = xs[:, 128 * k:128 * k + 128], xs[:, 512 + 128 * k:640 + 128 * k]
        mm(out, r32(xh), r32(wh), first, False)
        mm(out, r32(xh), r32(wl), False, False)
        return (mmt if tok else mm)(out, r32(xl), r32(wh), False, last)

    def expert_up(P, xo, txo, bias, tbias):
        h = ac.take()
        half = []
        for hf in range(2):
            pair = []
            for gl in range(2):
                b = ps.take()
                c0 = 1024 * gl + 512 * hf
                T.wait(txo, b.rel)
                mm(b[:, :], bias.to_broadcast([96, 128]), bsp[:, c0:c0 + 512], True, False, tbias)
                for pc in range(2):
                    piece = P.take()
                    wh = piece[0][:, :].rearrange("p (k n) -> p k n", k=4)
                    wl = piece[1][:, :].rearrange("p (k n) -> p k n", k=4)
                    T.wait(piece[2])
                    for k in range(4):
                        t = three(b[:, :], xo[:, 1024 * pc:1024 * pc + 1024], k, wh[:, k, :], wl[:, k, :],
                                  False, pc == 1 and k == 3, k == 3)
                    P.done(piece, t)
                pair.append((b, t))
            (bg, tg), (bl, tl) = pair
            g, l, s_ = scr.take(), scr.take(), scr.take()
            tg = ts(g[:, :], bg[:, :], 7.0, ALU.min, tg, g.rel)
            bg.free(tg)
            ta = act(s_[:, :], g[:, :], ACT.Sigmoid, tg, s_.rel, scale=1.702)
            tl = ts(l[:, :], bl[:, :], 7.0, ALU.min, tl, l.rel, s2=-7.0, o2=ALU.max)
            bl.free(tl)
            tl = stt(l[:, :], l[:, :], 1.0, g[:, :], ALU.add, ALU.mult, tl)
            g.free(tl)
            t = tt(h[:, 512 * hf:512 * hf + 512], l[:, :], s_[:, :], ALU.mult, tl, ta, h.rel)
            l.free(t)
            s_.free(t)
            half.append(t)
        xo.free(T.now())
        return h, half

    def turn_h(h, half):
        o = xt.take()
        to = []
        for hf in range(2):
            b = ps.take()
            T.wait(b.rel, half[hf])
            for k in range(4):
                t = tr(b[:, 128 * k:128 * k + 128], h[:, 512 * hf + 128 * k:512 * hf + 128 * k + 128], ident)
            to.append(parts(o[:, 1024 * hf:1024 * hf + 1024], b, t, o.rel))
        h.free(t)
        return o, to

    def expert_down(P, ho, tho, col, s_=None):
        o2 = [ps.take(), ps.take()]
        for pc in range(4):
            piece = P.take()
            wh = piece[0][:, :].rearrange("p (k n) -> p k n", k=2)
            wl = piece[1][:, :].rearrange("p (k n) -> p k n", k=2)
            T.wait(piece[2], tho[pc // 2], o2[0].rel, o2[1].rel)
            for k in range(2):
                for n in range(2):
                    t = three(o2[n][:, :], ho[:, 1024 * (pc // 2):1024 * (pc // 2) + 1024], 2 * (pc % 2) + k,
                              wh[:, k, 512 * n:512 * n + 512], wl[:, k, 512 * n:512 * n + 512],
                              pc == 0 and k == 0, pc == 3 and k == 1, k == 1 and n == 1)
            P.done(piece, t)
        ho.free(t)
        o = og.take()
        s_ = s_ or s_og[o.n]
        t1_ = acopy(o[:, 0:512], o2[0][:, :], t, o.rel)
        t2 = vcopy(o[:, 512:1024], o2[1][:, :], t, o.rel)
        o2[0].free(t1_)
        o2[1].free(t2)
        G.wait(t1_, t2)
        s_.n += 16
        G.put(lambda e: e.indirect_dma_start(yrd, bass.IndirectOffsetOnAxis(ap=col, axis=0), o[:, :], None,
                                             bounds_check=4 * S - 1, oob_is_err=False).then_inc(s_.handle, 16))
        o.free((s_, s_.n))
        return o

    for E in (T, V, A, G, Y):
        E.load("nov", ovi[0:1, 31:32], NOV, tovi, tno)
    for ob in range(NOV):
        Y.load(f"eid{ob}", ovi[0:1, ob:ob + 1], NE - 1)
    bf = [xg.tiles[0], xg.tiles[1]]
    s_bu = sem("s_bu")
    tbu = None
    for hf in range(2):
        u = bf[hf]
        for j in range(3):
            tbu = G.dma(s_bu, u[32 * j:32 * j + 32, :], io["exp_b_up"][:, 1024 * hf:1024 * hf + 1024], u.rel)
    for hf in range(2):
        u = bf[hf]
        dst = bsp[:, 1024 * hf:1024 * hf + 1024]
        t = vcopy(dst, u[0:96, :], tbu)
        for j in (1, 2, 2):
            pr = slice(32 * j, 32 * j + 32)
            t = tt(u[pr, :], u[pr, :], dst[pr, :], ALU.subtract, t)
            t = vcopy(dst[pr, :], u[pr, :], t)
        u.rel = [t]
    t2 = ts(selb[:, 0:32], io32[0:96, :], C("pmod")[0:96, :], ALU.is_equal)
    tbias = [t, t2]

    arena_h.close()
    arena_h = ExitStack()
    whi = Ring([sb(f"wh{i}", [128, 2048], stack=arena_h) for i in range(NHI)])
    wlo = Ring([sb(f"wl{i}", [128, 2048], stack=arena_h) for i in range(NHI)])
    for tile in whi.tiles + wlo.tiles:
        tile.rel = [T.now()]
    nxt = gather(idx[:, 0:1], tix_)
    xo, txo = turn_x(*nxt)
    nxt = gather(idx[:, 2:3], tix_)
    P = Pieces([("e", e) for e in range(NE)])
    for e in range(NE):
        h, half = expert_up(P, xo, txo, selb[:, e:e + 1], tbias)
        ho, tho = turn_h(h, half)
        if e + 1 < NE:
            xo, txo = turn_x(*nxt)
            if e + 2 < NE:
                nxt = gather(idx[:, 2 * e + 4:2 * e + 5], tix_)
        expert_down(P, ho, tho, idx[:, 2 * e + 1:2 * e + 2])

    tob = None
    for ob in range(NOV):
        for E in (T, V, A):
            E.enter([])
        G.enter([])
        q, q2 = scr.take(), scr.take()
        sel = q[:, 0:32]
        t = ts(sel, io32, ovl[:, ob:ob + 1], ALU.is_equal, q.rel)
        p4 = q[:, 32:160].rearrange("p (n e) -> p n e", n=NB)
        r4 = q[:, 160:288].rearrange("p (n e) -> p n e", n=NB)
        t2 = tt(p4, posm[:, :, :], bcm(sel, NB, 32), ALU.mult, t)
        t3 = tt(r4, vals[:, :, :, 1], bcm(sel, NB, 32), ALU.mult, t)
        t2 = red(q[:, 288:292], p4, ALU.add, t2)
        t2 = ts(q[:, 288:292], q[:, 288:292], ovl[:, 16 + ob:17 + ob], ALU.subtract, t2)
        pr_ = q[:, 296:304].rearrange("p (n a) -> p n a", a=2)
        t3 = red(pr_[:, :, 1], r4, ALU.add, t3)
        t3 = vcopy(pr_[:, :, 0], C("tok"), t3)
        for blk in range(NB):
            t = ts(q2[:, 128 * blk:128 * blk + 128], C("iota"), q[:, 288 + blk:289 + blk], ALU.is_equal, t2, q2.rel)
        b = ps.take()
        T.wait(b.rel, t, t3)
        for blk in range(NB):
            t = mmt(b[:, 0:2], q2[:, 128 * blk:128 * blk + 128], pr_[:, blk, :], blk == 0, blk == 3)
        q2.free(t)
        V.wait(tob)
        vcopy(idxo[:, 0:1], b[:, 0:1], t)
        t = ts(idxo[:, 1:2], b[:, 1:2], 4096.0, ALU.add, t)
        b.free(t)
        s_ox, s_oo = sem(f"s_ox{ob}"), sem(f"s_oo{ob}")
        nxt = gather(idxo[:, 0:1], t, s_ox)
        tb2 = ts(selb[:, 32:33], C("pmod")[0:96, :], ovl[0:96, ob:ob + 1], ALU.is_equal, tob)
        q.free(t)
        xo, txo = turn_x(*nxt)
        P = Pieces([("o", ob)])
        h, half = expert_up(P, xo, txo, selb[:, 32:33], tb2)
        ho, tho = turn_h(h, half)
        o = expert_down(P, ho, tho, idxo[:, 1:2], s_oo)
        tob = G.do(lambda e: e.memset(gfl[:, :], 0.0), o.rel, tob)
        o.rel = [tob]
        for E in (T, V, A, G):
            E.leave("nov", ob)

    tog = [(s, s.n) for s in s_og] + [tob]
    yd = yrd.rearrange("(n p j) d -> n p (j d)", p=128, j=4)
    arena_h.close()
    arena_h = ExitStack()
    hfl = sb("yl", [128, 4096], stack=arena_h)
    s_yl = [sem(f"s_yl{i}") for i in range(4)]
    ysum = [x.ap for x in xg.tiles + ac.tiles]
    th_ = T.now()
    tyl = [G.dma(s_yl[i], hfl[:, D * i:D * i + D], yd[0, :, D * i:D * i + D], tog, th_) for i in range(4)]
    tys = []
    V.wait(th_, *tog)
    for blk in range(NB):
        for j in range(4):
            src = hfl[:, D * j:D * j + D]
            if j == 0:
                t = ts(ysum[blk][:, :], src, gt[:, blk, 0:1], ALU.mult, tyl[0])
            else:
                t = stt(ysum[blk][:, :], src, gt[:, blk, j:j + 1], ysum[blk][:, :], ALU.mult, ALU.add, t, tyl[j])
            if blk + 1 < NB:
                tyl[j] = G.dma(s_yl[j], src, yd[blk + 1, :, D * j:D * j + D], t)
        tys.append(t)
    T.wait(tbd, tgmT)
    for k in range(8):
        b = ps.take()
        T.wait(b.rel)
        for blk in range(NB):
            sl = slice(128 * blk, 128 * blk + 128)
            mm(b[:, sl], ysum[blk][:, 128 * k:128 * k + 128], ident, True, False, tys[blk])
            f = mmt if blk == NB - 1 else mm
            t = f(b[:, sl], bdn[:, 128 * k:128 * k + 128], gmT[:, sl], False, True)
        tx = stt(xT[:, k, :], b[:, :], modT[:, 40 + k:41 + k], xT[:, k, :], ALU.mult, ALU.add, t)
        b.free(tx)
    barrier()
    arena_h.close()
    arena.close()
    if dbg == "block":
        return finish(nc, ctx, T, V, A, G, Y, io, xT, tx, sem)

    arena = ctx.enter_context(ExitStack())
    scr.idle += [Tile(scr, NSCR + i, sb(f"scx{i}", [128, 512], stack=arena)) for i in range(4)]
    hT = sb("h2", [128, 8, S], stack=arena)
    qk = sb("qk", [128, 8, S], stack=arena)
    sv = sb("sv", [128, NB, 512], stack=arena)
    nq = sb("nq", [128, 4, S], stack=arena)
    ksT = sb("ksT", [128, S], stack=arena)
    kwT = sb("kwT", [128, S], stack=arena)
    nv = sb("nv", [128, NB, 256], stack=arena)
    zs = sb("zs", [128, 8, S], stack=arena)
    gates = sb("gates", [128, NB, 24], stack=arena)
    kcT = sb("kcT", [128, 32], stack=arena)
    vcb = C("room").rearrange("p (g n) -> p g n", g=2)
    cosR = C("causal").rearrange("p (n d) -> p n d", n=NB)
    sinR = C("strict").rearrange("p (n d) -> p n d", n=NB)
    ccs = C("rw")[0:32, 0:64]
    posi = sb("posi", [128, NB], I32, stack=arena)
    posf = sb("posf", [128, NB + 1], stack=arena)
    s_p = sem("s_p")
    t = G.dma(s_p, posi[:, :], io["pos"])
    tpo = vcopy(posf[:, 0:NB], posi[:, :], t)
    tvz = V.do(lambda e: e.memset(vcb[:, :, :], 0.0))
    b = ps.take()
    T.wait(b.rel, tpo)
    av = C("avg").rearrange("p (n c) -> p n c", n=NB)
    for blk in range(NB):
        t = mmt(b[0:32, 0:1], av[:, blk, :], posf[:, blk:blk + 1], blk == 0, blk == 3)
    tpc = vcopy(posf[0:32, NB:NB + 1], b[0:32, 0:1], t)
    b.free(tpc)
    C1 = 6.28125
    C2 = math.floor((2 * math.pi - C1) * 2 ** 22) / 2 ** 22
    C3 = 2 * math.pi - C1 - C2
    MAGIC = 12582912.0
    PI = 3.1415925

    def angles(ang, sin, cos, n, P, t, *w):
        q = scr.take()
        k = q[0:P, 0:n]
        t = ts(k, ang, 1.0 / (2 * math.pi), ALU.mult, t, q.rel)
        t = ts(k, k, MAGIC, ALU.add, t)
        t = ts(k, k, MAGIC, ALU.subtract, t)
        for c in (C1, C2, C3):
            t = stt(ang, k, -c, ang, ALU.mult, ALU.add, t)
        t = ts(ang, ang, PI, ALU.min, t, s2=-PI, o2=ALU.max)
        ta = act(sin, ang, ACT.Sin, t)
        t = stt(k, ang, -1.0, ang, ALU.mult, ALU.min, t)
        t = ts(k, k, math.pi / 2, ALU.add, t)
        ta = act(cos, k, ACT.Sin, t)
        q.free(ta)
        return ta

    q = scr.take()
    for blk in range(NB):
        t = ts(q[:, 32 * blk:32 * blk + 32], C("invf"), posf[:, blk:blk + 1], ALU.mult, tpo, q.rel)
    t = ts(q[0:32, 128:160], C("invf")[0:32, :], posf[0:32, NB:NB + 1], ALU.mult, tpc)
    angles(q[:, 0:128], sinR[:, :, :].rearrange("p n d -> p (n d)"), cosR[:, :, :].rearrange("p n d -> p (n d)"), 128, 128, t)
    trp = angles(q[0:32, 128:160], ccs[:, 32:64], ccs[:, 0:32], 32, 32, t)
    q.free(trp)

    def rope(x, n, P, cos, sin, out, tx_, perm):
        q = scr.take()
        if perm:
            xv = x.rearrange("p (g j e d) -> p g j e d", g=2, j=4, e=2)
            ov = out.rearrange("p (j g e d) -> p g j e d", g=2, j=4, e=2)
            x1, x2, o1, o2 = xv[:, :, :, 0, :], xv[:, :, :, 1, :], ov[:, :, :, 0, :], ov[:, :, :, 1, :]
            u = q[0:P, 0:32 * n].rearrange("p (g j d) -> p g j d", g=2, j=4)
            cb, sb_ = [a.rearrange("p (a b d) -> p a b d", a=1, b=1).to_broadcast([P, 2, 4, 32]) for a in (cos, sin)]
        else:
            xv = x.rearrange("p (n e d) -> p n e d", n=n, e=2)
            ov = out.rearrange("p (n e d) -> p n e d", n=n, e=2)
            x1, x2, o1, o2 = xv[:, :, 0, :], xv[:, :, 1, :], ov[:, :, 0, :], ov[:, :, 1, :]
            u = q[0:P, 0:32 * n].rearrange("p (n d) -> p n d", n=n)
            cb, sb_ = bcm(cos, n, 32), bcm(sin, n, 32)
        t = tt(o1, x1, cb, ALU.mult, tx_, trp)
        t2 = tt(u, x2, sb_, ALU.mult, q.rel)
        t = tt(o1, o1, u, ALU.subtract, t2)
        t2 = tt(o2, x2, cb, ALU.mult)
        t = tt(u, x1, sb_, ALU.mult, t)
        t = tt(o2, o2, u, ALU.add, t)
        q.free(t)
        return t

    def norm_rope(b, c0, n, P, gain, cos, sin, perm, tpe):
        wd = 64 * n
        src = b[0:P, c0:c0 + wd]
        s1, tr_, ta = heads_rstd(src, n, 64, tpe)
        x, o = scr.take(), scr.take()
        xv = x[0:P, 0:wd].rearrange("p (n d) -> p n d", n=n)
        tb_ = tt(xv, src.rearrange("p (n d) -> p n d", n=n), bc(s1, n, 64), ALU.mult, tr_, x.rel)
        t = tt(xv, xv, bcm(gain, n, 64), ALU.mult, tb_)
        V.wait(o.rel)
        t = rope(x[0:P, 0:wd], n, P, cos, sin, o[0:P, 0:wd], t, perm)
        x.free(t)
        return o, t, [ta, tb_]

    def layer(l, tx):
        th = rms(tx, C("ng", 8 * l, 8 * l + 8), None)
        kg = C("kg2", 192 * l, 192 * l + 192)
        qg = C("qg2", 64 * l, 64 * l + 64)
        w = weights((l, "sbq"), 512)
        for c in range(4):
            b, tpe = projT(w, 128 * c, 128, th)
            t1_ = ts(qk[:, c, :], b[:, :], 0.125, ALU.mult, tpe)
            b.free(t1_)
        W.done(tpe)
        w = weights((l, "sbk"), 512)
        for c in range(4):
            b, tpe = projT(w, 128 * c, 128, th)
            t2_ = acopy(qk[:, 4 + c, :], b[:, :], tpe)
            b.free(t2_)
        W.done(tpe)
        w = weights((l, "sbv"), 512)
        tsb = []
        for blk in range(NB):
            b, tpe = projR(w, 0, 512, blk, th)
            t3_ = acopy(sv[:, blk, :], b[:, :], tpe)
            b.free(t3_)
            tsb.append([t1_, t2_, t3_])
        W.done(tpe)

        tn, tkv = [], {}
        tnz = []
        yn, ysb, tysb, tyn, tga = {}, {}, [], [], []

        def turn_k(o, t, dst):
            b = ps.take()
            t = tr(b[:, 0:128], o[:, 0:128], ident, b.rel, t)
            o.free(t)
            t = acopy(dst, b[:, 0:128], t)
            b.free(t)
            return t

        def nsa_proj():
            w = weights((l, "nq"), 512)
            for blk in range(NB):
                sl = slice(128 * blk, 128 * blk + 128)
                b, tpe = projR(w, 0, 512, blk, th)
                if blk == NB - 1:
                    W.done(tpe)
                o, t, rd = norm_rope(b, 0, 8, 128, qg, cosR[:, blk, :], sinR[:, blk, :], True, tpe)
                b.free(*rd)
                yield
                b = ps.take()
                T.wait(b.rel, t)
                for k in range(4):
                    t = tr(b[:, 128 * k:128 * k + 128], o[:, 128 * k:128 * k + 128], ident)
                o.free(t)
                t = ts(nq[:, :, sl], b[:, :].rearrange("p (m t) -> p m t", m=4), 0.125, ALU.mult, t)
                b.free(t)
                tn.append(t)
            w = weights((l, "kv"), 512)
            cmpt = []
            for c in range(2):
                b, tpe = projT(w, 128 * c, 128, th)
                t = acopy(zs[:, 4 + c, :], b[:, :], tpe)
                b.free(t)
                cmpt.append(t)
                yield
            pend = None
            for which, c0, dst in (("kv", 256, ksT), ("kw", 0, kwT)):
                br = 0 if which == "kv" else 1
                if br:
                    w = weights((l, "kw"), 280)
                for blk in range(NB):
                    sl = slice(128 * blk, 128 * blk + 128)
                    b, tpe = projR(w, c0, 280 if br else 256, blk, th)
                    if blk == NB - 1:
                        W.done(tpe)
                    t3 = acopy(nv[:, blk, 128 * br:128 * br + 128], b[:, 128:256], tpe)
                    t4 = None
                    if br:
                        t4 = tkv["gate"] = act(gates[:, blk, :], b[:, 256:280], ACT.Sigmoid, tpe)
                    o, t, rd = norm_rope(b, 0, 2, 128, kg[:, 64 + 64 * br:128 + 64 * br], cosR[:, blk, :],
                                         sinR[:, blk, :], False, tpe)
                    b.free(t3, t4, *rd)
                    if pend:
                        tkv[blk, br] = turn_k(*pend)
                    pend = (o, t, dst[:, sl])
                    yield
            tkv["k"] = turn_k(*pend)
            tkv["v"] = t3
            for kv in range(2):
                xc = [scr.take(), scr.take()]
                xcm = [x[:, :].rearrange("p (m g c) -> p m g c", m=8, g=2) for x in xc]
                o, _ = COL["pe"]
                o += 32 * l + 16 * kv
                txc = []
                for hf in range(2):
                    t2 = V.do(lambda e, x=xc[hf]: e.memset(x[:, :], 0.0), xc[hf].rel, cmpt[kv])
                    V.wait(t2)
                    A.wait(t2, cmpt[kv])
                    for g in range(2):
                        vw = zs[64 * g:64 * g + 64, 4 + kv, :].rearrange("p (c m r) -> p r m c", m=8, r=2)
                        for r in range(2):
                            t3 = (acopy if r else vcopy)(xcm[hf][64 * r:64 * r + 64, :, g, 0:31], vw[:, r, :, hf:hf + 31])
                            txc.append(t3)
                    pv = cst[:, o + 8 * hf:o + 8 * hf + 8].rearrange("p (m o) -> p m o", o=1).to_broadcast([128, 8, 64])
                    xv = xc[hf][:, :].rearrange("p (m c) -> p m c", m=8)
                    txc.append(tt(xv, xv, pv, ALU.add, txc))
                slot, tw = W.get((l, "w1", kv))
                wv = slot[:, :].rearrange("p (k n) -> p k n", k=16)
                yield
                b = ps.take()
                T.wait(tw, txc, b.rel)
                for k in range(16):
                    f = mmt if k == 15 else mm
                    t = f(b[0:64, 0:256], xc[k // 8][:, 64 * (k % 8):64 * (k % 8) + 64], wv[:, k, :], k == 0, k == 15)
                W.done(t)
                xc[0].free(t)
                xc[1].free(t)
                q, z = scr.take(), scr.take()
                t = acopy(q[0:64, 256:512], b[0:64, 0:256], t, q.rel)
                b.free(t)
                yield
                b = ps.take()
                T.wait(t, b.rel)
                for m in range(2):
                    t = tr(b[:, 64 * m:64 * m + 64], q[0:64, 256 + 128 * m:384 + 128 * m], ident[0:64, 0:64])
                o, _ = COL["cb1"]
                o += 4 * l + 2 * kv
                zc = z[:, 0:128]
                for m in range(2):
                    t3 = ts(z[:, 64 * m:64 * m + 64], b[:, 64 * m:64 * m + 64], cst[:, o + m:o + m + 1], ALU.add, t, z.rel)
                b.free(t3)
                t3 = act(q[:, 0:128], zc, ACT.Sigmoid, t3)
                t3 = tt(zc, zc, q[:, 0:128], ALU.mult, t3)
                zv = zc.rearrange("p (m g c) -> p g m c", g=2, m=2)
                o, _ = COL["cw2"]
                o += 256 * l + 128 * kv
                if kv == 0:
                    yield
                    b = ps.take()
                    T.wait(b.rel, t3)
                    for g in range(2):
                        for m in range(2):
                            f = mmt if g == 1 and m == 1 else mm
                            t = f(b[0:32, 64 * g:64 * g + 64], zv[:, g, m, :], cst[:, o + 64 * m:o + 64 * m + 64], m == 0, m == 1)
                    q.free(t3)
                    z.free(t)
                    ko, t, rd = norm_rope(b, 0, 2, 32, kg[0:32, 0:64], ccs[:, 0:32], ccs[:, 32:64], False, t)
                    b.free(*rd)
                    yield
                    b = ps.take()
                    t = tr(b[:, 0:32], ko[0:32, 0:128], ident[0:32, 0:32], b.rel, t)
                    ko.free(t)
                    tkv["ck"] = acopy(kcT[:, :], b[:, 0:32], t)
                    b.free(tkv["ck"])
                else:
                    qv = q[:, 0:512].rearrange("p (a r c) -> p a r c", a=4, r=4)
                    t = vcopy(qv, zc.rearrange("p (a r c) -> p a r c", a=4, r=1).to_broadcast([128, 4, 4, 32]), t3)
                    z.free(t)
                    yield
                    b = ps.take()
                    T.wait(b.rel, t)
                    for g in range(2):
                        for m in range(2):
                            f = mmt if g == 1 and m == 1 else mm
                            t = f(b[:, 64 * g:64 * g + 64], q[:, 128 * (2 * m + g):128 * (2 * m + g) + 128],
                                  cst[:, o + 64 * m:o + 64 * m + 64], m == 0, m == 1)
                    q.free(t)
                    V.wait(tvz)
                    for r in range(4):
                        pr = slice(32 * r, 32 * r + 32)
                        t2 = vcopy(vcb[pr, :, 64 * r:64 * r + 64], b[pr, 0:128].rearrange("p (g d) -> p g d", g=2), t)
                    tkv["cv"] = t2
                    b.free(t2)
            w = weights((l, "nz"), 512)
            for c in range(4):
                b, tpe = projT(w, 128 * c, 128, th)
                q = scr.take()
                t = act(q[:, :], b[:, :], ACT.Sigmoid, tpe, q.rel)
                t = tt(zs[:, 4 + c, :], b[:, :], q[:, :], ALU.mult, t, T.now())
                b.free(t)
                q.free(t)
                tnz.append(t)
                if c == 3:
                    W.done(tpe)
                yield

        def compressed(i):
            sl = slice(128 * i, 128 * i + 128)
            y = yn[i] = scr.take()
            q = scr.take()
            pv = q[:, 0:256].rearrange("p (n c) -> p n c", n=8)
            cm = C("cmask", 32 * i, 32 * i + 32)
            for g in range(2):
                pr = slice(64 * g, 64 * g + 64)
                b = ps.take()
                T.wait(b.rel, tkv["ck"], tn)
                for j in range(4):
                    f = mmt if j == 3 else mm
                    t = f(b[:, 32 * j:32 * j + 32], nq[pr, j, sl], kcT[pr, :], True, True)
                t = tt(pv[:, 4 * g:4 * g + 4, :], b[:, 0:128].rearrange("p (n c) -> p n c", n=4), bcm(cm, 4, 32), ALU.add, t, q.rel)
                b.free(t)
            s1 = stat(8)
            t = red(s1, pv, ALU.max, t)
            t = tt(pv, pv, bc(s1, 8, 32), ALU.subtract, t)
            t = act(q[:, 0:256], q[:, 0:256], ACT.Exp, t)
            s2 = stat(8)
            t = red(s2, pv, ALU.add, t)
            t = rec(s2, s2, t)
            t = stt(s2, s2, C("cany", i, i + 1), gates[:, i, 0:8], ALU.mult, ALU.mult, t, tkv["gate"])
            t = tt(pv, pv, bc(s2, 8, 32), ALU.mult, t)
            yield
            b = ps.take()
            T.wait(b.rel, t)
            for g in range(2):
                t = tr(b[:, 128 * g:128 * g + 128], q[:, 128 * g:128 * g + 128], ident)
            q.free(t)
            p = scr.take()
            t = acopy(p[:, 0:256], b[:, 0:256], t, p.rel)
            b.free(t)
            yield
            b = ps.take()
            T.wait(b.rel, t, tkv["cv"])
            for g in range(2):
                t = mmt(b[:, 256 * g:256 * g + 256], p[:, 128 * g:128 * g + 128], vcb[:, g, :], True, True)
            p.free(t)
            t = vcopy(y[:, :], b[:, :], t, y.rel)
            b.free(t)
            yield

        def outer():
            w = weights((l, "sbz"), 512)
            for c in range(4):
                b, tpe = projT(w, 128 * c, 128, th)
                q = scr.take()
                t = act(q[:, :], b[:, :], ACT.Tanh, tpe, q.rel, scale=0.5)
                t = stt(q[:, :], q[:, :], 1.0, b[:, :], ALU.add, ALU.mult, t)
                b.free(t)
                t = stt(zs[:, c, :], q[:, :], 0.5, zs[:, c, :], ALU.mult, ALU.mult, t, tysb)
                q.free(t)
                tnz.append(t)
                if c == 3:
                    W.done(tpe)
            yield
            tq = T.now()
            for j in range(2):
                w = weights((l, "ga", j), 512)
                for c in range(4):
                    b, tpe = projT(w, 128 * c, 128, th)
                    t = act(qk[:, 4 * j + c, :], b[:, :], ACT.Tanh, tpe, tq, scale=0.5)
                    b.free(t)
                    tga.append(t)
                    if c == 3:
                        W.done(tpe)
                    yield

        def put_y(y, t, a, sl):
            b = ps.take()
            T.wait(b.rel, t)
            for k in range(4):
                tp = tr(b[:, 128 * k:128 * k + 128], y[:, 128 * k:128 * k + 128], ident)
            y.free(tp)
            bv = b[:, :].rearrange("p (m t) -> p m t", m=4)
            zv = zs[:, 4 * a:4 * a + 4, sl]
            if a == 0:
                t = vcopy(zv, bv, tp)
                tysb.append(t)
            else:
                t = tt(zv, bv, zv, ALU.mult, tp, tnz)
                tyn.append(t)
            b.free(t)

        def fin_sb(h, i):
            def fin(b, t, u):
                if h == 0:
                    ysb[i] = scr.take()
                y = ysb[i]
                t = vcopy(y[:, 64 * h:64 * h + 64], b[:, 0:64], t, y.rel if h == 0 else None)
                if h == 7:
                    put_y(y, t, 0, slice(128 * i, 128 * i + 128))
                return t
            return fin

        def fin_n(n, br, i):
            def fin(b, t, u):
                y = yn[i]
                r = stat(2)
                t2 = rec(r[:, 0:1], u.rs, u.tp)
                t2 = tt(r[:, 1:2], r[:, 0:1], gates[:, i, 8 * br + n:8 * br + n + 1], ALU.mult, t2, tkv["gate"])
                o = y[:, 64 * n:64 * n + 64]
                t = stt(o, b[:, 0:64], r[:, 1:2], o, ALU.mult, ALU.add, t, t2)
                if n == 7 and br == 2:
                    put_y(y, t, 1, slice(128 * i, 128 * i + 128))
                return t
            return fin

        units = []
        for i in range(NB):
            for h in range(8):
                pr = slice(64 * (h % 2), 64 * (h % 2) + 64)
                units.append(Unit("stick", qk[pr, h // 2, :], qk[pr, 4 + h // 2, :], i,
                                  lambda k, h=h: sv[:, k, 64 * h:64 * h + 64], fin_sb(h, i), tsb[i]))
        f1 = Fill(nsa_proj(), *[compressed(i) for i in range(NB)])
        attend(units, lambda t: f1.step(NF1))
        f1.drain()
        units = []
        for i in range(NB):
            for br, kT in ((1, ksT), (2, kwT)):
                for n in range(8):
                    g, j = n // 4, n % 4
                    pr = slice(64 * g, 64 * g + 64)
                    c0 = 128 * (br - 1) + 64 * g
                    units.append(Unit("soft", nq[pr, j, :], kT[pr, :], i, lambda k, c0=c0: nv[:, k, c0:c0 + 64],
                                      fin_n(n, br, i), [tn, tkv["k"], tkv["v"]]))
        f2 = Fill(outer())
        attend(units, lambda t: f2.step(1 if t % NF2 == 0 else 0))
        f2.drain()

        mg = qk
        tmg = []
        for j in range(2):
            slot, tw = W.get((l, "up", j))
            up = slot[:, :].rearrange("p (a k n) -> p a k n", a=2, k=4)
            T.wait(tw, tyn, tnz)
            s_, tw = W.get((l, "gb", j))
            gb = s_[:, :].rearrange("p (k n) -> p k n", k=8)
            T.wait(tw)
            for c in range(4):
                f = 4 * j + c
                b, tpe = projT(gb, 128 * c, 128, th)
                q = scr.take()
                tq = act(q[:, :], b[:, :], ACT.Tanh, tpe, q.rel, scale=0.5)
                b.free(tq)
                b, tpe = projT(up[:, 0, :, :], 128 * c, 128, [None] * 4, n=4, src=zs[:, 0:4, :])
                t = stt(mg[:, f, :], mg[:, f, :], 1.0, b[:, :], ALU.add, ALU.mult, tpe, tga)
                b.free(t)
                b, tpe = projT(up[:, 1, :, :], 128 * c, 128, [None] * 4, n=4, src=zs[:, 4:8, :])
                t2 = stt(q[:, :], q[:, :], 1.0, b[:, :], ALU.add, ALU.mult, tpe, tq)
                b.free(t2)
                t = tt(mg[:, f, :], mg[:, f, :], q[:, :], ALU.add, t, t2)
                q.free(t)
                tmg.append(t)
            W.done(tpe)
            W.done(tpe)
        tx = add_out(lambda j: (l, "wout", j), mg, tmg, 0.5)
        barrier()
        return tx

    for l in range(2):
        tx = layer(l, tx)
        if dbg == f"layer{l}":
            break
    return finish(nc, ctx, T, V, A, G, Y, io, xT, tx, sem)


def finish(nc, ctx, T, V, A, G, Y, io, xT, tx, sem):
    s_out = sem("s_out")
    t = Y.dma(s_out, io["out"].rearrange("(k p) t -> p k t", p=128), xT[:, :, :], tx)
    Y.wait(t)
    block = ctx.enter_context(nc.Block())

    @block.sync
    def _(e):
        Y.flush(e)

    @block.scalar
    def _(e):
        A.flush(e)

    @block.gpsimd
    def _(e):
        G.flush(e)

    @block.tensor
    def _(e):
        T.flush(e)

    @block.vector
    def _(e):
        V.flush(e)


def _cols(a, k):
    return np.ascontiguousarray(a.reshape(k, 128).T)


def _rows(a):
    return np.broadcast_to(a.reshape(1, -1), (128, a.size))


def _layout(i):
    p = np.arange(128)[:, None]
    f = np.arange(128)[None, :]
    tok = 128 * np.arange(NB)[None, :] + p
    c32 = np.arange(32)
    out = {}
    out["ident"] = p == f
    out["iota"] = f + 0 * p
    out["tri"] = p < f
    out["causal"] = np.where(f > p, NEG, 0.0)
    out["strict"] = np.where(f >= p, NEG, 0.0)
    out["invf"] = _rows(10000.0 ** (-np.arange(32, dtype=np.float32) / np.float32(32)))
    inside = (tok[:, :, None] >= 16 * c32) & (tok[:, :, None] < 16 * c32 + 32) & (c32 < 31)
    out["avg"] = (inside / 32.0).reshape(128, -1)
    seen = (16 * c32 + 31 <= tok[:, :, None]) & (c32 < 31)
    out["cmask"] = np.where(seen, 0.0, NEG).reshape(128, -1)
    out["cany"] = tok >= 31
    out["tok"] = tok
    out["code"] = _rows(np.arange(96) + 32)
    out["thr"] = _rows(np.repeat([128, 256, 384], 32))
    out["ob"] = _rows(np.arange(16))
    out["c"] = _cols(i["c"][0], 8)
    out["ada_b"] = _cols(i["ada_b"][0], 48)
    out["n1"] = _cols(i["norm1_g"][0], 8)
    out["n2"] = _cols(i["norm2_g"][0], 8)
    out["ng"] = np.concatenate([_cols(i["norm_g_2"][l], 8) for l in range(2)], 1)
    for n, m in (("aqg", "a_q_gain"), ("akg", "a_k_gain"), ("aog", "a_out_gain"), ("bqg", "b_q_gain"),
                 ("bkg", "b_k_gain"), ("cog", "c_out_gain")):
        out[n] = np.tile(i[m][0], 128 // i[m].shape[1])[:, None]
    out["cbg"] = i["c_b_g"][0][:, None]
    out["lam"] = _rows(np.concatenate([i[f"a_lam_{n}"][0] for n in ("q1", "k1", "q2", "k2")]))
    w = np.zeros((128, 128), np.float32)
    w[0:16] = i["c_w_g2"][0]
    out["wg2"] = w
    out["convw"] = i["d_conv_w"][0].reshape(4, 2, 128).transpose(2, 1, 0)
    for n, m in (("convb", "d_conv_b"), ("dba", "d_b_a"), ("dbx", "d_b_x"), ("dlam", "d_lambda")):
        out[n] = _cols(i[m][0], 2)
    for n, m in (("dwa", "d_w_a"), ("dwx", "d_w_x")):
        w = np.zeros((128, 2, 128), np.float32)
        for k in range(4):
            a = 64 * (k % 2)
            w[a:a + 64, k // 2, a:a + 64] = i[m][0, k]
        out[n] = w
    out["rw"] = i["router_w"][0].reshape(8, 128, 32).transpose(1, 0, 2)
    out["rb"] = _rows(i["router_b"][0])
    out["pmod"] = p % 32
    out["room"] = np.zeros((128, 512))
    out["qg2"] = _rows(i["q_norm_g_2"])
    out["kg2"] = _rows(i["k_norm_g_2"])
    pe = i["cmp_pe_2"].transpose(3, 0, 1, 2)
    out["pe"] = pe.reshape(64, 2, 2, 16, 2).transpose(4, 0, 1, 2, 3)
    out["cb1"] = i["cmp_b1_2"].reshape(2, 2, 2, 128).transpose(3, 0, 1, 2)
    out["cw2"] = i["cmp_w2_2"].reshape(2, 2, 2, 128, 64).transpose(3, 0, 1, 2, 4)
    cst = np.empty((128, NCONST), np.float32)
    for n, (o, k) in COL.items():
        cst[:, o:o + k] = np.asarray(out[n]).reshape(128, k)
    j, t = p, f
    gm = []
    for L in LEVELS:
        if L:
            gm.append((j // (2 * L) == t // (2 * L)) & (j % (2 * L) < L) & (t % (2 * L) >= L))
        else:
            gm.append(j == t)
    return cst, np.concatenate(gm, 1).astype(np.float32)


_WHOLE = ["w_in_2", "cmp_w1_2", "w_up_a_2", "w_up_b_2", "w_out_2"]
_FIRST = ["ada_w", "w_in", "w_out", "exp_w_up", "exp_w_down", "exp_b_up", "exp_b_down"]


def _arrays(inputs):
    i = {k: np.asarray(v) for k, v in inputs.items()}
    cst, gmask = _layout(i)
    arrays = {"cst": cst, "gmask": gmask, "xT": np.ascontiguousarray(i["x"][0].T),
              "pos": np.ascontiguousarray(i["positions_2"][0].reshape(NB, 128).T)}
    for n in _FIRST:
        arrays[n] = i[n][0]
    for n in _WHOLE:
        arrays[n] = i[n]
    return arrays


def kernel(**inputs):
    import concourse.bacc as bacc
    from concourse.bass_utils import run_bass_kernel_spmd

    arrays = _arrays(inputs)
    nc = bacc.Bacc("TRN2", target_bir_lowering=False, num_devices=1)
    io = {n: nc.dram_tensor("in_" + n, a.shape, mybir.dt.from_np(a.dtype), kind="ExternalInput").ap()
          for n, a in arrays.items()}
    io["out"] = nc.dram_tensor("out", (D, S), F32, kind="ExternalOutput").ap()
    build(nc, io)
    r = run_bass_kernel_spmd(nc, [{"in_" + n: a for n, a in arrays.items()}], core_ids=[0])
    return np.ascontiguousarray(r.results[0]["out"].T).reshape(1, S, D)
```

```python
from contextlib import ExitStack
import math

import numpy as np
import concourse.bass as bass
from concourse import mybir

F32 = mybir.dt.float32
F32R = mybir.dt.float32r
BF16 = mybir.dt.bfloat16
I32 = mybir.dt.int32
U32 = mybir.dt.uint32
ALU = mybir.AluOpType
ACT = mybir.ActivationFunctionType
AX = mybir.AxisListType.X

NEG = -1e30
EPS = 1e-6
S = 512
D = 1024
NB = 4
NE = 32
NOV = 15
NSLOT = 3
NSCR = 6
POFF = 5
NHI = 4
NSCX = 6
NPH = 3
LAG = (2, 3)
DEFER = 2
NF0 = 1
ADA_AT = (4, 10, 15, 19, 23, 27, 31, 35)
NF1 = 99
NF2 = 4
LEVELS = [64, 32, 16, 8, 4, 2, 1, 0]

CONST = [
    ("ident", 128), ("causal", 128), ("strict", 128), ("invf", 32),
    ("avg", 128), ("cmask", 128), ("cany", 4), ("tok", 4),
    ("n1", 8), ("n2", 8), ("ng", 16), ("aqg", 1), ("akg", 1), ("aog", 1),
    ("bqg", 1), ("bkg", 1), ("cbg", 1), ("cog", 1), ("convw", 8), ("convb", 2),
    ("dba", 2), ("dbx", 2), ("dlam", 2), ("rb", 32), ("c", 8),
    ("pmod", 1), ("room", 512), ("qg2", 128), ("kg2", 384), ("pe", 64), ("cb1", 8), ("cw2", 512),
    ("dwa", 256), ("dwx", 256),
    ("iota", 128), ("tri", 128), ("wg2", 128), ("lam", 128),
    ("rw", 256), ("code", 96), ("thr", 96), ("ob", 16), ("ada_b", 48),
]
COL = {}
_at = 0
for _n, _w in CONST:
    COL[_n] = (_at, _w)
    _at += _w
NCONST = _at


class Sem:

    def __init__(self, handle):
        self.handle, self.n = handle, 0


class Engine:

    def __init__(self, handle):
        self.sem = Sem(handle)
        self.q = []
        self.stack = []
        self.passed = {}
        self.vals = {}

    def wait(self, *toks):
        for t in toks:
            if t is None:
                continue
            if isinstance(t, list):
                self.wait(*t)
                continue
            sem, n = t
            if self.passed.get(sem, 0) < n:
                self.passed[sem] = n
                self.q.append(lambda e, h=sem.handle, n=n: e.wait_ge(h, n))

    def put(self, fn, *toks):
        self.wait(*toks)
        self.q.append(fn)

    def do(self, fn, *toks):
        self.wait(*toks)
        self.sem.n += 1
        self.q.append(lambda e, h=self.sem.handle: fn(e).then_inc(h, 1))
        return (self.sem, self.sem.n)

    def dma(self, sem, out, in_, *toks):
        self.wait(*toks)
        sem.n += 16
        self.q.append(lambda e: e.dma_start(out, in_).then_inc(sem.handle, 16))
        return (sem, sem.n)

    def now(self):
        return (self.sem, self.sem.n)

    def load(self, name, ap, top, *toks):
        self.wait(*toks)

        def fn(e):
            self.vals[name] = e.value_load(ap, min_val=0, max_val=top)
        self.q.append(fn)

    def enter(self, sems):
        self.stack.append((self.q, dict(self.passed), [(s, s.n) for s in [self.sem] + sems]))
        self.q = []

    def leave(self, name, thr):
        body, (self.q, self.passed, before) = self.q, self.stack.pop()
        moved = [(s, n, s.n - n) for s, n in before if s.n > n]

        def fn(e):
            with e.If(self.vals[name] > thr):
                for f in body:
                    f(e)
            if moved:
                with e.Else():
                    for s, n, k in moved:
                        if n:
                            e.wait_ge(s.handle, n)
                        e.sem_inc(s.handle, k)
        if body:
            self.q.append(fn)

    def flush(self, e):
        for f in self.q:
            f(e)


class Tile:
    def __init__(self, ring, n, ap):
        self.ring, self.n, self.ap, self.rel = ring, n, ap, []

    def __getitem__(self, k):
        return self.ap[k]

    def free(self, *toks):
        assert self not in self.ring.idle
        self.rel = list(toks)
        self.ring.idle.append(self)


class Ring:

    def __init__(self, aps):
        self.idle = [Tile(self, n, a) for n, a in enumerate(aps)]
        self.tiles = list(self.idle)

    def take(self):
        return self.idle.pop(0)


class Stream:

    def __init__(self, eng, slots, sems, items):
        self.eng, self.slots, self.sems, self.items = eng, slots, sems, items
        self.keys = [i[0] for i in items]
        self.sent, self.used, self.freed = 0, 0, 0
        self.toks = {}
        for _ in range(len(slots)):
            self.send(None)

    def send(self, tok):
        if self.sent >= len(self.items):
            return
        n = self.sent
        self.sent += 1
        slot, sem = self.slots[n % len(self.slots)], self.sems[n % len(self.slots)]
        cond, parts = self.items[n][1], self.items[n][2]
        self.eng.wait(tok)
        if cond is not None:
            self.eng.enter([sem])
        for dst, src in parts(slot):
            self.toks[n] = self.eng.dma(sem, dst, src)
        if cond is not None:
            self.eng.leave("nov", cond)

    def get(self, key):
        n = self.used
        assert self.keys[n] == key, (self.keys[n], key)
        self.used += 1
        return self.slots[n % len(self.slots)], self.toks[n]

    def done(self, tok):
        self.freed += 1
        self.send(tok)


def build(nc, io, dbg=None):
    with ExitStack() as ctx:
        program(nc, ctx, io, dbg)


def program(nc, ctx, io, dbg):
    def sem(name):
        return Sem(ctx.enter_context(nc.semaphore(name)))

    def sb(name, shape, dt=F32, stack=ctx):
        return stack.enter_context(nc.sbuf_tensor("t_" + name, shape, dt))

    T, V, A, G, Y = [Engine(ctx.enter_context(nc.semaphore(n))) for n in ("s_pe", "s_dve", "s_act", "s_pool", "s_sp")]
    dump = {}

    def mm(out, lhsT, rhs, start, stop, *w):
        T.put(lambda e: e.matmul(out, lhsT, rhs, start=start, stop=stop, skip_group_check=True), *w)

    def mmt(out, lhsT, rhs, start, stop, *w):
        return T.do(lambda e: e.matmul(out, lhsT, rhs, start=start, stop=stop, skip_group_check=True), *w)

    def tr(out, in_, ident, *w):
        return T.do(lambda e: e.transpose(out, in_, ident), *w)

    def tt(out, a, b, op, *w, E=None):
        return (E or V).do(lambda e: e.tensor_tensor(out, a, b, op), *w)

    def ts(out, a, s1, o1, *w, s2=None, o2=ALU.bypass, E=None):
        return (E or V).do(lambda e: e.tensor_scalar(out, a, s1, s2, o1, o2), *w)

    def stt(out, a, s, b, o1, o2, *w):
        return V.do(lambda e: e.scalar_tensor_tensor(out=out, in0=a, scalar=s, in1=b, op0=o1, op1=o2), *w)

    def red(out, a, op, *w, negate=False):
        return V.do(lambda e: e.tensor_reduce(out, a, AX, op, negate=negate), *w)

    def rec(out, a, *w):
        return V.do(lambda e: e.reciprocal(out, a), *w)

    def vcopy(out, a, *w):
        return V.do(lambda e: e.tensor_copy(out, a), *w)

    def scan(out, a, b, *w):
        return V.do(lambda e: e.tensor_tensor_scan(out, a, b, 0.0, ALU.mult, ALU.add), *w)

    def act(out, a, f, *w, bias=0.0, scale=1.0, acc=None):
        return A.do(lambda e: e.activation(out, a, f, bias=bias, scale=scale, accum_out=acc), *w)

    def acopy(out, a, *w):
        return A.do(lambda e: e.activation(out, a, ACT.Copy), *w)

    cst = sb("cst", [128, NCONST])
    xT = sb("xT", [128, 8, S])
    hT = None
    modT = sb("modT", [128, 48])
    cond = sb("cond", [128, 8])
    ab = sb("ab", [128, 16])
    ones = sb("ones", [128, 128])
    epsc = sb("epsc", [128, 1])
    identb = sb("identb", [128, 128], BF16)
    causb = sb("causb", [128, 128], BF16)
    stricb = sb("stricb", [128, 128], BF16)
    rstd = sb("rstd", [128, S])
    st = sb("st", [128, 512])
    wslot = [sb(f"w{i}", [128, 4096]) for i in range(NSLOT)]
    scr = Ring([sb(f"scr{i}", [128, 512]) for i in range(NSCR)])
    ps = Ring([ctx.enter_context(nc.psum_tensor(f"ps{i}", [128, 512], F32)) for i in range(8)])
    h2d = nc.dram_tensor("h2d", [S, D], F32, kind="Internal").ap()
    yrd = nc.dram_tensor("yrd", [4 * S, D], F32, kind="Internal").ap()

    def C(name, a=0, b=None):
        o, w = COL[name]
        return cst[:, o + a:o + (w if b is None else b)]

    stn = [0]

    def stat(n):
        if stn[0] + n > 512:
            stn[0] = 0
        a = stn[0]
        stn[0] += n
        return st[:, a:a + n]

    items = []

    def kcols(name, w, c0, c1, cond=None):
        n = c1 - c0

        def parts(slot):
            k = w.shape[0] // 128
            return [(slot[:, 0:k * n].rearrange("p (k n) -> p k n", k=k),
                     w[:, c0:c1].rearrange("(k p) n -> p k n", p=128))]
        items.append((name, cond, parts))

    for j in range(4):
        kcols(("ada", j), io["ada_w"], 512 * j, 512 * j + 512)
    WIN = [("g0", 0, 512), ("g1", 512, 1024), ("g2", 1024, 1536), ("g5", 2320, 2832), ("g3", 1536, 2048), ("g4", 2048, 2320)]
    for n, a, b in WIN:
        kcols(("win", n), io["w_in"], a, b)
        for j in {"g5": (4,), "g3": (5,), "g4": range(6, 12)}.get(n, ()):
            kcols(("ada", j), io["ada_w"], 512 * j, 512 * j + 512)
    for j in range(2):
        kcols(("wout", j), io["w_out"], 512 * j, 512 * j + 512)

    SLOTS = [("e", e, q) for e in range(NE + 1) for (e, q) in
             ([(e, q) for q in range(4)] if e < NE else []) + ([(e - 1, q) for q in (4, 5)] if e else [])]
    for tag, e, q in SLOTS:
        if q < 4:
            c0 = (0, 1024, 512, 1536)[q]
            kcols(((tag, e), q), io["exp_w_up"][e], c0, c0 + 512)
        else:
            kcols(((tag, e), q), io["exp_w_down"][e][512 * (q - 4):512 * (q - 4) + 512, :], 0, 1024)

    def over_item(ob, q):
        c0 = (0, 1024, 512, 1536, 0, 0)[q]

        def parts(slot):
            def src():
                v = Y.vals[f"eid{ob}"]
                if q < 4:
                    w = io["exp_w_up"][bass.ds(v, 1), :, c0:c0 + 512]
                    return w.rearrange("a (k p) n -> p (a k) n", p=128)
                w = io["exp_w_down"][bass.ds(v, 1), 512 * (q - 4):512 * (q - 4) + 512, :]
                return w.rearrange("a (k p) n -> p (a k) n", p=128)
            k = 8 if q < 4 else 4
            return [(slot[:, :].rearrange("p (k n) -> p k n", k=k), src)]
        items.append(((("o", ob), q), ob, parts))

    for ob in range(NOV):
        for q in range(6):
            over_item(ob, q)
    W2 = [("sbq", 0, 512), ("sbk", 512, 1024), ("sbv", 1024, 1536), ("nq", 2048, 2560), ("kv", 2560, 3072),
          ("kw", 3072, 3352)]
    for l in range(2):
        for n, a, b in W2:
            kcols((l, n), io["w_in_2"][l], a, b)
        for kv in range(2):
            def parts(slot, l=l, kv=kv):
                return [(slot[:, :].rearrange("p (k n) -> p k n", k=16),
                         io["cmp_w1_2"][l, kv].rearrange("(k p) n -> p k n", p=128))]
            items.append(((l, "w1", kv), None, parts))
        kcols((l, "nz"), io["w_in_2"][l], 3352, 3864)
        kcols((l, "sbz"), io["w_in_2"][l], 1536, 2048)
        for j in range(2):
            kcols((l, "ga", j), io["w_in_2"][l], 3864 + 512 * j, 4376 + 512 * j)
        for j in range(2):
            kcols((l, "gb", j), io["w_in_2"][l], 4888 + 512 * j, 5400 + 512 * j)
        for j in range(2):
            def parts(slot, l=l, j=j):
                return [(slot[:, 2048 * a:2048 * a + 2048].rearrange("p (k n) -> p k n", k=4),
                         io[n][l][:, 512 * j:512 * j + 512].rearrange("(k p) n -> p k n", p=128))
                        for a, n in enumerate(("w_up_a_2", "w_up_b_2"))]
            items.append(((l, "up", j), None, parts))
        for j in range(2):
            kcols((l, "wout", j), io["w_out_2"][l], 512 * j, 512 * j + 512)

    s_c, s_x = sem("s_c"), sem("s_x")
    tc = A.dma(s_c, cst[:, :], io["cst"])
    tx = A.dma(s_x, xT[:, :, :], io["xT"].rearrange("(k p) t -> p k t", p=128))
    Y_dma = Y.dma

    def dyn_dma(sem_, out, in_, *toks):
        Y.wait(*toks)
        sem_.n += 16
        Y.q.append(lambda e: e.dma_start(out, in_() if callable(in_) else in_).then_inc(sem_.handle, 16))
        return (sem_, sem_.n)
    Y.dma = dyn_dma
    W = Stream(Y, wslot, [sem(f"s_w{i}") for i in range(NSLOT)], items)

    t0 = V.do(lambda e: e.memset(ones[:, :], 1.0))
    t1 = V.do(lambda e: e.memset(epsc[:, :], EPS))
    V.wait(tc)
    vcopy(identb[:, :], C("ident"))
    vcopy(causb[:, :], C("causal"))
    tk = vcopy(stricb[:, :], C("strict"))
    for E in (T, A):
        E.wait(tk, tc)
    ident = C("ident")

    a1 = act(cond[:, :], C("c"), ACT.Sigmoid, tc)
    tcond = tt(cond[:, :], cond[:, :], C("c"), ALU.mult, a1)

    def ada(j, pool=False):
        slot, tw = W.get(("ada", j))
        w = slot[:, :].rearrange("p (k n) -> p k n", k=8)
        q = scr.take()
        if pool:
            r = scr.take()
            t = ts(q[:, :], w[:, 0, :], cond[:, 0:1], ALU.mult, tw, tcond, q.rel, E=G)
            t2 = r.rel
            for k in range(1, 8):
                t2 = ts(r[:, :], w[:, k, :], cond[:, k:k + 1], ALU.mult, t2, E=G)
                t2 = t = tt(q[:, :], q[:, :], r[:, :], ALU.add, t, t2, E=G)
            r.free(t)
        else:
            t = ts(q[:, :], w[:, 0, :], cond[:, 0:1], ALU.mult, tw, tcond, q.rel)
            for k in range(1, 8):
                t = stt(q[:, :], w[:, k, :], cond[:, k:k + 1], q[:, :], ALU.mult, ALU.add, t)
        W.done(t)

        def rest():
            b = ps.take()
            T.wait(t, t0, b.rel)
            for n in range(4):
                t2 = mmt(b[:, n:n + 1], q[:, 128 * n:128 * n + 128], ones[:, 0:1], True, True)
            q.free(t2)
            o, _ = COL["ada_b"]
            t2 = tt(modT[:, 4 * j:4 * j + 4], b[:, 0:4], cst[:, o + 4 * j:o + 4 * j + 4], ALU.add, t2, tc)
            b.free(t2)
            return t2
        return rest

    def rms_sum(tx):
        b = ps.take()
        for k in range(8):
            q = scr.take()
            if k % 2:
                t = tt(q[:, :], xT[:, k, :], xT[:, k, :], ALU.mult, tx, q.rel)
            else:
                t = act(q[:, :], xT[:, k, :], ACT.Square, tx, q.rel)
            t = mmt(b[:, :], ones[:, :], q[:, :], k == 0, k == 7, t, b.rel, t0)
            q.free(t)
        t = act(rstd[:, :], b[:, :], ACT.Ln, t, t1, bias=epsc[:, 0:1], scale=1.0 / D)
        b.free(t)
        return act(rstd[:, :], rstd[:, :], ACT.Exp, t, scale=-0.5)

    def rms(tx, tr_, a, bias, *w):
        V.wait(*w)
        out = []
        for k in range(8):
            t = stt(hT[:, k, :], xT[:, k, :], a[:, k:k + 1], rstd[:, :], ALU.mult, ALU.mult, tr_, tx)
            out.append(ts(hT[:, k, :], hT[:, k, :], bias[:, k:k + 1], ALU.add, t))
        return out

    def projT(slot, c0, m, th, n=8, src=None):
        nw = slot.shape[2]
        b = ps.take()
        T.wait(b.rel)
        for k in range(n):
            f = mmt if k == n - 1 else mm
            t = f(b[0:m, :], slot[:, k, c0:c0 + m], src[k] if isinstance(src, list) else (src or hT)[:, k, :], k == 0, k == n - 1, th[k])
        return b, t

    def projR(slot, c0, n, blk, th):
        b = ps.take()
        T.wait(b.rel)
        for k in range(8):
            f = mmt if k == 7 else mm
            t = f(b[:, 0:n], hT[:, k, 128 * blk:128 * blk + 128], slot[:, k, c0:c0 + n], k == 0, k == 7, th[k])
        return b, t

    def weights(key, n):
        slot, tw = W.get(key)
        T.wait(tw)
        return slot[:, 0:8 * n].rearrange("p (k n) -> p k n", k=8)

    def heads_rstd(src, n, hd, *w):
        q = scr.take()
        P = src.shape[0]
        ta = act(q[0:P, 0:n * hd], src, ACT.Square, w and list(w), q.rel)
        s1 = stat(n)[0:P, :]
        t = red(s1, q[0:P, 0:n * hd].rearrange("p (n d) -> p n d", n=n), ALU.add, ta)
        q.free(t)
        t = act(s1, s1, ACT.Sqrt, t, t1, bias=epsc[0:P, 0:1], scale=1.0 / hd)
        t = rec(s1, s1, t)
        return s1, t, ta

    def heads_rstds(srcs, n, hd, w):
        s1 = stat(n * len(srcs))
        for i, src in enumerate(srcs):
            q = scr.take()
            ta = act(q[:, 0:n * hd], src, ACT.Square, w[i], q.rel)
            t = red(s1[:, n * i:n * i + n], q[:, 0:n * hd].rearrange("p (n d) -> p n d", n=n), ALU.add, ta)
            q.free(t)
        t = act(s1, s1, ACT.Sqrt, t, t1, bias=epsc[:, 0:1], scale=1.0 / hd)
        t = rec(s1, s1, t)
        return [(s1[:, n * i:n * i + n], t, ta) for i in range(len(srcs))]

    def bc(ap, n, d):
        return ap.rearrange("p (n o) -> p n o", o=1).to_broadcast([ap.shape[0], n, d])

    def bcm(ap, n, d):
        return ap.rearrange("p (o d) -> p o d", o=1).to_broadcast([ap.shape[0], n, d])

    class Unit:
        def __init__(self, kind, q, k, i, v, fin, deps):
            self.kind, self.q, self.k, self.i, self.v, self.fin, self.deps = kind, q, k, i, v, fin, deps

        def scores(self):
            i, w = self.i, 128 * self.i + 128
            b = ps.take()
            T.wait(b.rel, self.deps)
            mm(b[:, 0:w], self.q[:, 128 * i:w], self.k[:, 0:w], True, False)
            t = mmt(b[:, 128 * i:w], identb[:, :], (causb if self.kind == "soft" else stricb)[:, :], False, True)
            if self.kind == "soft":
                mx = stat(2)
                tm = red(mx[:, 0:1], b[:, 0:w], ALU.max, t, negate=True)
                p = scr.take()
                self.rs = mx[:, 1:2]
                self.tp = act(p[:, 0:w], b[:, 0:w], ACT.Exp, tm, p.rel, bias=mx[:, 0:1], acc=self.rs)
                b.free(self.tp)
                self.p = p
            else:
                a, c = scr.take(), scr.take()
                ta = act(a[:, 0:w], b[:, 0:w], ACT.Sigmoid, t, a.rel, scale=-1.0)
                tb = act(c[:, 0:w], b[:, 0:w], ACT.Sigmoid, c.rel)
                b.free(tb)
                one = ones[:, 0:1].to_broadcast([128, w])
                ta = V.do(lambda e: e.tensor_tensor_scan(a[:, 0:w][:, ::-1], a[:, 0:w][:, ::-1], one, 1.0,
                                                         ALU.mult, ALU.mult), ta, t0)
                self.tp = tt(c[:, 0:w - 1], c[:, 0:w - 1], a[:, 1:w], ALU.mult, ta, tb)
                a.free(self.tp)
                self.p = c

        def turn(self, on_act):
            i, w = self.i, 128 * self.i + 128
            b = ps.take()
            T.wait(b.rel, self.tp)
            for k in range(i + 1):
                t = tr(b[:, 128 * k:128 * k + 128], self.p[:, 128 * k:128 * k + 128], ident)
            self.p.free(t)
            self.pt = scr.take()
            self.tt = (acopy if on_act else vcopy)(self.pt[:, 0:w], b[:, 0:w], t, self.pt.rel)
            b.free(self.tt)

        def mix(self):
            b = ps.take()
            T.wait(b.rel, self.tt)
            for k in range(self.i + 1):
                f = mmt if k == self.i else mm
                t = f(b[:, 0:64], self.pt[:, 128 * k:128 * k + 128], self.v(k), k == 0, k == self.i)
            self.pt.free(t)
            b.free(self.fin(b, t, self))

    def attend(units, filler=None):
        n = len(units)
        for t in range(n + LAG[1]):
            if t < n:
                units[t].scores()
            if 0 <= t - LAG[0] < n:
                units[t - LAG[0]].turn(t % 2 == 0)
            if 0 <= t - LAG[1] < n:
                units[t - LAG[1]].mix()
            while deferred and deferred[0][0] <= t:
                deferred.pop(0)[1]()
            step[0] = t
            if filler is not None:
                filler(t)
        while deferred:
            deferred.pop(0)[1]()

    step, deferred = [0], []

    def defer(fn):
        deferred.append((step[0] + DEFER, fn))

    class Fill:

        def __init__(self, *gens):
            self.gens = list(gens)

        def step(self, n=1):
            while n > 0 and self.gens:
                if next(self.gens[0], self) is self:
                    self.gens.pop(0)
                else:
                    n -= 1

        def drain(self):
            self.step(1 << 30)

    def barrier():
        toks = [E.now() for E in (T, V, A, G)]
        for E in (T, V, A, G):
            E.wait(*toks)

    trs = rms_sum(tx)
    for j in range(4):
        t = ada(j)()
    a1 = ab[:, 0:8]
    t = stt(a1, modT[:, 8:16], 1.0, C("n1"), ALU.add, ALU.mult, t, tc)
    arena = ExitStack()
    hT = sb("h0", [128, 8, S], stack=arena)
    th = rms(tx, trs, a1, modT[:, 0:8], t)
    extra = [Tile(scr, NSCR + i, sb(f"scr{NSCR + i}", [128, 512], stack=arena)) for i in range(12)]
    scr.idle += extra
    aqT = sb("aqT", [128, 2, S], stack=arena)
    akT = sb("akT", [128, 2, S], stack=arena)
    bqT = sb("bqT", [128, 2, S], stack=arena)
    bkT = sb("bkT", [128, 2, S], stack=arena)
    vR = sb("vR", [128, NB, 768], stack=arena)
    cq = sb("cq", [128, S], stack=arena)
    ck = sb("ck", [128, S], stack=arena)
    bcum = sb("bcum", [128, S], stack=arena)
    dx = sb("dx", [128, 2, S + 3], stack=arena)
    dg = sb("dg", [128, 2, S], stack=arena)
    hd_ = dx[:, :, 3:S + 3]
    crs = sb("crs", [128, NB, 256], stack=arena)
    gmask = sb("gmask", [128, len(LEVELS) * 128], stack=arena)
    sta = sb("sta", [128, 256], stack=arena)
    sm = sb("sm", [128, 32], stack=arena)
    glow = sb("glow", [16, S], stack=arena)
    yab = sb("yab", [128, 4, S], stack=arena)
    yT = [yab[:, k, :] for k in range(4)] + [hT[:, k, :] for k in (4, 5)] + [dx[:, c, 3:S + 3] for c in range(2)]
    s_g = sem("s_g")
    tgm = A.dma(s_g, gmask[:, :], io["gmask"])

    q = scr.take()
    lm = C("lam").rearrange("p (a b d) -> p a b d", a=2, b=2)
    t = tt(q[:, 0:64].rearrange("p (a d) -> p a d", a=2), lm[:, :, 0, :], lm[:, :, 1, :], ALU.mult, tc, q.rel)
    t = red(sm[:, 0:2], q[:, 0:64].rearrange("p (a d) -> p a d", a=2), ALU.add, t)
    q.free(t)
    t = act(sm[:, 0:2], sm[:, 0:2], ACT.Exp, t)
    t = tt(sm[:, 2:3], sm[:, 1:2], sm[:, 0:1], ALU.subtract, t)
    tlam = ts(sm[:, 2:3], sm[:, 2:3], 0.2, ALU.subtract, t)
    nlam = sm[:, 2:3]

    def norm_turn(b, tpe, c0, n, hd, outs):
        wdt = n * hd
        s1, tr_, ta = heads_rstd(b[:, c0:c0 + wdt], n, hd, tpe)
        x = scr.take()
        t = tt(x[:, 0:wdt].rearrange("p (n d) -> p n d", n=n), b[:, c0:c0 + wdt].rearrange("p (n d) -> p n d", n=n),
               bc(s1, n, hd), ALU.mult, tr_, x.rel)
        def turn():
            b2 = ps.take()
            T.wait(b2.rel, t)
            nch = wdt // 128
            for k in range(nch):
                t2 = tr(b2[:, 128 * k:128 * k + 128], x[:, 128 * k:128 * k + 128], ident)
            x.free(t2)
            k = 0
            for m, dst, gain, scale in outs:
                t2 = ts(dst, b2[:, 128 * k:128 * k + 128 * m].rearrange("p (m t) -> p m t", m=m), gain, ALU.mult, t2,
                        s2=scale, o2=ALU.mult)
                k += m
            b2.free(t2)
            return t2
        return [t, ta], turn

    tAB = [[] for _ in range(NB)]
    pend = None
    for name in ("g0", "g1", "g2"):
        w = weights(("win", name), 512)
        for blk in range(NB):
            sl = slice(128 * blk, 128 * blk + 128)
            b, tpe = projR(w, 0, 512, blk, th)
            t3 = None
            if name == "g0":
                c0, n, hd = 0, 16, 32
                outs = [(2, aqT[:, :, sl], C("aqg"), 32.0 ** -0.5), (2, akT[:, :, sl], C("akg"), 1.0)]
            elif name == "g1":
                t3 = acopy(vR[:, blk, 0:256], b[:, 0:256], tpe)
                c0, n, hd, outs = 256, 4, 64, [(2, bqT[:, :, sl], C("bqg"), 0.125)]
            else:
                t3 = acopy(vR[:, blk, 256:512], b[:, 256:512], tpe)
                c0, n, hd, outs = 0, 4, 64, [(2, bkT[:, :, sl], C("bkg"), 1.0)]
            r_, turn = norm_turn(b, tpe, c0, n, hd, outs)
            b.free(t3, *r_)
            if pend:
                tAB[pend[1]].append(pend[0]())
            pend = (turn, blk)
            tAB[blk].append(t3)
        W.done(tpe)
    tAB[pend[1]].append(pend[0]())

    td = []

    def group_d():
        w = weights(("win", "g5"), 512)
        tz = V.do(lambda e: e.memset(dx[:, :, 0:3], 0.0))
        tdx, tdg = [], []
        for c in range(2):
            b, t = projT(w, 128 * c, 128, th)
            t = acopy(dx[:, c, 3:S + 3], b[:, :], t)
            b.free(t)
            tdx.append(t)
            yield
        for c in range(2):
            b, tpe = projT(w, 256 + 128 * c, 128, th)
            t = vcopy(dg[:, c, :], b[:, :], tpe)
            b.free(t)
            tdg.append(t)
            if c == 1:
                W.done(tpe)
            yield
        t = act(sm[:, 4:6], C("dlam"), ACT.Abs)
        t = act(sm[:, 4:6], sm[:, 4:6], ACT.Exp, t, scale=-1.0)
        t = act(sm[:, 4:6], sm[:, 4:6], ACT.Ln, t, bias=ones[:, 0:1])
        tls = stt(sm[:, 6:8], C("dlam"), 0.0, sm[:, 4:6], ALU.min, ALU.subtract, t)
        cw = C("convw").rearrange("p (c w) -> p c w", c=2)

        def lru(c):
            xc = scr.take()
            t = ts(xc[:, :], dx[:, c, 3:S + 3], cw[:, c, 3:4], ALU.mult, tdx[c], tz, xc.rel, s2=C("convb", c, c + 1), o2=ALU.add)
            for k in range(3):
                t = stt(xc[:, :], dx[:, c, k:k + S], cw[:, c, k:k + 1], xc[:, :], ALU.mult, ALU.add, t)
            yield 1
            gates = []
            for name, nb in (("dwa", "dba"), ("dwx", "dbx")):
                b = ps.take()
                wv = C(name).rearrange("p (c e) -> p c e", c=2)
                T.wait(b.rel, t)
                tg = mmt(b[:, :], wv[:, c, :], xc[:, :], True, True)
                g = scr.take()
                tg = act(g[:, :], b[:, :], ACT.Sigmoid, tg, g.rel, bias=C(nb, c, c + 1))
                b.free(tg)
                gates.append((g, tg))
            yield 1
            (r, tr_), (ig, ti) = gates
            tla = ts(r[:, :], r[:, :], sm[:, 6 + c:7 + c], ALU.mult, tr_, tls, s2=8.0, o2=ALU.mult)
            th_ = scr.take()
            t2 = act(th_[:, :], r[:, :], ACT.Tanh, tla, th_.rel)
            ta = act(r[:, :], r[:, :], ACT.Exp, tla)
            u = scr.take()
            t3 = ts(u[:, :], th_[:, :], -1.0, ALU.mult, t2, u.rel, s2=1.0, o2=ALU.add)
            t3 = rec(u[:, :], u[:, :], t3)
            t3 = tt(u[:, :], u[:, :], th_[:, :], ALU.mult, t3)
            th_.free(t3)
            t3 = act(u[:, :], u[:, :], ACT.Sqrt, t3, scale=-2.0)
            t4 = tt(ig[:, :], ig[:, :], xc[:, :], ALU.mult, ti)
            xc.free(t4)
            t4 = tt(ig[:, :], ig[:, :], u[:, :], ALU.mult, t4, t3)
            u.free(t4)
            t4 = scan(hd_[:, c, :], r[:, :], ig[:, :], t4, ta)
            r.free(t4)
            ig.free(t4)
            g = scr.take()
            t5 = tt(g[:, :], dg[:, c, :], dg[:, c, :], ALU.mult, tdg[c], g.rel)
            t5 = ts(g[:, :], g[:, :], 0.044715, ALU.mult, t5, s2=1.0, o2=ALU.add)
            t5 = tt(g[:, :], g[:, :], dg[:, c, :], ALU.mult, t5)
            t5 = act(g[:, :], g[:, :], ACT.Sigmoid, t5, scale=2.0 * math.sqrt(2.0 / math.pi))
            t5 = tt(g[:, :], g[:, :], dg[:, c, :], ALU.mult, t5)
            t5 = tt(hd_[:, c, :], hd_[:, c, :], g[:, :], ALU.mult, t5, t4)
            g.free(t5)
            td.append(t5)
            yield 1

        rec_d.extend([lru(0), lru(1)])

    def group_c():
        w = weights(("win", "g3"), 512)
        b, t = projT(w, 0, 128, th)
        tcq = ts(cq[:, :], b[:, :], 32.0 ** -0.5, ALU.mult, t)
        b.free(tcq)
        yield
        b, t = projT(w, 128, 128, th)
        tck = acopy(ck[:, :], b[:, :], t)
        b.free(tck)
        yield
        tv = {}
        for blk in range(NB):
            b, tpe = projR(w, 256, 256, blk, th)
            t = acopy(vR[:, blk, 512:768], b[:, 0:256], tpe)
            b.free(t)
            if blk == NB - 1:
                W.done(tpe)
            yield
        tcv = t
        w = weights(("win", "g4"), 272)
        b, t = projT(w, 0, 16, th)
        tgl = acopy(glow[:, :], b[0:16, :], t)
        b.free(tgl)
        yield
        tcr = []
        for blk in range(NB):
            b, tpe = projR(w, 16, 256, blk, th)
            q = scr.take()
            t = act(q[:, 0:256], b[:, 0:256], ACT.Sigmoid, tpe, q.rel)
            t = tt(crs[:, blk, :], b[:, 0:256], q[:, 0:256], ALU.mult, t)
            b.free(t)
            q.free(t)
            tcr.append(t)
            if blk == NB - 1:
                W.done(tpe)
            yield

        b = ps.take()
        t = mmt(b[:, :], C("wg2")[0:16, :], glow[:, :], True, True, tgl, b.rel)
        q = scr.take()
        tabs = act(q[:, :], b[:, :], ACT.Abs, t, q.rel, bias=C("cbg"))
        ta = act(q[:, :], q[:, :], ACT.Exp, tabs, scale=-1.0)
        ta = act(q[:, :], q[:, :], ACT.Ln, ta, bias=ones[:, 0:1])
        z = scr.take()
        t = ts(z[:, :], b[:, :], C("cbg"), ALU.add, tabs, z.rel, s2=0.0, o2=ALU.min)
        b.free(t)
        t = tt(q[:, :], z[:, :], q[:, :], ALU.subtract, t, ta)
        z.free(t)
        for n in range(NB):
            sl = slice(128 * n, 128 * n + 128)
            t = scan(bcum[:, sl], ones[:, :], q[:, sl], t)
        q.free(t)
        tb = ts(bcum[:, :], bcum[:, :], 1.0 / 16.0, ALU.mult, t)
        bv = bcum[:, :].rearrange("p (n t) -> p n t", n=NB)
        AT = [scr.take() for _ in range(NB)]
        tat = [V.do(lambda e, a=a: e.memset(a[:, :], 0.0), a.rel) for a in AT]
        def level(L):
            if not L:
                return cq, ck, tcq, tck
            f = scr.take()
            nbk = S // (2 * L)
            bl = bcum[:, :].rearrange("p (n t) -> p n t", n=nbk)
            fl = f[:, :].rearrange("p (n t) -> p n t", n=nbk)
            t = tt(fl, bl, bl[:, :, L - 1:L].to_broadcast([128, nbk, 2 * L]), ALU.subtract, tb, f.rel)
            t = act(f[:, :], f[:, :], ACT.Abs, t)
            t = act(f[:, :], f[:, :], ACT.Exp, t, scale=-1.0)
            ql, kl = scr.take(), scr.take()
            tq = tt(ql[:, :], cq[:, :], f[:, :], ALU.mult, t, tcq, ql.rel)
            tk = tt(kl[:, :], ck[:, :], f[:, :], ALU.mult, t, tck, kl.rel)
            f.free(tq, tk)
            return ql, kl, tq, tk

        ahead = level(LEVELS[0])
        yield
        yield
        for li, L in enumerate(LEVELS):
            ql, kl, tq, tk = ahead
            qa, ka = (ql.ap, kl.ap) if L else (ql, kl)
            if li + 1 < len(LEVELS):
                ahead = level(LEVELS[li + 1])
            for h in range(4):
                b = ps.take()
                T.wait(b.rel, tq, tk)
                for n in range(NB):
                    sl = slice(128 * n, 128 * n + 128)
                    f_ = mmt if n == NB - 1 else mm
                    t = f_(b[:, sl], ka[32 * h:32 * h + 32, sl], qa[32 * h:32 * h + 32, sl], True, True)
                m = bcm(gmask[:, 128 * li:128 * li + 128].bitcast(I32), 4, 128)
                tat[h] = V.do(lambda e, h=h, b=b, m=m: e.copy_predicated(
                    AT[h][:, :].rearrange("p (n t) -> p n t", n=NB), m, b[:, :].rearrange("p (n t) -> p n t", n=NB)),
                    t, tat[h], tgm)
                b.free(tat[h])
                if h % 2:
                    yield
            if L:
                ql.free(t)
                kl.free(t)
        qe, kd = scr.take(), scr.take()
        t = act(qe[:, :], bcum[:, :], ACT.Exp, tb, qe.rel)
        tqe = tt(qe[:, :], qe[:, :], cq[:, :], ALU.mult, t, tcq)
        t = tt(kd[:, :].rearrange("p (n t) -> p n t", n=NB), bv[:, :, 127:128].to_broadcast([128, NB, 128]), bv,
               ALU.subtract, tb, kd.rel)
        t = act(kd[:, :], kd[:, :], ACT.Exp, t)
        tkd = tt(kd[:, :], kd[:, :], ck[:, :], ALU.mult, t, tck)
        teb = act(sm[:, 16:20], bv[:, :, 127], ACT.Exp, tb)
        tst = None
        tsz = V.do(lambda e: e.memset(sta[:, :], 0.0))
        for n in range(NB):
            sl = slice(128 * n, 128 * n + 128)
            o = ps.take()
            T.wait(o.rel, tat, tcv, tst, tqe)
            if n:
                mm(o[:, 0:256], qe[:, sl], sta[:, :], True, False)
            for h in range(4):
                f_ = mmt if h == 3 else mm
                t = f_(o[:, 64 * h:64 * h + 64], AT[h][:, sl], vR[:, n, 512 + 64 * h:576 + 64 * h], n == 0, True)
            to = t
            if n < NB - 1:
                b = ps.take()
                t = tr(b[:, 0:128], kd[:, sl], ident, b.rel, tkd)
                kr = scr.take()
                t = acopy(kr[:, 0:128], b[:, 0:128], t, kr.rel)
                b.free(t)
                yield
                b = ps.take()
                t = mmt(b[:, 0:256], kr[:, 0:128], vR[:, n, 512:768], True, True, t, b.rel)
                kr.free(t)
                V.wait(to)
                for h in range(4):
                    pr = slice(32 * h, 32 * h + 32)
                    hs = slice(64 * h, 64 * h + 64)
                    if n == 0:
                        t2 = vcopy(sta[pr, hs], b[pr, hs], t, tsz)
                    else:
                        t2 = stt(sta[pr, hs], sta[pr, hs], sm[pr, 16 + n:17 + n], b[pr, hs], ALU.mult, ALU.add, t, teb, tst)
                b.free(t2)
                tst = t2
            s1, t2, ta = heads_rstd(o[:, 0:256], 4, 64, to)
            y = scr.take()
            yv = y[:, 0:256].rearrange("p (n d) -> p n d", n=4)
            t = tt(yv, o[:, 0:256].rearrange("p (n d) -> p n d", n=4), bc(s1, 4, 64), ALU.mult, t2, y.rel)
            o.free(t, ta)
            t = tt(y[:, 0:256], y[:, 0:256], crs[:, n, :], ALU.mult, t, tcr[n])
            yield
            b = ps.take()
            T.wait(b.rel, t)
            for k in range(2):
                t = tr(b[:, 128 * k:128 * k + 128], y[:, 128 * k:128 * k + 128], ident)
            y.free(t)
            t = ts(hT[:, 4:6, sl], b[:, 0:256].rearrange("p (m t) -> p m t", m=2), C("cog"), ALU.mult, t)
            b.free(t)
            typ.append(t)
        for x in [qe, kd] + AT:
            x.free(T.now())


    units = []
    ystate = {}
    typ = []

    def y_tile(blk):
        if blk not in ystate:
            q = scr.take()
            ystate[blk] = [q, q.rel]
        return ystate[blk]

    def finA(h, m, i):
        def fin(b, t, u):
            y, rel = y_tile(i)
            r = stat(2)
            t2 = rec(r[:, 0:1], u.rs, u.tp)
            o = y[:, 64 * h:64 * h + 64]
            if m == 0:
                return ts(o, b[:, 0:64], r[:, 0:1], ALU.mult, t, t2, rel)
            t2 = tt(r[:, 1:2], r[:, 0:1], nlam, ALU.mult, t2, tlam)
            return stt(o, b[:, 0:64], r[:, 1:2], o, ALU.mult, ALU.add, t, t2)
        return fin

    def finB(h, i):
        def fin(b, t, u):
            y, rel = y_tile(i)
            r = stat(1)
            t2 = rec(r, u.rs, u.tp)
            t = ts(y[:, 256 + 64 * h:320 + 64 * h], b[:, 0:64], r, ALU.mult, t, t2, rel)
            if h == 3:
                finish_ab(i, t)
            return t
        return fin

    def finish_ab(i, t):
        y, _ = ystate[i]
        s1, t2, _ = heads_rstd(y[:, 0:256], 4, 64, t)
        yv = y[:, 0:256].rearrange("p (n d) -> p n d", n=4)
        ty = tt(yv, yv, bc(s1, 4, 64), ALU.mult, t2)

        def rest():
            b = ps.take()
            T.wait(b.rel, ty)
            for k in range(4):
                t = tr(b[:, 128 * k:128 * k + 128], y[:, 128 * k:128 * k + 128], ident)
            y.free(t)
            bv = b[:, :].rearrange("p (m t) -> p m t", m=4)
            sl = slice(128 * i, 128 * i + 128)
            ts(yab[:, 0:2, sl], bv[:, 0:2, :], C("aog"), ALU.mult, t, s2=0.8, o2=ALU.mult)
            t = vcopy(yab[:, 2:4, sl], bv[:, 2:4, :], t)
            b.free(t)
            typ.append(t)

        defer(rest)

    for i in range(NB):
        for h in range(4):
            for m in range(2):
                r = 2 * h + m
                p0 = 32 * (r % 4)
                units.append(Unit("soft", aqT[p0:p0 + 32, r // 4, :], akT[p0:p0 + 32, r // 4, :], i,
                                  lambda k, h=h: vR[:, k, 64 * h:64 * h + 64], finA(h, m, i), tAB[i]))
        for h in range(4):
            p0 = 64 * (h % 2)
            units.append(Unit("soft", bqT[p0:p0 + 64, h // 2, :], bkT[p0:p0 + 64, h // 2, :], i,
                              lambda k, h=h: vR[:, k, 256 + 64 * h:320 + 64 * h], finB(h, i), tAB[i]))
    rec_d = []

    def side():
        n, left, rest = 0, list(range(4, 12)), []
        for g in (group_d(), group_c()):
            for _ in g:
                n += 1
                if left and n in ADA_AT:
                    if len(rest) == 2:
                        rest.pop(0)()
                    rest.append(ada(left[0], left.pop(0) % 2 == 0))
                elif rec_d and next(rec_d[0], 0) == 0:
                    rec_d.pop(0)
                yield
        for r in rest:
            r()
        while left:
            ada(left.pop(0))()

    fill = Fill(side())
    attend(units, lambda t: fill.step(NF0))
    fill.drain()
    tmod = V.now()

    def add_out(key, src, deps, gain):
        txs = []
        for j in range(2):
            slot, tw = W.get(key(j))
            w = slot[:, :].rearrange("p (k n) -> p k n", k=8)
            T.wait(tw, deps)
            for c in range(4):
                b, tpe = projT(w, 128 * c, 128, [None] * 8, src=src)
                f = 4 * j + c
                if isinstance(gain, float):
                    t = stt(xT[:, f, :], b[:, :], gain, xT[:, f, :], ALU.mult, ALU.add, tpe)
                else:
                    t = stt(xT[:, f, :], b[:, :], gain[:, f:f + 1], xT[:, f, :], ALU.mult, ALU.add, tpe, tmod)
                b.free(t)
                txs.append(t)
            W.done(tpe)
        return txs

    tx = add_out(lambda j: ("wout", j), yT, typ + td, modT[:, 16:24])
    barrier()
    for x in extra:
        scr.idle.remove(x)
    arena.close()
    if dbg == "mixer":
        return finish(nc, ctx, T, V, A, G, Y, io, xT, tx, sem)

    arena = ExitStack()
    lg = sb("lg", [128, NB, 32], stack=arena)
    top = sb("top", [128, NB, 8], stack=arena)
    tix = sb("tix", [128, NB, 8], U32, stack=arena)
    tif = sb("tif", [128, NB, 4], stack=arena)
    gt = sb("gt", [128, NB, 4], stack=arena)
    oh = C("room").rearrange("p (n j e) -> p n j e", n=NB, j=4)
    mask = sb("mask", [128, NB, 32], stack=arena)
    posm = sb("posm", [128, NB, 32], stack=arena)
    vals = sb("vals", [128, NB, 32, 2], stack=arena)
    gm = sb("gm", [128, NB, 32], stack=arena)
    gmT = sb("gmT", [32, S], stack=arena)
    cnt = sb("cnt", [128, 32], stack=arena)
    ovl = sb("ovl", [128, 64], stack=arena)
    ovi = sb("ovi", [1, 32], I32, stack=arena)
    idx = sb("idx", [128, 64], U32, stack=arena)
    idxo = sb("idxo", [128, 2], U32, stack=arena)
    gfl = sb("gfl", [128, 1], stack=arena)
    bdn = sb("bdn", [32, D], stack=arena)
    xg = Ring([sb(f"xg{i}", [128, D], stack=arena) for i in range(2)])
    xt = Ring([sb(f"xt{i}", [128, 2 * D], stack=arena) for i in range(2)])
    bsp = sb("bsp", [96, 2 * D], BF16, stack=arena)
    selb = sb("selb", [96, 33], BF16, stack=arena)
    ac = Ring([sb(f"ac{i}", [128, D], stack=arena) for i in range(1)])
    og = Ring([sb(f"og{i}", [128, D], stack=arena) for i in range(1)])
    arena_h = ExitStack()
    hT = sb("h1", [128, 8, S], stack=arena_h)
    s_b, s_h, s_bo = sem("s_b"), sem("s_h"), sem("s_bo")
    s_xg = [sem(f"s_xg{i}") for i in range(2)]
    s_og = [sem(f"s_og{i}") for i in range(2)]
    tbd = G.dma(s_b, bdn[:, :], io["exp_b_down"], G.now())

    trs = rms_sum(tx)
    t = stt(ab[:, 8:16], modT[:, 32:40], 1.0, C("n2"), ALU.add, ALU.mult, tmod)
    th = rms(tx, trs, ab[:, 8:16], modT[:, 24:32], t)

    tst = []
    for blk in range(NB):
        o = (og, ac, xg, xg)[blk].take()
        for hf in range(2):
            b = ps.take()
            T.wait(b.rel)
            for k in range(4):
                t = tr(b[:, 128 * k:128 * k + 128], hT[:, 4 * hf + k, 128 * blk:128 * blk + 128], ident, th[4 * hf + k])
            t = (acopy if hf else vcopy)(o[:, 512 * hf:512 * hf + 512], b[:, :], t)
            b.free(t)
            G.wait(t)
        t = G.dma(s_h, h2d[128 * blk:128 * blk + 128, :], o[:, :])
        o.free(t)
        th2 = t
    th2 = (s_h, 64)
    for r in (og, ac, xg):
        for tile in r.tiles:
            tile.rel = [th2]

    b = ps.take()
    rw = C("rw").rearrange("p (k n) -> p k n", k=8)
    T.wait(b.rel)
    for blk in range(NB):
        for k in range(8):
            f = mmt if k == 7 else mm
            t = f(b[:, 32 * blk:32 * blk + 32], hT[:, k, 128 * blk:128 * blk + 128], rw[:, k, :], k == 0, k == 7, th[k])
    t = tt(lg[:, :, :], b[:, 0:128].rearrange("p (n e) -> p n e", n=NB), bcm(C("rb"), NB, 32), ALU.add, t)
    b.free(t)
    io32 = C("iota", 0, 32)
    tl = t
    ti = []
    for blk in range(NB):
        t = V.do(lambda e, k=blk: e.max(top[:, k, :], lg[:, k, :]), tl)
        t = V.do(lambda e, k=blk: e.max_index(tix[:, k, :], top[:, k, :], lg[:, k, :]), t)
        ti.append(t)
    t = vcopy(tif[:, :, :], tix[:, :, 0:4], *ti)
    for blk in range(NB):
        for j in range(4):
            t2 = ts(oh[:, blk, j, :], io32, tif[:, blk, j:j + 1], ALU.is_equal, t)
    tmk = red(mask[:, :, :], oh[:, :, :, :].rearrange("p n j e -> p n e j"), ALU.add, t2)
    g1 = stat(4)
    t = tt(gt[:, :, :], top[:, :, 0:4], top[:, :, 0:1].to_broadcast([128, NB, 4]), ALU.subtract, ti[-1])
    t = act(gt[:, :, :], gt[:, :, :], ACT.Exp, t)
    t = red(g1, gt[:, :, :], ALU.add, t)
    t = rec(g1, g1, t)
    tgt = tt(gt[:, :, :], gt[:, :, :], bc(g1, NB, 4), ALU.mult, t)
    b = ps.take()
    T.wait(b.rel, tmk)
    for blk in range(NB):
        for k in range(blk + 1):
            f = mmt if k == blk else mm
            t = f(b[:, 32 * blk:32 * blk + 32], C("tri") if k == blk else ones[:, :], mask[:, k, :], k == 0, k == blk)
    for k in range(NB):
        f = mmt if k == 3 else mm
        t = f(b[:, 128:160], ones[:, :], mask[:, k, :], k == 0, k == 3)
    t2 = ts(posm[:, :, :], mask[:, :, :], -1.0, ALU.add, tmk, s2=1e6, o2=ALU.mult)
    tpos = tt(posm[:, :, :], posm[:, :, :], b[:, 0:128].rearrange("p (n e) -> p n e", n=NB), ALU.add, t, t2)
    tcn = vcopy(cnt[:, :], b[:, 128:160], t)
    b.free(tcn)
    q = scr.take()
    qv = q[:, 0:128].rearrange("p (n e) -> p n e", n=NB)
    t = ts(qv, oh[:, :, 2, :], 2.0, ALU.mult, t2, q.rel)
    t = tt(qv, qv, oh[:, :, 1, :], ALU.add, t)
    q2 = scr.take()
    q2v = q2[:, 0:128].rearrange("p (n e) -> p n e", n=NB)
    t3 = ts(q2v, oh[:, :, 3, :], 3.0, ALU.mult, q2.rel)
    t = tt(qv, qv, q2v, ALU.add, t, t3)
    q2.free(t)
    for blk in range(NB):
        tk = C("tok", blk, blk + 1)
        ts(vals[:, blk, :, 0], io32, 0.0, ALU.mult, s2=tk, o2=ALU.add)
        t4 = ts(q[:, 256 + blk:257 + blk], tk, 4.0, ALU.mult, s2=-4096.0, o2=ALU.add)
        t5 = ts(vals[:, blk, :, 1], qv[:, blk, :], q[:, 256 + blk:257 + blk], ALU.add, t, t4)
    q.free(t5)
    tva = t5
    tgm_ = None
    for blk in range(NB):
        for j in range(4):
            if j == 0:
                t = ts(gm[:, blk, :], oh[:, blk, 0, :], gt[:, blk, 0:1], ALU.mult, tgt)
            else:
                t = stt(gm[:, blk, :], oh[:, blk, j, :], gt[:, blk, j:j + 1], gm[:, blk, :], ALU.mult, ALU.add, t)
    b = ps.take()
    T.wait(b.rel, t)
    for blk in range(NB):
        t = tr(b[0:32, 128 * blk:128 * blk + 128], gm[:, blk, :], ident)
    tgmT = acopy(gmT[:, :], b[0:32, :], t)
    b.free(tgmT)
    iv = idx[:, :].rearrange("p (e a) -> p e a", a=2)
    batch = {}

    def table(e):
        g = e // 8
        q = scr.take()
        t = tt(q[:, :].rearrange("p (n s) -> p n s", n=NB), bcm(C("iota"), NB, 128),
               posm[:, :, e:e + 1].to_broadcast([128, NB, 128]), ALU.is_equal, tpos, q.rel)
        yield
        if e % 8 == 0:
            batch[g] = ps.take()
            T.wait(batch[g].rel, tva)
        for blk in range(NB):
            t2 = mmt(batch[g][:, 2 * (e % 8):2 * (e % 8) + 2], q[:, 128 * blk:128 * blk + 128], vals[:, blk, e, :],
                     blk == 0, blk == 3, t)
        q.free(t2)
        if e % 8 == 7:
            bv_ = batch[g][:, 0:16].rearrange("p (e a) -> p e a", a=2)
            vcopy(iv[:, 8 * g:8 * g + 8, 0], bv_[:, :, 0], t2)
            batch[g, "t"] = ts(iv[:, 8 * g:8 * g + 8, 1], bv_[:, :, 1], 4096.0, ALU.add)
            batch[g].free(batch[g, "t"])

    for e in range(8):
        for _ in table(e):
            pass

    sc_n = [0]

    def gather(col, dep, s_=None):
        x = xg.take()
        s_ = s_ or s_xg[x.n]
        G.wait(x.rel, dep, th2)
        s_.n += 16
        G.put(lambda e: e.indirect_dma_start(x[:, :], None, h2d, bass.IndirectOffsetOnAxis(ap=col, axis=0))
              .then_inc(s_.handle, 16))
        return x, (s_, s_.n)

    def r32(ap):
        return ap.bitcast(F32R)

    class Pieces:

        def __init__(self, slots):
            self.keys = [(tag, q, hf) for tag, q in slots for hf in range(2)]
            self.n, self.ready, self.slot, self.last = 0, [], None, []
            for _ in range(2):
                self.split()

        def split(self):
            if self.n == len(self.keys):
                return
            tag, q, hf = self.keys[self.n]
            if hf == 0:
                self.slot = W.get((tag, q))
            slot, tw = self.slot
            raw = slot[:, 2048 * hf:2048 * hf + 2048]
            h, l = whi.take(), wlo.take()
            ta = act(r32(h[:, :]), raw, ACT.Copy, tw, h.rel)
            tl = tt(r32(l[:, :]), raw, h[:, :], ALU.subtract, ta, tw, l.rel, E=G if self.n % 6 == POFF else V)
            self.n += 1
            self.last = (self.last + [tl])[-2:]
            if hf == 1:
                W.done(self.last)
            self.ready.append((h, l, [ta, tl]))

        def take(self):
            return self.ready.pop(0)

        def done(self, piece, t):
            piece[0].free(t)
            piece[1].free(t)
            self.split()

    def parts(dst, b, t, rel):
        ta = act(r32(dst[:, 0:512]), b[:, :], ACT.Copy, t, rel)
        tl = tt(r32(dst[:, 512:1024]), b[:, :], dst[:, 0:512], ALU.subtract, ta, rel)
        b.free(tl)
        return [ta, tl]

    def turn_x(x, tg):
        o = xt.take()
        to = []
        for hf in range(2):
            b = ps.take()
            T.wait(b.rel, tg)
            for k in range(4):
                t = tr(b[:, 128 * k:128 * k + 128], x[:, 512 * hf + 128 * k:512 * hf + 128 * k + 128], ident)
            to.append(parts(o[:, 1024 * hf:1024 * hf + 1024], b, t, o.rel))
        x.free(t)
        return o, to

    def three(out, xs, k, wh, wl, first, last, tok):
        xh, xl = xs[:, 128 * k:128 * k + 128], xs[:, 512 + 128 * k:640 + 128 * k]
        mm(out, r32(xh), r32(wh), first, False)
        mm(out, r32(xh), r32(wl), False, False)
        return (mmt if tok else mm)(out, r32(xl), r32(wh), False, last)

    def expert_up(P, xo, txo, bias, tbias):
        h = ac.take()
        half = []
        for hf in range(2):
            pair = []
            for gl in range(2):
                b = ps.take()
                c0 = 1024 * gl + 512 * hf
                T.wait(txo, b.rel)
                mm(b[:, :], bias.to_broadcast([96, 128]), bsp[:, c0:c0 + 512], True, False, tbias)
                for pc in range(2):
                    piece = P.take()
                    wh = piece[0][:, :].rearrange("p (k n) -> p k n", k=4)
                    wl = piece[1][:, :].rearrange("p (k n) -> p k n", k=4)
                    T.wait(piece[2])
                    for k in range(4):
                        t = three(b[:, :], xo[:, 1024 * pc:1024 * pc + 1024], k, wh[:, k, :], wl[:, k, :],
                                  False, pc == 1 and k == 3, k == 3)
                    P.done(piece, t)
                pair.append((b, t))
            (bg, tg), (bl, tl) = pair
            g, l, s_ = scr.take(), scr.take(), scr.take()
            tg = ts(g[:, :], bg[:, :], 7.0, ALU.min, tg, g.rel)
            bg.free(tg)
            ta = act(s_[:, :], g[:, :], ACT.Sigmoid, tg, s_.rel, scale=1.702)
            tl = ts(l[:, :], bl[:, :], 7.0, ALU.min, tl, l.rel, s2=-7.0, o2=ALU.max)
            bl.free(tl)
            tl = stt(l[:, :], l[:, :], 1.0, g[:, :], ALU.add, ALU.mult, tl)
            g.free(tl)
            t = tt(h[:, 512 * hf:512 * hf + 512], l[:, :], s_[:, :], ALU.mult, tl, ta, h.rel)
            l.free(t)
            s_.free(t)
            half.append(t)
        xo.free(T.now())
        return h, half

    def turn_h(h, half):
        o = xt.take()
        to = []
        for hf in range(2):
            b = ps.take()
            T.wait(b.rel, half[hf])
            for k in range(4):
                t = tr(b[:, 128 * k:128 * k + 128], h[:, 512 * hf + 128 * k:512 * hf + 128 * k + 128], ident)
            to.append(parts(o[:, 1024 * hf:1024 * hf + 1024], b, t, o.rel))
        h.free(t)
        return o, to

    def expert_down(P, ho, tho, col, s_=None):
        o2 = [ps.take(), ps.take()]
        for pc in range(4):
            piece = P.take()
            wh = piece[0][:, :].rearrange("p (k n) -> p k n", k=2)
            wl = piece[1][:, :].rearrange("p (k n) -> p k n", k=2)
            T.wait(piece[2], tho[pc // 2], o2[0].rel, o2[1].rel)
            for k in range(2):
                for n in range(2):
                    t = three(o2[n][:, :], ho[:, 1024 * (pc // 2):1024 * (pc // 2) + 1024], 2 * (pc % 2) + k,
                              wh[:, k, 512 * n:512 * n + 512], wl[:, k, 512 * n:512 * n + 512],
                              pc == 0 and k == 0, pc == 3 and k == 1, k == 1 and n == 1)
            P.done(piece, t)
        ho.free(t)
        o = og.take()
        s_ = s_ or s_og[o.n]
        t1_ = acopy(o[:, 0:512], o2[0][:, :], t, o.rel)
        t2 = vcopy(o[:, 512:1024], o2[1][:, :], t, o.rel)
        o2[0].free(t1_)
        o2[1].free(t2)
        G.wait(t1_, t2)
        s_.n += 16
        G.put(lambda e: e.indirect_dma_start(yrd, bass.IndirectOffsetOnAxis(ap=col, axis=0), o[:, :], None,
                                             bounds_check=4 * S - 1, oob_is_err=False).then_inc(s_.handle, 16))
        o.free((s_, s_.n))
        return o

    bf = [xg.tiles[0], xg.tiles[1]]
    s_bu = sem("s_bu")
    tbu = None
    for hf in range(2):
        u = bf[hf]
        for j in range(3):
            tbu = G.dma(s_bu, u[32 * j:32 * j + 32, :], io["exp_b_up"][:, 1024 * hf:1024 * hf + 1024], u.rel)
    for hf in range(2):
        u = bf[hf]
        dst = bsp[:, 1024 * hf:1024 * hf + 1024]
        t = vcopy(dst, u[0:96, :], tbu)
        for j in (1, 2, 2):
            pr = slice(32 * j, 32 * j + 32)
            t = tt(u[pr, :], u[pr, :], dst[pr, :], ALU.subtract, t)
            t = vcopy(dst[pr, :], u[pr, :], t)
        u.rel = [t]
    t2 = ts(selb[:, 0:32], io32[0:96, :], C("pmod")[0:96, :], ALU.is_equal)
    tbias = [t, t2]

    arena_h.close()
    arena_h = ExitStack()
    whi = Ring([sb(f"wh{i}", [128, 2048], stack=arena_h) for i in range(NHI)])
    wlo = Ring([sb(f"wl{i}", [128, 2048], stack=arena_h) for i in range(NHI)])
    for tile in whi.tiles + wlo.tiles:
        tile.rel = [T.now()]
    nxt = gather(idx[:, 0:1], batch[0, "t"])
    xo, txo = turn_x(*nxt)
    nxt = gather(idx[:, 2:3], batch[0, "t"])
    def overflow_list():
        q, q2 = scr.take(), scr.take()
        fl = q[:, 0:96]
        t = tt(fl.rearrange("p (a e) -> p a e", a=3), bcm(cnt[:, :], 3, 32), C("thr").rearrange("p (a e) -> p a e", a=3),
               ALU.is_gt, tcn, q.rel)
        inc = q[:, 96:192]
        t = scan(inc, ones[:, 0:96], fl, t)
        tno = vcopy(ovi[0:1, 31:32], inc[0:1, 95:96], t)
        t = tt(inc, inc, fl, ALU.mult, tno)
        for ob in range(NOV):
            t2 = ts(q2[:, 0:96], inc, float(ob + 1), ALU.is_equal, t, q2.rel if ob == 0 else t2)
            t2 = tt(q2[:, 0:96], q2[:, 0:96], C("code"), ALU.mult, t2)
            t2 = red(ovl[:, ob:ob + 1], q2[:, 0:96], ALU.add, t2)
        t = ts(ovl[:, 16:31], ovl[:, 0:15], 63.5, ALU.is_gt, t2)
        t = ts(ovl[:, 32:47], ovl[:, 0:15], 95.5, ALU.is_gt, t)
        t = tt(ovl[:, 16:31], ovl[:, 16:31], ovl[:, 32:47], ALU.add, t)
        t = ts(ovl[:, 16:31], ovl[:, 16:31], 1.0, ALU.add, t)
        t = stt(ovl[:, 0:15], ovl[:, 16:31], -32.0, ovl[:, 0:15], ALU.mult, ALU.add, t)
        t = ts(ovl[:, 0:15], ovl[:, 0:15], 0.0, ALU.max, t)
        tov = ts(ovl[:, 16:31], ovl[:, 16:31], 128.0, ALU.mult, t)
        tovi = vcopy(ovi[0:1, 0:15], ovl[0:1, 0:15], tov)
        q.free(tov)
        q2.free(tov)
        for E in (T, V, A, G, Y):
            E.load("nov", ovi[0:1, 31:32], NOV, tovi, tno)
        for ob in range(NOV):
            Y.load(f"eid{ob}", ovi[0:1, ob:ob + 1], NE - 1)
        return tov, tovi

    P = Pieces([((tag, e), q) for tag, e, q in SLOTS])
    held = None
    for e in range(NE):
        a = 8 * (e // 8) + 8 + 2 * (e % 8)
        tables = [table(a + k) for k in range(2)] if e % 8 < 4 and a < NE else []
        for g in tables:
            next(g)
        h, half = expert_up(P, xo, txo, selb[:, e:e + 1], tbias)
        if e == 14:
            overflow_list()
        for g in tables:
            next(g, None)
        if e + 1 < NE:
            xo, txo = turn_x(*nxt)
            if e + 2 < NE:
                nxt = gather(idx[:, 2 * e + 4:2 * e + 5], batch[(e + 2) // 8, "t"])
        if e:
            expert_down(P, *held)
        held = (*turn_h(h, half), idx[:, 2 * e + 1:2 * e + 2])
    expert_down(P, *held)

    tob = None
    for ob in range(NOV):
        for E in (T, V, A):
            E.enter([])
        G.enter([])
        q, q2 = scr.take(), scr.take()
        sel = q[:, 0:32]
        t = ts(sel, io32, ovl[:, ob:ob + 1], ALU.is_equal, q.rel)
        p4 = q[:, 32:160].rearrange("p (n e) -> p n e", n=NB)
        r4 = q[:, 160:288].rearrange("p (n e) -> p n e", n=NB)
        t2 = tt(p4, posm[:, :, :], bcm(sel, NB, 32), ALU.mult, t)
        t3 = tt(r4, vals[:, :, :, 1], bcm(sel, NB, 32), ALU.mult, t)
        t2 = red(q[:, 288:292], p4, ALU.add, t2)
        t2 = ts(q[:, 288:292], q[:, 288:292], ovl[:, 16 + ob:17 + ob], ALU.subtract, t2)
        pr_ = q[:, 296:304].rearrange("p (n a) -> p n a", a=2)
        t3 = red(pr_[:, :, 1], r4, ALU.add, t3)
        t3 = vcopy(pr_[:, :, 0], C("tok"), t3)
        for blk in range(NB):
            t = ts(q2[:, 128 * blk:128 * blk + 128], C("iota"), q[:, 288 + blk:289 + blk], ALU.is_equal, t2, q2.rel)
        b = ps.take()
        T.wait(b.rel, t, t3)
        for blk in range(NB):
            t = mmt(b[:, 0:2], q2[:, 128 * blk:128 * blk + 128], pr_[:, blk, :], blk == 0, blk == 3)
        q2.free(t)
        V.wait(tob)
        vcopy(idxo[:, 0:1], b[:, 0:1], t)
        t = ts(idxo[:, 1:2], b[:, 1:2], 4096.0, ALU.add, t)
        b.free(t)
        s_ox, s_oo = sem(f"s_ox{ob}"), sem(f"s_oo{ob}")
        nxt = gather(idxo[:, 0:1], t, s_ox)
        tb2 = ts(selb[:, 32:33], C("pmod")[0:96, :], ovl[0:96, ob:ob + 1], ALU.is_equal, tob)
        q.free(t)
        xo, txo = turn_x(*nxt)
        P = Pieces([(("o", ob), q) for q in range(6)])
        h, half = expert_up(P, xo, txo, selb[:, 32:33], tb2)
        ho, tho = turn_h(h, half)
        o = expert_down(P, ho, tho, idxo[:, 1:2], s_oo)
        tob = G.do(lambda e: e.memset(gfl[:, :], 0.0), o.rel, tob)
        o.rel = [tob]
        for E in (T, V, A, G):
            E.leave("nov", ob)

    tog = [(s, s.n) for s in s_og] + [tob]
    yd = yrd.rearrange("(n p j) d -> n p (j d)", p=128, j=4)
    arena_h.close()
    arena_h = ExitStack()
    hfl = sb("yl", [128, 4096], stack=arena_h)
    s_yl = [sem(f"s_yl{i}") for i in range(4)]
    ysum = [x.ap for x in xg.tiles + ac.tiles + og.tiles]
    th_ = T.now()
    tyl = [G.dma(s_yl[i], hfl[:, D * i:D * i + D], yd[0, :, D * i:D * i + D], tog, th_) for i in range(4)]
    tys = []
    V.wait(th_, *tog)
    for blk in range(NB):
        for j in range(4):
            src = hfl[:, D * j:D * j + D]
            if j == 0:
                t = ts(ysum[blk][:, :], src, gt[:, blk, 0:1], ALU.mult, tyl[0])
            else:
                t = stt(ysum[blk][:, :], src, gt[:, blk, j:j + 1], ysum[blk][:, :], ALU.mult, ALU.add, t, tyl[j])
            if blk + 1 < NB:
                tyl[j] = G.dma(s_yl[j], src, yd[blk + 1, :, D * j:D * j + D], t)
        tys.append(t)
    T.wait(tbd, tgmT)
    for blk in range(NB):
        sl = slice(128 * blk, 128 * blk + 128)
        for hf in range(2):
            b = ps.take()
            T.wait(b.rel, tys[blk])
            for k in range(4):
                f = 512 * hf + 128 * k
                mm(b[:, 128 * k:128 * k + 128], ysum[blk][:, f:f + 128], ident, True, False)
                t = (mmt if k == 3 else mm)(b[:, 128 * k:128 * k + 128], bdn[:, f:f + 128], gmT[:, sl], False, True)
            for k in range(4):
                f = 4 * hf + k
                tx = stt(xT[:, f, sl], b[:, 128 * k:128 * k + 128], modT[:, 40 + f:41 + f], xT[:, f, sl], ALU.mult, ALU.add, t)
            b.free(tx)
    barrier()
    arena_h.close()
    arena.close()
    if dbg == "block":
        return finish(nc, ctx, T, V, A, G, Y, io, xT, tx, sem)

    arena = ctx.enter_context(ExitStack())
    scr.idle += [Tile(scr, NSCR + i, sb(f"scx{i}", [128, 512], stack=arena)) for i in range(NSCX)]
    scr.idle += [Tile(scr, 100 + i, C(n, 0, 512)) for i, n in enumerate(("dwa", "iota", "rw"))]
    hT = None
    hh = sb("hh", [128, 8, S], F32R, stack=arena)
    hl = sb("hl", [128, 8, S], F32R, stack=arena)
    phi = Ring([sb(f"ph{i}", [128, 1024], F32R, stack=arena) for i in range(NPH)])
    plo = Ring([sb(f"pl{i}", [128, 1024], F32R, stack=arena) for i in range(NPH)])
    qk = sb("qk", [128, 8, S], stack=arena)
    sv = sb("sv", [128, NB, 512], stack=arena)
    nq = sb("nq", [128, 4, S], stack=arena)
    ksT = sb("ksT", [128, S], stack=arena)
    kwT = sb("kwT", [128, S], stack=arena)
    nv = sb("nv", [128, NB, 256], stack=arena)
    zs = xT
    xd = nc.dram_tensor("xd", [128, 8 * S], F32, kind="Internal").ap().rearrange("p (k t) -> p k t", k=8)
    gates = sb("gates", [128, NB, 24], stack=arena)
    kcT = sb("kcT", [128, 32], stack=arena)
    vcb = C("room").rearrange("p (g n) -> p g n", g=2)
    cosR = C("causal").rearrange("p (n d) -> p n d", n=NB)
    sinR = C("strict").rearrange("p (n d) -> p n d", n=NB)
    ccs = sb("ccs", [32, 64], stack=arena)
    posi = sb("posi", [128, NB], I32, stack=arena)
    posf = sb("posf", [128, NB + 1], stack=arena)
    s_p = sem("s_p")
    t = G.dma(s_p, posi[:, :], io["pos"])
    tpo = vcopy(posf[:, 0:NB], posi[:, :], t)
    tvz = V.do(lambda e: e.memset(vcb[:, :, :], 0.0))
    b = ps.take()
    T.wait(b.rel, tpo)
    av = C("avg").rearrange("p (n c) -> p n c", n=NB)
    for blk in range(NB):
        t = mmt(b[0:32, 0:1], av[:, blk, :], posf[:, blk:blk + 1], blk == 0, blk == 3)
    tpc = vcopy(posf[0:32, NB:NB + 1], b[0:32, 0:1], t)
    b.free(tpc)
    C1 = 6.28125
    C2 = math.floor((2 * math.pi - C1) * 2 ** 22) / 2 ** 22
    C3 = 2 * math.pi - C1 - C2
    MAGIC = 12582912.0
    PI = 3.1415925

    def angles(ang, sin, cos, n, P, t, *w):
        q = scr.take()
        k = q[0:P, 0:n]
        t = ts(k, ang, 1.0 / (2 * math.pi), ALU.mult, t, q.rel)
        t = ts(k, k, MAGIC, ALU.add, t)
        t = ts(k, k, MAGIC, ALU.subtract, t)
        for c in (C1, C2, C3):
            t = stt(ang, k, -c, ang, ALU.mult, ALU.add, t)
        t = ts(ang, ang, PI, ALU.min, t, s2=-PI, o2=ALU.max)
        ta = act(sin, ang, ACT.Sin, t)
        t = stt(k, ang, -1.0, ang, ALU.mult, ALU.min, t)
        t = ts(k, k, math.pi / 2, ALU.add, t)
        ta = act(cos, k, ACT.Sin, t)
        q.free(ta)
        return ta

    q = scr.take()
    for blk in range(NB):
        t = ts(q[:, 32 * blk:32 * blk + 32], C("invf"), posf[:, blk:blk + 1], ALU.mult, tpo, q.rel)
    t = ts(q[0:32, 128:160], C("invf")[0:32, :], posf[0:32, NB:NB + 1], ALU.mult, tpc)
    angles(q[:, 0:128], sinR[:, :, :].rearrange("p n d -> p (n d)"), cosR[:, :, :].rearrange("p n d -> p (n d)"), 128, 128, t)
    trp = angles(q[0:32, 128:160], ccs[:, 32:64], ccs[:, 0:32], 32, 32, t)
    q.free(trp)

    def rope(x, n, P, cos, sin, out, tx_, perm):
        q = scr.take()
        if perm:
            xv = x.rearrange("p (g j e d) -> p g j e d", g=2, j=4, e=2)
            ov = out.rearrange("p (j g e d) -> p g j e d", g=2, j=4, e=2)
            x1, x2, o1, o2 = xv[:, :, :, 0, :], xv[:, :, :, 1, :], ov[:, :, :, 0, :], ov[:, :, :, 1, :]
            u = q[0:P, 0:32 * n].rearrange("p (g j d) -> p g j d", g=2, j=4)
            cb, sb_ = [a.rearrange("p (a b d) -> p a b d", a=1, b=1).to_broadcast([P, 2, 4, 32]) for a in (cos, sin)]
        else:
            xv = x.rearrange("p (n e d) -> p n e d", n=n, e=2)
            ov = out.rearrange("p (n e d) -> p n e d", n=n, e=2)
            x1, x2, o1, o2 = xv[:, :, 0, :], xv[:, :, 1, :], ov[:, :, 0, :], ov[:, :, 1, :]
            u = q[0:P, 0:32 * n].rearrange("p (n d) -> p n d", n=n)
            cb, sb_ = bcm(cos, n, 32), bcm(sin, n, 32)
        t = tt(o1, x1, cb, ALU.mult, tx_, trp)
        t2 = tt(u, x2, sb_, ALU.mult, q.rel)
        t = tt(o1, o1, u, ALU.subtract, t2)
        t2 = tt(o2, x2, cb, ALU.mult)
        t = tt(u, x1, sb_, ALU.mult, t)
        t = tt(o2, o2, u, ALU.add, t)
        q.free(t)
        return t

    def norm_rope(b, c0, n, P, gain, cos, sin, perm, tpe, rs=None):
        wd = 64 * n
        src = b[0:P, c0:c0 + wd]
        s1, tr_, ta = rs or heads_rstd(src, n, 64, tpe)
        x, o = scr.take(), scr.take()
        xv = x[0:P, 0:wd].rearrange("p (n d) -> p n d", n=n)
        tb_ = tt(xv, src.rearrange("p (n d) -> p n d", n=n), bc(s1, n, 64), ALU.mult, tr_, x.rel)
        t = tt(xv, xv, bcm(gain, n, 64), ALU.mult, tb_)
        V.wait(o.rel)
        t = rope(x[0:P, 0:wd], n, P, cos, sin, o[0:P, 0:wd], t, perm)
        x.free(t)
        return o, t, [ta, tb_]

    class Split:

        def __init__(self, slots):
            self.keys = [(key, n, p) for key, n in slots for p in range(4)]
            self.n, self.ready, self.slot, self.last = 0, [], None, []
            for _ in range(NPH - 1):
                self.split()

        def split(self):
            if self.n == len(self.keys):
                return
            key, n, p = self.keys[self.n]
            if p == 0:
                self.slot, self.last = W.get(key), []
            slot, tw = self.slot
            raw = slot[:, 2 * n * p:2 * n * p + 2 * n]
            h, l = phi.take(), plo.take()
            ta = act(h[:, 0:2 * n], raw, ACT.Copy, tw, h.rel)
            tl = tt(l[:, 0:2 * n], raw, h[:, 0:2 * n].bitcast(F32), ALU.subtract, ta, tw, l.rel, E=G if p == 3 else V)
            self.n += 1
            self.last.append(tl)
            if p == 3:
                W.done(self.last)
            self.ready.append((h, l, [ta, tl], n))

        def pieces(self):
            for p in range(4):
                h, l, tw, n = self.ready.pop(0)
                T.wait(tw)
                yield p, *[x[:, 0:2 * n].rearrange("p (k n) -> p k n", k=2) for x in (h, l)]
                h.free(T.now())
                l.free(T.now())
                self.split()

    def mulT(out, wh, wl, k, j, c0, first, last, f):
        ws = slice(c0, c0 + 128)
        mm(out, wh[:, j, ws], hh[:, k, :], first, False)
        mm(out, wh[:, j, ws], hl[:, k, :], False, False)
        return f(out, wl[:, j, ws], hh[:, k, :], False, last)

    def mulR(out, wh, wl, k, j, cs, blk, first, last, f):
        ts_ = slice(128 * blk, 128 * blk + 128)
        mm(out, hh[:, k, ts_], wh[:, j, cs], first, False)
        mm(out, hh[:, k, ts_], wl[:, j, cs], False, False)
        return f(out, hl[:, k, ts_], wh[:, j, cs], False, last)

    def four(P, jobs, th, out):
        banks = {}
        for p, wh, wl in P.pieces():
            seen = set()
            for n, (bk, oc, tr_, cs, blk) in enumerate(jobs):
                half = tr_ and blk is not None
                if half and p // 2 != blk:
                    continue
                if bk not in banks:
                    banks[bk] = ps.take()
                    T.wait(banks[bk].rel)
                for j in range(2):
                    k = 2 * p + j
                    T.wait(th[k])
                    f = mmt if j == 1 else mm
                    first = p == (2 * blk if half else 0) and j == 0 and bk not in seen
                    last = j == 1 and p == (2 * blk + 1 if half else 3)
                    o = banks[bk][:, oc]
                    t = (mulT(o, wh, wl, k, j, cs.start, first, last, f) if tr_
                         else mulR(o, wh, wl, k, j, cs, blk, first, last, f))
                    seen.add(bk)
                if last:
                    out.append([banks[bk], t])
            if p < 3:
                yield
        for o in out:
            if o:
                o[1] = t

    FULL = slice(0, 512)
    COLS4 = [(c, FULL, True, slice(128 * c, 128 * c + 128), None) for c in range(4)]
    ROWS4 = [(blk, FULL, False, FULL, blk) for blk in range(NB)]

    UP4 = [(4 * a + c, FULL, True, slice(128 * c, 128 * c + 128), a) for a in range(2) for c in range(4)]

    def split_h(src, toks):
        out = []
        tw = T.now()
        for k in range(8):
            ta = act(hh[:, k, :], src[:, k, :], ACT.Copy, toks[k], tw)
            out.append([ta, tt(hl[:, k, :], src[:, k, :], hh[:, k, :].bitcast(F32), ALU.subtract, ta, tw, toks[k])])
        return out

    def now(g):
        for _ in g:
            pass

    def rms2(tx, a):
        b = ps.take()
        for k in range(8):
            q = scr.take()
            tk_ = tx[k] if len(tx) == 8 else tx
            if k % 2:
                t = tt(q[:, :], xT[:, k, :], xT[:, k, :], ALU.mult, tk_, q.rel)
            else:
                t = act(q[:, :], xT[:, k, :], ACT.Square, tk_, q.rel)
            t = mmt(b[:, :], ones[:, :], q[:, :], k == 0, k == 7, t, b.rel, t0)
            q.free(t)
        t = act(rstd[:, :], b[:, :], ACT.Ln, t, t1, bias=epsc[:, 0:1], scale=1.0 / D)
        b.free(t)
        tr_ = act(rstd[:, :], rstd[:, :], ACT.Exp, t, scale=-0.5)
        out = []
        for k in range(8):
            q = scr.take()
            t = stt(q[:, :], xT[:, k, :], a[:, k:k + 1], rstd[:, :], ALU.mult, ALU.mult, tr_, tx, q.rel)
            ta = act(hh[:, k, :], q[:, :], ACT.Copy, t)
            tl = tt(hl[:, k, :], q[:, :], hh[:, k, :].bitcast(F32), ALU.subtract, ta)
            q.free(tl)
            out.append([ta, tl])
        return out

    def layer(l, tx):
        P = Split([((l, n), m) for n, m in (("sbq", 512), ("sbk", 512), ("sbv", 512), ("nq", 512), ("kv", 512), ("kw", 280))])
        th = rms2(tx, C("ng", 8 * l, 8 * l + 8))
        s_xs, s_xl = sem(f"s_xs{l}"), sem(f"s_xl{l}")
        tsv = A.dma(s_xs, xd, xT[:, :, :], tx)
        kg = C("kg2", 192 * l, 192 * l + 192)
        qg = C("qg2", 64 * l, 64 * l + 64)
        r = []
        now(four(P, COLS4, th, r))
        for c, (b, tpe) in enumerate(r):
            t1_ = ts(qk[:, c, :], b[:, :], 0.125, ALU.mult, tpe)
            b.free(t1_)
        V.wait(tsv)
        A.wait(tsv)
        r = []
        now(four(P, COLS4, th, r))
        for c, (b, tpe) in enumerate(r):
            t2_ = acopy(qk[:, 4 + c, :], b[:, :], tpe)
            b.free(t2_)
        r = []
        tsb = []
        now(four(P, ROWS4, th, r))
        for blk, (b, tpe) in enumerate(r):
            t3_ = acopy(sv[:, blk, :], b[:, :], tpe)
            b.free(t3_)
            tsb.append([t1_, t2_, t3_])

        tn, tkv = [], {}
        tnz = []
        P2 = []
        yn, ysb, tysb, tyn, tga = {}, {}, [], [], []

        def turn_k(o, t, dst):
            b = ps.take()
            t = tr(b[:, 0:128], o[:, 0:128], ident, b.rel, t)
            o.free(t)
            t = acopy(dst, b[:, 0:128], t)
            b.free(t)
            return t

        def nsa_proj():
            def beside(g, work):
                for _ in g:
                    if work:
                        next(work[0], None)
                        work.append(work.pop(0))
                    yield
                while work:
                    for w_ in list(work):
                        if next(w_, 0) == 0:
                            work.remove(w_)
                    yield

            def keep(r):
                for x in r:
                    q = scr.take()
                    t = acopy(q[:, 0:x[2]], x[0][:, 0:x[2]], x[1], q.rel)
                    x[0].free(t)
                    x[0], x[1] = q, t

            def nq_rows(b, tpe, blk, rs):
                sl = slice(128 * blk, 128 * blk + 128)
                o, t, rd = norm_rope(b, 0, 8, 128, qg, cosR[:, blk, :], sinR[:, blk, :], True, tpe, rs)
                b.free(*rd)
                yield 1
                b = ps.take()
                T.wait(b.rel, t)
                for k in range(4):
                    t = tr(b[:, 128 * k:128 * k + 128], o[:, 128 * k:128 * k + 128], ident)
                o.free(t)
                t = ts(nq[:, :, sl], b[:, :].rearrange("p (m t) -> p m t", m=4), 0.125, ALU.mult, t)
                b.free(t)
                tn.append(t)

            def kv_rows(b, c0, tpe, blk, br, last, rs):
                sl = slice(128 * blk, 128 * blk + 128)
                t3 = acopy(nv[:, blk, 128 * br:128 * br + 128], b[:, c0 + 128:c0 + 256], tpe)
                t4 = None
                if br:
                    t4 = tkv["gate"] = act(gates[:, blk, :], b[:, 256:280], ACT.Sigmoid, tpe)
                o, t, rd = norm_rope(b, c0, 2, 128, kg[:, 64 + 64 * br:128 + 64 * br], cosR[:, blk, :],
                                     sinR[:, blk, :], False, tpe, rs)
                if last:
                    b.free(t3, t4, *rd)
                tkv["v"] = t3
                yield 1
                tkv["k"] = turn_k(o, t, (kwT if br else ksT)[:, sl])

            r = []
            yield from four(P, ROWS4, th, r)
            for x in r:
                x.append(512)
            keep(r)
            rs = heads_rstds([x[0][:, 0:512] for x in r], 8, 64, [x[1] for x in r])
            work = [nq_rows(b, tpe, blk, rs[blk]) for blk, (b, tpe, _) in enumerate(r)]
            r = []
            jobs = COLS4[0:2] + [(2 + blk // 2, slice(256 * (blk % 2), 256 * (blk % 2) + 256), False,
                                  slice(256, 512), blk) for blk in range(NB)]
            yield from beside(four(P, jobs, th, r), work)
            cmpt = []
            for c in range(2):
                b, tpe = r.pop(0)
                t = acopy(zs[:, 4 + c, :], b[:, :], tpe)
                b.free(t)
                cmpt.append(t)
            r = [r[0] + [512], r[2] + [512]]
            keep(r)
            rs = heads_rstds([r[blk // 2][0][:, 256 * (blk % 2):256 * (blk % 2) + 128] for blk in range(NB)], 2, 64,
                             [r[blk // 2][1] for blk in range(NB)])
            work = [kv_rows(r[blk // 2][0], 256 * (blk % 2), r[blk // 2][1], blk, 0, blk % 2, rs[blk]) for blk in range(NB)]
            r = []
            jobs = [(blk, slice(0, 280), False, slice(0, 280), blk) for blk in range(NB)]
            yield from beside(four(P, jobs, th, r), work)
            for x in r:
                x.append(280)
            keep(r)
            rs = heads_rstds([x[0][:, 0:128] for x in r], 2, 64, [x[1] for x in r])
            work = [kv_rows(b, 0, tpe, blk, 1, True, rs[blk]) for blk, (b, tpe, _) in enumerate(r)]
            yield from beside(compress(cmpt), work)

        def compress(cmpt):
            for kv in range(2):
                xc = [scr.take(), scr.take()]
                xcm = [x[:, :].rearrange("p (m g c) -> p m g c", m=8, g=2) for x in xc]
                o, _ = COL["pe"]
                o += 32 * l + 16 * kv
                txc = []
                for hf in range(2):
                    t2 = V.do(lambda e, x=xc[hf]: e.memset(x[:, :], 0.0), xc[hf].rel, cmpt[kv])
                    V.wait(t2)
                    A.wait(t2, cmpt[kv])
                    for g in range(2):
                        vw = zs[64 * g:64 * g + 64, 4 + kv, :].rearrange("p (c m r) -> p r m c", m=8, r=2)
                        for r in range(2):
                            t3 = (acopy if r else vcopy)(xcm[hf][64 * r:64 * r + 64, :, g, 0:31], vw[:, r, :, hf:hf + 31])
                            txc.append(t3)
                    pv = cst[:, o + 8 * hf:o + 8 * hf + 8].rearrange("p (m o) -> p m o", o=1).to_broadcast([128, 8, 64])
                    xv = xc[hf][:, :].rearrange("p (m c) -> p m c", m=8)
                    txc.append(tt(xv, xv, pv, ALU.add, txc))
                slot, tw = W.get((l, "w1", kv))
                wv = slot[:, :].rearrange("p (k n) -> p k n", k=16)
                yield
                b = ps.take()
                T.wait(tw, txc, b.rel)
                for k in range(16):
                    f = mmt if k == 15 else mm
                    t = f(b[0:64, 0:256], xc[k // 8][:, 64 * (k % 8):64 * (k % 8) + 64], wv[:, k, :], k == 0, k == 15)
                W.done(t)
                xc[0].free(t)
                xc[1].free(t)
                q, z = scr.take(), scr.take()
                t = acopy(q[0:64, 256:512], b[0:64, 0:256], t, q.rel)
                b.free(t)
                yield
                b = ps.take()
                T.wait(t, b.rel)
                for m in range(2):
                    t = tr(b[:, 64 * m:64 * m + 64], q[0:64, 256 + 128 * m:384 + 128 * m], ident[0:64, 0:64])
                o, _ = COL["cb1"]
                o += 4 * l + 2 * kv
                zc = z[:, 0:128]
                for m in range(2):
                    t3 = ts(z[:, 64 * m:64 * m + 64], b[:, 64 * m:64 * m + 64], cst[:, o + m:o + m + 1], ALU.add, t, z.rel)
                b.free(t3)
                t3 = act(q[:, 0:128], zc, ACT.Sigmoid, t3)
                t3 = tt(zc, zc, q[:, 0:128], ALU.mult, t3)
                zv = zc.rearrange("p (m g c) -> p g m c", g=2, m=2)
                o, _ = COL["cw2"]
                o += 256 * l + 128 * kv
                if kv == 0:
                    yield
                    b = ps.take()
                    T.wait(b.rel, t3)
                    for g in range(2):
                        for m in range(2):
                            f = mmt if g == 1 and m == 1 else mm
                            t = f(b[0:32, 64 * g:64 * g + 64], zv[:, g, m, :], cst[:, o + 64 * m:o + 64 * m + 64], m == 0, m == 1)
                    q.free(t3)
                    z.free(t)
                    ko, t, rd = norm_rope(b, 0, 2, 32, kg[0:32, 0:64], ccs[:, 0:32], ccs[:, 32:64], False, t)
                    b.free(*rd)
                    yield
                    b = ps.take()
                    t = tr(b[:, 0:32], ko[0:32, 0:128], ident[0:32, 0:32], b.rel, t)
                    ko.free(t)
                    tkv["ck"] = acopy(kcT[:, :], b[:, 0:32], t)
                    b.free(tkv["ck"])
                else:
                    qv = q[:, 0:512].rearrange("p (a r c) -> p a r c", a=4, r=4)
                    t = vcopy(qv, zc.rearrange("p (a r c) -> p a r c", a=4, r=1).to_broadcast([128, 4, 4, 32]), t3)
                    z.free(t)
                    yield
                    b = ps.take()
                    T.wait(b.rel, t)
                    for g in range(2):
                        for m in range(2):
                            f = mmt if g == 1 and m == 1 else mm
                            t = f(b[:, 64 * g:64 * g + 64], q[:, 128 * (2 * m + g):128 * (2 * m + g) + 128],
                                  cst[:, o + 64 * m:o + 64 * m + 64], m == 0, m == 1)
                    q.free(t)
                    V.wait(tvz)
                    for r in range(4):
                        pr = slice(32 * r, 32 * r + 32)
                        t2 = vcopy(vcb[pr, :, 64 * r:64 * r + 64], b[pr, 0:128].rearrange("p (g d) -> p g d", g=2), t)
                    tkv["cv"] = t2
                    b.free(t2)

        def silu_n():
            P2.append(Split([((l, n), 512) for n in ("nz", "sbz")] + [((l, n, j), 512) for n in ("ga", "gb", "up", "wout") for j in range(2)]))
            r = []
            yield from four(P2[0], COLS4, th, r)
            tq = T.now()
            for c, (b, tpe) in enumerate(r):
                q = scr.take()
                t = act(q[:, :], b[:, :], ACT.Sigmoid, tpe, q.rel)
                t = tt(zs[:, 4 + c, :], b[:, :], q[:, :], ALU.mult, t, tq)
                b.free(t)
                q.free(t)
                tnz.append(t)
            yield

        def compressed(i):
            sl = slice(128 * i, 128 * i + 128)
            y = yn[i] = scr.take()
            q = scr.take()
            pv = q[:, 0:256].rearrange("p (n c) -> p n c", n=8)
            cm = C("cmask", 32 * i, 32 * i + 32)
            for g in range(2):
                pr = slice(64 * g, 64 * g + 64)
                b = ps.take()
                T.wait(b.rel, tkv["ck"], tn)
                for j in range(4):
                    f = mmt if j == 3 else mm
                    t = f(b[:, 32 * j:32 * j + 32], nq[pr, j, sl], kcT[pr, :], True, True)
                t = tt(pv[:, 4 * g:4 * g + 4, :], b[:, 0:128].rearrange("p (n c) -> p n c", n=4), bcm(cm, 4, 32), ALU.add, t, q.rel)
                b.free(t)
            s1 = stat(8)
            t = red(s1, pv, ALU.max, t)
            t = tt(pv, pv, bc(s1, 8, 32), ALU.subtract, t)
            t = act(q[:, 0:256], q[:, 0:256], ACT.Exp, t)
            s2 = stat(8)
            t = red(s2, pv, ALU.add, t)
            t = rec(s2, s2, t)
            t = stt(s2, s2, C("cany", i, i + 1), gates[:, i, 0:8], ALU.mult, ALU.mult, t, tkv["gate"])
            t = tt(pv, pv, bc(s2, 8, 32), ALU.mult, t)
            yield
            b = ps.take()
            T.wait(b.rel, t)
            for g in range(2):
                t = tr(b[:, 128 * g:128 * g + 128], q[:, 128 * g:128 * g + 128], ident)
            q.free(t)
            p = scr.take()
            t = acopy(p[:, 0:256], b[:, 0:256], t, p.rel)
            b.free(t)
            yield
            b = ps.take()
            T.wait(b.rel, t, tkv["cv"])
            for g in range(2):
                t = mmt(b[:, 256 * g:256 * g + 256], p[:, 128 * g:128 * g + 128], vcb[:, g, :], True, True)
            p.free(t)
            t = vcopy(y[:, :], b[:, :], t, y.rel)
            b.free(t)
            yield

        def outer():
            r = []
            yield from four(P2[0], COLS4, th, r)
            for c, (b, tpe) in enumerate(r):
                q = scr.take()
                t = act(q[:, :], b[:, :], ACT.Tanh, tpe, q.rel, scale=0.5)
                t = stt(q[:, :], q[:, :], 1.0, b[:, :], ALU.add, ALU.mult, t)
                b.free(t)
                t = stt(zs[:, c, :], q[:, :], 0.5, zs[:, c, :], ALU.mult, ALU.mult, t, tysb)
                q.free(t)
                tnz.append(t)
            yield
            tq = T.now()
            for j in range(2):
                r = []
                yield from four(P2[0], COLS4, th, r)
                for c, (b, tpe) in enumerate(r):
                    t = act(qk[:, 4 * j + c, :], b[:, :], ACT.Tanh, tpe, tq, scale=0.5)
                    b.free(t)
                    tga.append(t)
                yield

        def put_y(y, t, a, sl):
            b = ps.take()
            T.wait(b.rel, t)
            for k in range(4):
                tp = tr(b[:, 128 * k:128 * k + 128], y[:, 128 * k:128 * k + 128], ident)
            y.free(tp)
            bv = b[:, :].rearrange("p (m t) -> p m t", m=4)
            zv = zs[:, 4 * a:4 * a + 4, sl]
            if a == 0:
                t = vcopy(zv, bv, tp)
                tysb.append(t)
            else:
                t = tt(zv, bv, zv, ALU.mult, tp, tnz)
                tyn.append(t)
            b.free(t)

        def fin_sb(h, i):
            def fin(b, t, u):
                if h == 0:
                    ysb[i] = scr.take()
                y = ysb[i]
                t = vcopy(y[:, 64 * h:64 * h + 64], b[:, 0:64], t, y.rel if h == 0 else None)
                if h == 7:
                    defer(lambda: put_y(y, t, 0, slice(128 * i, 128 * i + 128)))
                return t
            return fin

        def fin_n(n, br, i):
            def fin(b, t, u):
                y = yn[i]
                r = stat(2)
                t2 = rec(r[:, 0:1], u.rs, u.tp)
                t2 = tt(r[:, 1:2], r[:, 0:1], gates[:, i, 8 * br + n:8 * br + n + 1], ALU.mult, t2, tkv["gate"])
                o = y[:, 64 * n:64 * n + 64]
                t = stt(o, b[:, 0:64], r[:, 1:2], o, ALU.mult, ALU.add, t, t2)
                if n == 7 and br == 2:
                    defer(lambda: put_y(y, t, 1, slice(128 * i, 128 * i + 128)))
                return t
            return fin

        units = []
        for i in range(NB):
            for h in range(8):
                pr = slice(64 * (h % 2), 64 * (h % 2) + 64)
                units.append(Unit("stick", qk[pr, h // 2, :], qk[pr, 4 + h // 2, :], i,
                                  lambda k, h=h: sv[:, k, 64 * h:64 * h + 64], fin_sb(h, i), tsb[i]))
        f1 = Fill(nsa_proj(), silu_n(), compressed(0))
        attend(units, lambda t: f1.step(2 if t % NF1 == NF1 - 1 else 1))
        f1.drain()
        units = []
        for i in range(NB):
            for br, kT in ((1, ksT), (2, kwT)):
                for n in range(8):
                    g, j = n // 4, n % 4
                    pr = slice(64 * g, 64 * g + 64)
                    c0 = 128 * (br - 1) + 64 * g
                    units.append(Unit("soft", nq[pr, j, :], kT[pr, :], i, lambda k, c0=c0: nv[:, k, c0:c0 + 64],
                                      fin_n(n, br, i), [tn, tkv["k"], tkv["v"]]))
        f2 = Fill(*[compressed(i) for i in range(1, NB)], outer())
        attend(units, lambda t: f2.step(1 if t < 9 or t % NF2 == 0 else 0))
        f2.drain()

        mg = qk
        tmg = []
        tgb = []
        gb = [scr.take() for _ in range(8)]
        for j in range(2):
            r = []
            now(four(P2[0], COLS4, th, r))
            for c, (b, tpe) in enumerate(r):
                q = gb[4 * j + c]
                t = act(q[:, :], b[:, :], ACT.Tanh, tpe, q.rel, scale=0.5)
                b.free(t)
                tgb.append(t)
        tz = split_h(zs, [tyn + tnz] * 8)
        tma = []
        for j in range(2):
            r = []
            for _ in four(P2[0], UP4, tz, r):
                if len(r) == 4:
                    for c in range(4):
                        f = 4 * j + c
                        t = stt(mg[:, f, :], mg[:, f, :], 1.0, r[c][0][:, :], ALU.add, ALU.mult, r[c][1], tga)
                        r[c][0].free(t)
                        tma.append(t)
                    r.append(None)
            for c in range(4):
                f = 4 * j + c
                q = gb[f]
                b, tpe = r[5 + c]
                t = stt(q[:, :], q[:, :], 1.0, b[:, :], ALU.add, ALU.mult, tpe, tgb[f])
                b.free(t)
                t = tt(mg[:, f, :], mg[:, f, :], q[:, :], ALU.add, t, tma[f], E=G)
                q.free(t)
                tmg.append(t)
        txl = G.dma(s_xl, xT[:, :, :], xd, T.now(), V.now(), A.now(), tsv)
        tz = split_h(mg, tmg)
        V.wait(txl)
        tx = []
        for j in range(2):
            r = []
            now(four(P2[0], COLS4, tz, r))
            for c, (b, tpe) in enumerate(r):
                f = 4 * j + c
                t = stt(xT[:, f, :], b[:, :], 0.5, xT[:, f, :], ALU.mult, ALU.add, tpe)
                b.free(t)
                tx.append(t)
        return tx

    for l in range(2):
        tx = layer(l, tx)
        if dbg == f"layer{l}":
            break
    return finish(nc, ctx, T, V, A, G, Y, io, xT, tx, sem)


def finish(nc, ctx, T, V, A, G, Y, io, xT, tx, sem):
    s_out = sem("s_out")
    t = Y.dma(s_out, io["out"].rearrange("(k p) t -> p k t", p=128), xT[:, :, :], tx)
    Y.wait(t)
    block = ctx.enter_context(nc.Block())

    @block.sync
    def _(e):
        Y.flush(e)

    @block.scalar
    def _(e):
        A.flush(e)

    @block.gpsimd
    def _(e):
        G.flush(e)

    @block.tensor
    def _(e):
        T.flush(e)

    @block.vector
    def _(e):
        V.flush(e)


def _cols(a, k):
    return np.ascontiguousarray(a.reshape(k, 128).T)


def _rows(a):
    return np.broadcast_to(a.reshape(1, -1), (128, a.size))


def _layout(i):
    p = np.arange(128)[:, None]
    f = np.arange(128)[None, :]
    tok = 128 * np.arange(NB)[None, :] + p
    c32 = np.arange(32)
    out = {}
    out["ident"] = p == f
    out["iota"] = f + 0 * p
    out["tri"] = p < f
    out["causal"] = np.where(f > p, NEG, 0.0)
    out["strict"] = np.where(f >= p, NEG, 0.0)
    out["invf"] = _rows(10000.0 ** (-np.arange(32, dtype=np.float32) / np.float32(32)))
    inside = (tok[:, :, None] >= 16 * c32) & (tok[:, :, None] < 16 * c32 + 32) & (c32 < 31)
    out["avg"] = (inside / 32.0).reshape(128, -1)
    seen = (16 * c32 + 31 <= tok[:, :, None]) & (c32 < 31)
    out["cmask"] = np.where(seen, 0.0, NEG).reshape(128, -1)
    out["cany"] = tok >= 31
    out["tok"] = tok
    out["code"] = _rows(np.arange(96) + 32)
    out["thr"] = _rows(np.repeat([128, 256, 384], 32))
    out["ob"] = _rows(np.arange(16))
    out["c"] = _cols(i["c"][0], 8)
    out["ada_b"] = _cols(i["ada_b"][0], 48)
    out["n1"] = _cols(i["norm1_g"][0], 8)
    out["n2"] = _cols(i["norm2_g"][0], 8)
    out["ng"] = np.concatenate([_cols(i["norm_g_2"][l], 8) for l in range(2)], 1)
    for n, m in (("aqg", "a_q_gain"), ("akg", "a_k_gain"), ("aog", "a_out_gain"), ("bqg", "b_q_gain"),
                 ("bkg", "b_k_gain"), ("cog", "c_out_gain")):
        out[n] = np.tile(i[m][0], 128 // i[m].shape[1])[:, None]
    out["cbg"] = i["c_b_g"][0][:, None]
    out["lam"] = _rows(np.concatenate([i[f"a_lam_{n}"][0] for n in ("q1", "k1", "q2", "k2")]))
    w = np.zeros((128, 128), np.float32)
    w[0:16] = i["c_w_g2"][0]
    out["wg2"] = w
    out["convw"] = i["d_conv_w"][0].reshape(4, 2, 128).transpose(2, 1, 0)
    for n, m in (("convb", "d_conv_b"), ("dba", "d_b_a"), ("dbx", "d_b_x"), ("dlam", "d_lambda")):
        out[n] = _cols(i[m][0], 2)
    for n, m in (("dwa", "d_w_a"), ("dwx", "d_w_x")):
        w = np.zeros((128, 2, 128), np.float32)
        for k in range(4):
            a = 64 * (k % 2)
            w[a:a + 64, k // 2, a:a + 64] = i[m][0, k]
        out[n] = w
    out["rw"] = i["router_w"][0].reshape(8, 128, 32).transpose(1, 0, 2)
    out["rb"] = _rows(i["router_b"][0])
    out["pmod"] = p % 32
    out["room"] = np.zeros((128, 512))
    out["qg2"] = _rows(i["q_norm_g_2"])
    out["kg2"] = _rows(i["k_norm_g_2"])
    pe = i["cmp_pe_2"].transpose(3, 0, 1, 2)
    out["pe"] = pe.reshape(64, 2, 2, 16, 2).transpose(4, 0, 1, 2, 3)
    out["cb1"] = i["cmp_b1_2"].reshape(2, 2, 2, 128).transpose(3, 0, 1, 2)
    out["cw2"] = i["cmp_w2_2"].reshape(2, 2, 2, 128, 64).transpose(3, 0, 1, 2, 4)
    cst = np.empty((128, NCONST), np.float32)
    for n, (o, k) in COL.items():
        cst[:, o:o + k] = np.asarray(out[n]).reshape(128, k)
    j, t = p, f
    gm = []
    for L in LEVELS:
        if L:
            gm.append((j // (2 * L) == t // (2 * L)) & (j % (2 * L) < L) & (t % (2 * L) >= L))
        else:
            gm.append(j == t)
    return cst, np.concatenate(gm, 1).astype(np.float32)


_WHOLE = ["w_in_2", "cmp_w1_2", "w_up_a_2", "w_up_b_2", "w_out_2"]
_FIRST = ["ada_w", "w_in", "w_out", "exp_w_up", "exp_w_down", "exp_b_up", "exp_b_down"]


def _arrays(inputs):
    i = {k: np.asarray(v) for k, v in inputs.items()}
    cst, gmask = _layout(i)
    arrays = {"cst": cst, "gmask": gmask, "xT": np.ascontiguousarray(i["x"][0].T),
              "pos": np.ascontiguousarray(i["positions_2"][0].reshape(NB, 128).T)}
    for n in _FIRST:
        arrays[n] = i[n][0]
    for n in _WHOLE:
        arrays[n] = i[n]
    return arrays


def kernel(**inputs):
    import concourse.bacc as bacc
    from concourse.bass_utils import run_bass_kernel_spmd

    arrays = _arrays(inputs)
    nc = bacc.Bacc("TRN2", target_bir_lowering=False, num_devices=1)
    io = {n: nc.dram_tensor("in_" + n, a.shape, mybir.dt.from_np(a.dtype), kind="ExternalInput").ap()
          for n, a in arrays.items()}
    io["out"] = nc.dram_tensor("out", (D, S), F32, kind="ExternalOutput").ap()
    build(nc, io)
    r = run_bass_kernel_spmd(nc, [{"in_" + n: a for n, a in arrays.items()}], core_ids=[0])
    return np.ascontiguousarray(r.results[0]["out"].T).reshape(1, S, D)
```
